# Optimizing a Trainium2 kernel written in Bass

```python
import math
import jax, jax.numpy as jnp
from jax import lax
import numpy as np

D_MODEL = 1024
BATCH = 1
SEQ = 1024
DEPTH = 1

N_MEM = 256
SWA_HEADS = 8
SWA_KV_HEADS = 2
SWA_HEAD_DIM = 64
WINDOW = 128
FOX_HEADS = 8
FOX_HEAD_DIM = 64
MEM_HEADS = 4
MEM_HEAD_DIM = 128
N_BRANCHES = 3
D_FF = 4 * D_MODEL
REL_BUCKETS = 32
REL_MAX_DIST = 128
BLOCK = 128
EPS = 1e-6
NEG = -1e30

SWA_Q = SWA_HEADS * SWA_HEAD_DIM
SWA_KV = SWA_KV_HEADS * SWA_HEAD_DIM
FOX_W = FOX_HEADS * FOX_HEAD_DIM
MEM_W = MEM_HEADS * MEM_HEAD_DIM
GATE_W = N_BRANCHES * D_MODEL
SPLIT_POINTS = (
    SWA_Q,
    SWA_Q + SWA_KV,
    SWA_Q + 2 * SWA_KV,
    SWA_Q + 2 * SWA_KV + FOX_W,
    SWA_Q + 2 * SWA_KV + 2 * FOX_W,
    SWA_Q + 2 * SWA_KV + 3 * FOX_W,
    SWA_Q + 2 * SWA_KV + 3 * FOX_W + FOX_HEADS,
    SWA_Q + 2 * SWA_KV + 3 * FOX_W + FOX_HEADS + MEM_W,
)
IN_WIDTH = SWA_Q + 2 * SWA_KV + 3 * FOX_W + FOX_HEADS + MEM_W + GATE_W

kernel_name = "hybrid_swa_fox_memory_gated_block"

def rmsnorm(x, g):
    xf = x.astype(jnp.float32)
    y = xf * lax.rsqrt(jnp.mean(xf * xf, axis=-1, keepdims=True) + EPS)
    return (y * g.astype(jnp.float32)).astype(x.dtype)

def t5_causal_bucket(dist):
    max_exact = REL_BUCKETS // 2
    d = jnp.maximum(dist, 0)
    df = jnp.maximum(d, 1).astype(jnp.float32)
    large = max_exact + (jnp.log(df / max_exact) / math.log(REL_MAX_DIST / max_exact)
                         * (REL_BUCKETS - max_exact)).astype(jnp.int32)
    large = jnp.minimum(large, REL_BUCKETS - 1)
    return jnp.where(d < max_exact, d, large)

def swa_attention(q, k, v, sinks, rel_bias):
    B, S = q.shape[0], q.shape[1]
    nb = S // BLOCK
    G = SWA_HEADS // SWA_KV_HEADS
    qb = q.reshape(B, nb, BLOCK, SWA_KV_HEADS, G, SWA_HEAD_DIM)
    pad = ((0, 0), (BLOCK, 0), (0, 0), (0, 0))
    kp = jnp.pad(k, pad).reshape(B, nb + 1, BLOCK, SWA_KV_HEADS, SWA_HEAD_DIM)
    vp = jnp.pad(v, pad).reshape(B, nb + 1, BLOCK, SWA_KV_HEADS, SWA_HEAD_DIM)
    kb = jnp.concatenate([kp[:, :-1], kp[:, 1:]], axis=2)
    vb = jnp.concatenate([vp[:, :-1], vp[:, 1:]], axis=2)
    scale = SWA_HEAD_DIM ** -0.5
    s = jnp.einsum('bnqhgd,bnkhd->bnhgqk', qb, kb).astype(jnp.float32) * scale
    t_loc = jnp.arange(BLOCK)[:, None] + BLOCK
    s_loc = jnp.arange(2 * BLOCK)[None, :]
    dist = t_loc - s_loc
    bias = rel_bias[t5_causal_bucket(dist)]
    bias = bias.reshape(BLOCK, 2 * BLOCK, SWA_KV_HEADS, G).transpose(2, 3, 0, 1)
    s = s + bias.astype(jnp.float32)
    band = (dist >= 0) & (dist < WINDOW)
    key_pos = jnp.arange(nb)[:, None] * BLOCK + s_loc - BLOCK
    valid = band[None] & (key_pos >= 0)[:, None, :]
    s = jnp.where(valid[None, :, None, None], s, NEG)
    sink = sinks.astype(jnp.float32).reshape(1, 1, SWA_KV_HEADS, G, 1, 1)
    m = jnp.maximum(jnp.max(s, axis=-1, keepdims=True), sink)
    p = jnp.exp(s - m)
    denom = jnp.sum(p, axis=-1, keepdims=True) + jnp.exp(sink - m)
    p = (p / denom).astype(v.dtype)
    o = jnp.einsum('bnhgqk,bnkhd->bnqhgd', p, vb)
    return o.reshape(B, S, SWA_Q)

def forgetting_attention(q, k, v, log_f):
    B, S = q.shape[0], q.shape[1]
    nb = S // BLOCK
    scale = FOX_HEAD_DIM ** -0.5
    c = jnp.cumsum(log_f, axis=1)
    c_k = c.transpose(0, 2, 1)
    qb = q.reshape(B, nb, BLOCK, FOX_HEADS, FOX_HEAD_DIM).transpose(1, 0, 2, 3, 4)
    cqb = c.reshape(B, nb, BLOCK, FOX_HEADS).transpose(1, 0, 3, 2)
    key_pos = jnp.arange(S)

    def one_block(args):
        qi, cqi, i = args
        s = jnp.einsum('bqhd,bkhd->bhqk', qi, k).astype(jnp.float32) * scale
        s = s + cqi[..., None] - c_k[:, :, None, :]
        q_pos = i * BLOCK + jnp.arange(BLOCK)
        causal = key_pos[None, :] <= q_pos[:, None]
        s = jnp.where(causal, s, NEG)
        p = jax.nn.softmax(s, axis=-1).astype(v.dtype)
        return jnp.einsum('bhqk,bkhd->bqhd', p, v)

    o = lax.map(one_block, (qb, cqb, jnp.arange(nb)))
    return o.transpose(1, 0, 2, 3, 4).reshape(B, S, FOX_W)

def memory_attention(q, mk, mv):
    B, S = q.shape[0], q.shape[1]
    scale = MEM_HEAD_DIM ** -0.5
    s = jnp.einsum('bshd,bmhd->bhsm', q, mk).astype(jnp.float32) * scale
    p = jax.nn.softmax(s, axis=-1).astype(mv.dtype)
    o = jnp.einsum('bhsm,bmhd->bshd', p, mv)
    return o.reshape(B, S, MEM_W)

def setup_inputs(seed: int = 0) -> dict:
    key = jax.random.key(seed)
    ks = jax.random.split(key, 24)
    f32 = jnp.float32

    def w(k, shape, fan_in):
        return jax.random.normal(k, shape, f32) * fan_in ** -0.5

    def gain(k, shape):
        return 1.0 + 0.05 * jax.random.normal(k, shape, f32)

    return {
        "x": jax.random.normal(ks[0], (BATCH, SEQ, D_MODEL), f32),
        "mem": jax.random.normal(ks[1], (BATCH, N_MEM, D_MODEL), f32),
        "g_mix": gain(ks[2], (DEPTH, D_MODEL)),
        "w_in": w(ks[3], (DEPTH, D_MODEL, IN_WIDTH), D_MODEL),
        "b_gate": 0.02 * jax.random.normal(ks[4], (DEPTH, GATE_W), f32),
        "b_forget": 3.0 + 0.1 * jax.random.normal(ks[5], (DEPTH, FOX_HEADS), f32),
        "qn_swa": gain(ks[6], (DEPTH, SWA_HEAD_DIM)),
        "kn_swa": gain(ks[7], (DEPTH, SWA_HEAD_DIM)),
        "sink_swa": 0.5 * jax.random.normal(ks[8], (DEPTH, SWA_HEADS), f32),
        "rel_bias": 0.5 * jax.random.normal(ks[9], (REL_BUCKETS, SWA_HEADS), f32),
        "qn_fox": gain(ks[10], (DEPTH, FOX_HEAD_DIM)),
        "kn_fox": gain(ks[11], (DEPTH, FOX_HEAD_DIM)),
        "g_mem": gain(ks[12], (DEPTH, D_MODEL)),
        "w_mem_kv": w(ks[13], (DEPTH, D_MODEL, 2 * MEM_W), D_MODEL),
        "qn_mem": gain(ks[14], (DEPTH, MEM_HEAD_DIM)),
        "kn_mem": gain(ks[15], (DEPTH, MEM_HEAD_DIM)),
        "w_o_swa": w(ks[16], (DEPTH, SWA_Q, D_MODEL), SWA_Q),
        "w_o_fox": w(ks[17], (DEPTH, FOX_W, D_MODEL), FOX_W),
        "w_o_mem": w(ks[18], (DEPTH, MEM_W, D_MODEL), MEM_W),
        "w_out": w(ks[19], (DEPTH, D_MODEL, D_MODEL), D_MODEL),
        "g_mlp": gain(ks[20], (DEPTH, D_MODEL)),
        "w_mlp_up": w(ks[21], (DEPTH, D_MODEL, D_FF), D_MODEL),
        "w_mlp_down": w(ks[22], (DEPTH, D_FF, D_MODEL), D_FF),
    }

def reference(x, mem, g_mix, w_in, b_gate, b_forget, qn_swa, kn_swa, sink_swa, rel_bias,
              qn_fox, kn_fox, g_mem, w_mem_kv, qn_mem, kn_mem, w_o_swa, w_o_fox, w_o_mem,
              w_out, g_mlp, w_mlp_up, w_mlp_down):
    B, S = x.shape[0], x.shape[1]
    M = mem.shape[1]
    for layer in range(DEPTH):
        h = rmsnorm(x, g_mix[layer])
        proj = h @ w_in[layer]
        qa, ka, va, qf, kf, vf, fl, qm, gl = jnp.split(proj, SPLIT_POINTS, axis=-1)

        qa = rmsnorm(qa.reshape(B, S, SWA_HEADS, SWA_HEAD_DIM), qn_swa[layer])
        ka = rmsnorm(ka.reshape(B, S, SWA_KV_HEADS, SWA_HEAD_DIM), kn_swa[layer])
        va = va.reshape(B, S, SWA_KV_HEADS, SWA_HEAD_DIM)
        ya = swa_attention(qa, ka, va, sink_swa[layer], rel_bias) @ w_o_swa[layer]

        qf = rmsnorm(qf.reshape(B, S, FOX_HEADS, FOX_HEAD_DIM), qn_fox[layer])
        kf = rmsnorm(kf.reshape(B, S, FOX_HEADS, FOX_HEAD_DIM), kn_fox[layer])
        vf = vf.reshape(B, S, FOX_HEADS, FOX_HEAD_DIM)
        log_f = jax.nn.log_sigmoid(fl.astype(jnp.float32) + b_forget[layer].astype(jnp.float32))
        yf = forgetting_attention(qf, kf, vf, log_f) @ w_o_fox[layer]

        mem_n = rmsnorm(mem, g_mem[layer])
        mk, mv = jnp.split(mem_n @ w_mem_kv[layer], 2, axis=-1)
        mk = rmsnorm(mk.reshape(B, M, MEM_HEADS, MEM_HEAD_DIM), kn_mem[layer])
        mv = mv.reshape(B, M, MEM_HEADS, MEM_HEAD_DIM)
        qm = rmsnorm(qm.reshape(B, S, MEM_HEADS, MEM_HEAD_DIM), qn_mem[layer])
        ym = memory_attention(qm, mk, mv) @ w_o_mem[layer]

        gates = jax.nn.sigmoid((gl + b_gate[layer]).astype(jnp.float32)).astype(x.dtype)
        gates = gates.reshape(B, S, N_BRANCHES, D_MODEL)
        merged = gates[:, :, 0] * ya + gates[:, :, 1] * yf + gates[:, :, 2] * ym
        x = x + merged @ w_out[layer]

        hm = rmsnorm(x, g_mlp[layer])
        u = jnp.square(jax.nn.relu(hm @ w_mlp_up[layer]))
        x = x + u @ w_mlp_down[layer]
    return x


_drawn_inputs = setup_inputs


def setup_inputs(seed=0):
    import zlib

    import numpy as np

    out = dict(_drawn_inputs(seed))
    spreads = {}
    factors = {'g_mix': 3.446,
     'b_gate': 8.0,
     'b_forget': 48.488,
     'qn_swa': 8.0,
     'kn_swa': 8.0,
     'sink_swa': 64.0,
     'qn_fox': 7.36,
     'kn_fox': 7.954,
     'g_mem': 8.0,
     'qn_mem': 8.0,
     'kn_mem': 8.0,
     'g_mlp': 5.018}
    for name, (base, spread) in spreads.items():
        noise = np.random.default_rng([zlib.crc32(name.encode()), seed]).standard_normal(out[name].shape)
        drawn = base * np.exp(spread * noise) if base else spread * noise
        out[name] = __import__('jax').numpy.asarray(drawn.astype(out[name].dtype))
    for name, factor in factors.items():
        out[name] = (out[name] * factor).astype(out[name].dtype)
    return out
```

```python
from contextlib import ExitStack

import numpy as np

import concourse.bass as bass
from concourse import mybir
from concourse.alu_op_type import AluOpType as ALU

ACT = mybir.ActivationFunctionType
AX = mybir.AxisListType
F32 = mybir.dt.float32
F32R = mybir.dt.float32r

P = 128
D = 1024
S = 1024
M = 256
KD = D // P
NT = S // P
BANK = 512
SWA_H, SWA_KV, HD = 8, 2, 64
FOX_H = 8
MEM_H, MEM_D = 4, 128
GROUP = 4
FF = 4 * D
WINDOW = 128
BUCKETS, MAX_DIST = 32, 128
EPS = 1e-6
NEG = -1e30
C_QA, C_KA, C_VA, C_QF, C_KF, C_VF, C_FL, C_QM, C_G = 0, 512, 640, 768, 1280, 1792, 2304, 2312, 2824
G_MIX, G_MEM, G_MLP, B_GATE, QN_A, KN_A, QN_F, KN_F, QN_M, KN_M, N_VEC = 0, 8, 16, 24, 48, 49, 50, 51, 52, 53, 54
DIAGS = 383


def bucket_table():
    table = np.zeros((BUCKETS + 1, DIAGS + 1), np.float32)
    exact = BUCKETS // 2
    for j in range(DIAGS):
        dist = 255 - j
        if 0 <= dist < WINDOW:
            if dist < exact:
                b = dist
            else:
                b = exact + int(np.float32(np.log(np.float32(dist / exact))) / np.float32(np.log(MAX_DIST / exact)) * (BUCKETS - exact))
            table[min(b, BUCKETS - 1), j] = 1.0
        else:
            table[BUCKETS, j] = NEG
    table[BUCKETS, DIAGS] = NEG
    return table


def block_program(nc, io):
    top = ExitStack()
    with top:
        def tensor(ctx, name, shape, dt=F32):
            return ctx.enter_context(nc.sbuf_tensor(name, shape, dt))

        def clear(sems):
            with nc.Block(no_gpsimd_drain=True) as block:
                @block.sync
                def _(sp):
                    for s in sems:
                        sp.sem_clear(s)

        class Scope:

            def __init__(self, name):
                self.name, self.ctx, self.sems = name, ExitStack(), []

            def __enter__(self):
                self.ctx.__enter__()
                return self

            def sem(self, name):
                s = self.ctx.enter_context(nc.semaphore(f"{self.name}_{name}"))
                self.sems.append(s)
                return s

            def sb(self, name, shape, dt=F32):
                return tensor(self.ctx, f"{self.name}_{name}", shape, dt)

            def __exit__(self, *e):
                if e[0] is None:
                    clear(self.sems)
                return self.ctx.__exit__(*e)

        psum = top.enter_context(nc.psum_tensor("psum", [P, 8, BANK], F32))
        ident = tensor(top, "ident", [P, P])
        ident_r = tensor(top, "ident_r", [P, P], F32R)
        causal_r = tensor(top, "causal_r", [P, P], F32R)
        vecs = tensor(top, "vecs", [P, 64])
        sinks = tensor(top, "sinks", [P, SWA_H])
        b_forget = tensor(top, "b_forget", [P, FOX_H])
        minus_half = tensor(top, "minus_half", [P, 64])
        act_hi = tensor(top, "act_hi", [P, KD, S], F32R)
        act_lo = tensor(top, "act_lo", [P, KD, S], F32R)
        c_query = nc.dram_tensor("c_query", [FOX_H, 4, S], F32).ap()
        c_key = nc.dram_tensor("c_key", [FOX_H, 4, S], F32).ap()
        diagonals = nc.dram_tensor("diagonals", [P, SWA_H, DIAGS + 1], F32).ap()

        class Weights:

            def __init__(self, sc, per, stages=4, slots=8, loads=None):
                assert per % stages == 0 and per % slots == 0
                loads = loads or [1] * per
                self.at = [16 * sum(loads[j % stages:j + 1:stages]) for j in range(per)]
                self.turn = [16 * sum(loads[s::stages]) for s in range(stages)]
                self.per, self.stages, self.slots = per, stages, slots
                self.stage = sc.sb("w_stage", [P, stages, BANK])
                self.hi = sc.sb("w_hi", [P, slots, BANK], F32R)
                self.lo = sc.sb("w_lo", [P, slots, BANK], F32R)
                self.landed = [sc.sem(f"w_landed{s}") for s in range(stages)]
                self.zeros = sc.sb("w_zeros", [P, BANK])
                self.hi_done = sc.sem("w_hi_done")
                self.zeroed = sc.sem("w_zeroed")
                self.split = sc.sem("w_split")
                self.used = sc.sem("w_used")
                self.asked = sc.sem("w_asked")

            def load(self, sp, i, j, *sources):
                sp.wait_ge(self.split, i * self.per + j + 1)
                if not isinstance(i, int):
                    sp.sem_inc(self.asked, 1)
                at = 0
                for src in sources:
                    width = src.shape[-1] * (src.shape[1] if len(src.shape) == 3 else 1)
                    dst = self.stage[:, j % self.stages, at:at + width]
                    if len(src.shape) == 3:
                        dst = dst.rearrange("p (a b) -> p a b", a=src.shape[1])
                    sp.dma_start(dst, src).then_inc(self.landed[j % self.stages], 16)
                    at += width

            def start_pool(self, pool):
                nc.gpsimd.memset(self.zeros[:], 0.0).then_inc(self.zeroed, 1)
                pool.wait_ge(self.zeroed, 1)
                pool.sem_inc(self.split, self.stages)

            def start_pe(self, pe):
                pe.sem_inc(self.used, self.slots)

            def split_piece(self, pool, i, j, width=BANK):
                s, r = j % self.stages, j % self.slots
                pool.wait_ge(self.landed[s], i * self.turn[s] + self.at[j])
                pool.wait_ge(self.used, i * self.per + j + 1)
                nc.gpsimd.tensor_tensor(self.hi[:, r, 0:width], self.stage[:, s, 0:width], self.zeros[:, 0:width],
                                        ALU.add).then_inc(self.hi_done, 1)
                pool.wait_ge(self.hi_done, i * self.per + j + 1)
                nc.gpsimd.tensor_tensor(self.lo[:, r, 0:width], self.stage[:, s, 0:width],
                                        self.hi[:, r, 0:width].bitcast(F32), ALU.subtract).then_inc(self.split, 1)

            def ready(self, pe, i, j):
                pe.wait_ge(self.split, i * self.per + j + 1 + self.stages)

        def three(out, a_hi, a_lo, b_hi, b_lo, first, last):
            nc.tensor.matmul(out, a_hi, b_hi, start=first, stop=False)
            nc.tensor.matmul(out, a_hi, b_lo, start=False, stop=False)
            return nc.tensor.matmul(out, a_lo, b_hi, start=False, stop=last)

        def norm_to_features(sc, raw, n_tiles, gain, dst_hi, dst_lo, raw_ready):
            per = min(4, n_tiles)
            width = per * P
            normed = sc.sb("normed", [P, n_tiles, D])
            ssq = sc.sb("ssq", [P, n_tiles])
            rstd = sc.sb("rstd", [P, n_tiles])
            squared, stat, scaled = sc.sem("squared"), sc.sem("stat"), sc.sem("scaled")
            turned, hi_done, lo_done = sc.sem("turned"), sc.sem("nt_hi"), sc.sem("nt_lo")
            groups = n_tiles // per

            def act_stats(act):
                for t in range(n_tiles):
                    raw_ready(act, t)
                    nc.scalar.activation(normed[:, t, :], raw[:, t, :], ACT.Square,
                                         accum_out=ssq[:, t:t + 1]).then_inc(squared, 1)

            def pool(pool):
                for g in range(groups):
                    r = slice(g * per, (g + 1) * per)
                    pool.wait_ge(squared, (g + 1) * per)
                    nc.gpsimd.tensor_scalar(rstd[:, r], ssq[:, r], 1.0 / D, EPS, ALU.mult, ALU.add).then_inc(stat, 1)
                    pool.wait_ge(stat, 2 * g + 1)
                    nc.gpsimd.tensor_tensor(rstd[:, r], rstd[:, r], minus_half[:, r], ALU.pow).then_inc(stat, 1)

            def dve_scale(dve, g):
                dve.wait_ge(stat, 2 * g + 2)
                for t in range(g * per, (g + 1) * per):
                    raw_ready(dve, t)
                    nc.vector.tensor_scalar(normed[:, t, :], raw[:, t, :], rstd[:, t:t + 1], None,
                                            ALU.mult).then_inc(scaled, 1)

            def pe(pe):
                for g in range(groups):
                    pe.wait_ge(scaled, (g + 1) * per)
                    for k in range(KD):
                        n = g * KD + k
                        if n >= 8:
                            pe.wait_ge(lo_done, n - 7)
                        for t in range(per):
                            last = nc.tensor.transpose(psum[:, n % 8, t * P:(t + 1) * P],
                                                       normed[:, g * per + t, k * P:(k + 1) * P], ident[:])
                        last.then_inc(turned, 1)

            def act_hi_half(act):
                for g in range(groups):
                    for k in range(KD):
                        n = g * KD + k
                        act.wait_ge(turned, n + 1)
                        nc.scalar.activation(dst_hi[:, k, g * width:(g + 1) * width], psum[:, n % 8, 0:width], ACT.Copy,
                                             scale=vecs[:, gain + k:gain + k + 1]).then_inc(hi_done, 1)

            def dve(dve):
                for g in range(groups):
                    dve_scale(dve, g)
                    for k in range(KD):
                        n = g * KD + k
                        cols = slice(g * width, (g + 1) * width)
                        dve.wait_ge(hi_done, n + 1)
                        nc.vector.scalar_tensor_tensor(
                            out=dst_lo[:, k, cols], in0=psum[:, n % 8, 0:width], scalar=vecs[:, gain + k:gain + k + 1],
                            in1=dst_hi[:, k, cols].bitcast(F32), op0=ALU.mult, op1=ALU.subtract).then_inc(lo_done, 1)

            return act_stats, pool, pe, act_hi_half, dve

        def setup_block():
            with Scope("setup") as sc:
                rows = sc.sb("rows", [64, P])
                rel = sc.sb("rel", [BUCKETS + 1, SWA_H])
                hot = sc.sb("hot", [BUCKETS + 1, DIAGS + 1])
                rel_wide = sc.sb("rel_wide", [BUCKETS + 1, SWA_H, P])
                diag = sc.sb("diag", [P, SWA_H, DIAGS + 1])
                causal = sc.sb("causal", [P, P])
                x_raw = sc.sb("x_raw", [P, NT, D])
                x_landed = [sc.sem(f"x_landed{t}") for t in range(NT)]
                small = sc.sem("small_landed")
                made, ident_ready, causal_ready, rel_made, rel_ready, diag_copied, vec_t, diag_t, copied, stored = (sc.sem(n) for n in (
                    "made", "ident_ready", "causal_ready", "rel_made", "rel_ready", "diag_copied", "vec_turned", "diag_made", "copied", "diag_stored"))
                act_stats, pool_stats, pe_turn, act_hi_half, dve_part = norm_to_features(
                    sc, x_raw, NT, G_MIX, act_hi, act_lo, lambda e, t: e.wait_ge(x_landed[t], 16))

                with nc.Block() as block:
                    @block.sync
                    def _(sp):
                        for t in range(NT):
                            sp.dma_start(x_raw[:, t, :], io["x"][0, t * P:(t + 1) * P, :]).then_inc(x_landed[t], 16)
                        sp.wait_ge(diag_copied, SWA_H)
                        sp.dma_start(diagonals, diag[:]).then_inc(stored, 16)
                        sp.wait_ge(stored, 16)

                    @block.gpsimd
                    def _(pool):
                        nc.gpsimd.memset(ident[:], 0.0).then_inc(made, 1)
                        nc.gpsimd.memset(causal[:], 0.0).then_inc(made, 1)
                        nc.gpsimd.memset(minus_half[:], -0.5).then_inc(made, 1)
                        pool.wait_ge(made, 3)
                        nc.gpsimd.affine_select(out=ident[:], in_=ident[:], compare_op=ALU.not_equal, fill=1.0, base=0,
                                                pattern=[[-1, P]], channel_multiplier=1).then_inc(ident_ready, 1)
                        nc.gpsimd.affine_select(out=causal[:], in_=causal[:], compare_op=ALU.is_ge, fill=NEG, base=0,
                                                pattern=[[-1, P]], channel_multiplier=1).then_inc(causal_ready, 1)
                        pool_stats(pool)

                    @block.scalar
                    def _(act):
                        for at, name, n in ((G_MIX, "g_mix", 8), (G_MEM, "g_mem", 8), (G_MLP, "g_mlp", 8), (B_GATE, "b_gate", 24)):
                            act.dma_start(rows[at:at + n, :], io[name].rearrange("a (r c) -> (a r) c", c=P)).then_inc(small, 16)
                        for at, name in ((QN_A, "qn_swa"), (KN_A, "kn_swa"), (QN_F, "qn_fox"), (KN_F, "kn_fox")):
                            for half in range(2):
                                act.dma_start(rows[at:at + 1, half * HD:(half + 1) * HD], io[name]).then_inc(small, 16)
                        act.dma_start(rows[QN_M:QN_M + 1, :], io["qn_mem"]).then_inc(small, 16)
                        act.dma_start(rows[KN_M:KN_M + 1, :], io["kn_mem"]).then_inc(small, 16)
                        act.dma_start(sinks[:], bass.AP(io["sink_swa"].tensor, 0, [[0, P], [1, SWA_H]])).then_inc(small, 16)
                        act.dma_start(b_forget[:], bass.AP(io["b_forget"].tensor, 0, [[0, P], [1, FOX_H]])).then_inc(small, 16)
                        act.dma_start(hot[:], io["bucket_table"]).then_inc(small, 16)
                        act.dma_start(rel[0:BUCKETS, :], io["rel_bias"]).then_inc(small, 16)
                        act_stats(act)
                        act_hi_half(act)

                    @block.tensor
                    def _(pe):
                        pe.wait_ge(ident_ready, 1)
                        pe.wait_ge(small, 18 * 16)
                        nc.tensor.transpose(psum[:, 0, 0:N_VEC], rows[0:N_VEC, :], ident[0:N_VEC, 0:N_VEC]).then_inc(vec_t, 1)
                        pe.wait_ge(rel_ready, 1)
                        for h in range(SWA_H):
                            if h >= 7:
                                pe.wait_ge(diag_copied, h - 6)
                            nc.tensor.matmul(psum[:, 1 + h % 7, 0:DIAGS + 1], rel_wide[:, h, :], hot[:], start=True,
                                             stop=True).then_inc(diag_t, 1)
                        pe.wait_ge(diag_copied, SWA_H)
                        pe.wait_ge(copied, 1)
                        pe_turn(pe)

                    @block.vector
                    def _(dve):
                        nc.vector.memset(rel[BUCKETS:BUCKETS + 1, :], 1.0).then_inc(rel_made, 1)
                        dve.wait_ge(rel_made, 1)
                        dve.wait_ge(small, 18 * 16)
                        nc.vector.tensor_copy(rel_wide[:], rel[:].unsqueeze(2).to_broadcast([BUCKETS + 1, SWA_H, P])).then_inc(rel_ready, 1)
                        dve.wait_ge(vec_t, 1)
                        nc.vector.tensor_copy(vecs[:, 0:N_VEC], psum[:, 0, 0:N_VEC]).then_inc(copied, 1)
                        for h in range(SWA_H):
                            dve.wait_ge(diag_t, h + 1)
                            nc.vector.tensor_copy(diag[:, h, :], psum[:, 1 + h % 7, 0:DIAGS + 1]).then_inc(diag_copied, 1)
                        dve.wait_ge(ident_ready, 1)
                        dve.wait_ge(causal_ready, 1)
                        nc.vector.tensor_copy(ident_r[:], ident[:]).then_inc(copied, 1)
                        nc.vector.tensor_copy(causal_r[:], causal[:]).then_inc(copied, 1)
                        dve.wait_ge(copied, 1)
                        for at in (QN_A, QN_F):
                            nc.vector.tensor_scalar(vecs[:, at:at + 1], vecs[:, at:at + 1], HD ** -0.5, None,
                                                    ALU.mult).then_inc(copied, 1)
                        dve_part(dve)

        class Chain:

            def __init__(self, eng, sem):
                self.eng, self.sem, self.n = eng, sem, 0

            def __call__(self, instruction):
                self.n += 1
                instruction.then_inc(self.sem, 1)
                self.eng.wait_ge(self.sem, self.n)

        def project_block(name, src_hi, src_lo, n_tiles, chunks):
            n_pieces = KD * len(chunks)
            with Scope(name) as sc:
                w = Weights(sc, n_pieces, loads=[len(c["src"](0)) for c in chunks for _ in range(KD)])
                squares = sc.sb("squares", [P, 2, BANK])
                filled, raw_done, freed_norm, v_hi_done, freed_value = (sc.sem(n) for n in (
                    "filled", "raw_done", "freed_norm", "v_hi_done", "freed_value"))
                reduced, stat, logits_done, scaled = (sc.sem(n) for n in ("reduced", "stat", "logits_done", "scaled"))
                total = [(c, t) for c in range(len(chunks)) for t in range(n_tiles)]
                order = {kind: [q for q, (c, _) in enumerate(total) if chunks[c]["kind"] == kind] for kind in ("norm", "value")}
                norms = [c for c in range(len(chunks)) if chunks[c]["kind"] == "norm"]
                ssq = sc.sb("ssq", [P, max(len(norms), 1), 64])

                with nc.Block(no_gpsimd_drain=True) as block:
                    @block.sync
                    def _(sp):
                        for c, chunk in enumerate(chunks):
                            for k in range(KD):
                                w.load(sp, 0, c * KD + k, *chunk["src"](k))

                    @block.gpsimd
                    def _(pool):
                        w.start_pool(pool)

                        def stats(c):
                            n = norms.index(c)
                            r = slice(0, n_tiles * chunks[c]["heads"])
                            pool.wait_ge(reduced, (n + 1) * n_tiles)
                            nc.gpsimd.tensor_scalar(ssq[:, n, r], ssq[:, n, r], 1.0 / chunks[c]["hd"], EPS,
                                                    ALU.mult, ALU.add).then_inc(stat, 1)
                            pool.wait_ge(stat, 2 * n + 1)
                            nc.gpsimd.tensor_tensor(ssq[:, n, r], ssq[:, n, r], minus_half[:, r], ALU.pow).then_inc(stat, 1)

                        for c, chunk in enumerate(chunks):
                            for k in range(KD):
                                w.split_piece(pool, 0, c * KD + k, chunk["width"])
                            if c and chunks[c - 1]["kind"] == "norm":
                                stats(c - 1)
                        if chunks[-1]["kind"] == "norm":
                            stats(len(chunks) - 1)

                    @block.tensor
                    def _(pe):
                        w.start_pe(pe)
                        for c, chunk in enumerate(chunks):
                            for k in range(KD):
                                w.ready(pe, 0, c * KD + k)
                                for t in range(n_tiles):
                                    q = c * n_tiles + t
                                    if k == 0 and q >= 8:
                                        kind = chunks[total[q - 8][0]]["kind"]
                                        pe.wait_ge(freed_norm if kind == "norm" else freed_value, order[kind].index(q - 8) + 1)
                                    rows = slice(t * P, (t + 1) * P)
                                    r = (c * KD + k) % w.slots
                                    wd = chunk["width"]
                                    last = three(psum[:, q % 8, 0:wd], src_hi[:, k, rows], src_lo[:, k, rows],
                                                 w.hi[:, r, 0:wd], w.lo[:, r, 0:wd], k == 0, k == KD - 1)
                                    if k == KD - 1 and t < n_tiles - 1:
                                        last.then_inc(filled, 1)
                                last.then_inc(w.used, 1)

                    @block.scalar
                    def _(act):
                        for q, (c, t) in enumerate(total):
                            chunk = chunks[c]
                            if t < n_tiles - 1:
                                act.wait_ge(filled, c * (n_tiles - 1) + t + 1)
                            else:
                                act.wait_ge(w.used, w.slots + (c + 1) * KD)
                            if chunk["kind"] == "norm":
                                n = order["norm"].index(q)
                                wd = chunk["heads"] * chunk["hd"]
                                nc.scalar.activation(chunk["dst"][:, t, :], psum[:, q % 8, 0:wd], ACT.Copy).then_inc(raw_done, 1)
                                if n >= 2:
                                    act.wait_ge(reduced, n - 1)
                                nc.scalar.activation(squares[:, n % 2, 0:wd], psum[:, q % 8, 0:wd],
                                                     ACT.Square).then_inc(freed_norm, 1)
                            else:
                                nc.scalar.activation(chunk["hi"](t), chunk["view"](psum[:, q % 8, :]), ACT.Copy).then_inc(v_hi_done, 1)

                    @block.vector
                    def _(dve):
                        for q, (c, t) in enumerate(total):
                            chunk = chunks[c]
                            if chunk["kind"] == "norm":
                                n, heads = order["norm"].index(q), chunk["heads"]
                                dve.wait_ge(freed_norm, n + 1)
                                nc.vector.tensor_reduce(
                                    ssq[:, norms.index(c), t * heads:(t + 1) * heads],
                                    squares[:, n % 2, 0:heads * chunk["hd"]].rearrange("p (h d) -> p h d", h=heads),
                                    AX.X, ALU.add).then_inc(reduced, 1)
                                if t == n_tiles - 1:
                                    dve.wait_ge(stat, 2 * norms.index(c) + 2)
                                    for u in range(n_tiles):
                                        dve.wait_ge(raw_done, norms.index(c) * n_tiles + u + 1)
                                        tok = chunk["dst"][:, u, :].rearrange("p (h d) -> p h d", h=heads)
                                        r = ssq[:, norms.index(c), u * heads:(u + 1) * heads]
                                        nc.vector.tensor_tensor(
                                            tok, tok, r.unsqueeze(2).to_broadcast([P, heads, chunk["hd"]]), ALU.mult).then_inc(scaled, 1)
                            else:
                                n = order["value"].index(q)
                                dve.wait_ge(v_hi_done, n + 1)
                                if "logits" in chunk:
                                    nc.vector.tensor_tensor(chunk["logits"](t), psum[:, q % 8, chunk["width"] - FOX_H:chunk["width"]],
                                                            b_forget[:], ALU.add).then_inc(logits_done, 1)
                                nc.vector.tensor_tensor(chunk["lo"](t), chunk["view"](psum[:, q % 8, :]),
                                                        chunk["hi"](t).bitcast(F32), ALU.subtract).then_inc(freed_value, 1)

        def decay_block(logits):
            with Scope("decay") as sc:
                n = NT * FOX_H
                names = ("neg", "mag", "e", "u", "d", "ln", "is0", "num", "den", "l1p", "logf")
                t = {k: sc.sb(k, [P, n]) for k in names}
                upto = sc.sb("upto", [P, BANK])
                ones = sc.sb("ones", [P, BANK])
                cq = sc.sb("cq", [FOX_H, 4, S], F32R)
                ck = sc.sb("ck", [FOX_H, 4, S], F32R)
                own, e_done, u_done, ln_done, logf_done, made, upto_done, summed, c_act, rows_done, stored = (sc.sem(k) for k in (
                    "own", "e_done", "u_done", "ln_done", "logf_done", "made", "upto_done", "summed", "c_act", "rows_done", "stored"))
                with nc.Block(no_gpsimd_drain=True) as block:
                    @block.gpsimd
                    def _(pool):
                        nc.gpsimd.memset(ones[:], 1.0).then_inc(made, 1)
                        pool.wait_ge(made, 1)
                        nc.gpsimd.affine_select(out=upto[:], in_=ones[:], compare_op=ALU.is_ge, fill=0.0, base=0,
                                                pattern=[[1, BANK]], channel_multiplier=-1).then_inc(upto_done, 1)

                    @block.vector
                    def _(dve):
                        done = Chain(dve, own)
                        ts, tt = nc.vector.tensor_scalar, nc.vector.tensor_tensor
                        done(ts(t["neg"][:], logits, -1.0, None, ALU.mult))
                        tt(t["mag"][:], t["neg"][:], logits, ALU.max).then_inc(e_done, 1)
                        dve.wait_ge(e_done, 2)
                        ts(t["u"][:], t["e"][:], 1.0, None, ALU.add).then_inc(u_done, 1)
                        dve.wait_ge(u_done, 1)
                        done(ts(t["d"][:], t["u"][:], -1.0, None, ALU.add))
                        done(ts(t["is0"][:], t["d"][:], 0.0, None, ALU.is_equal))
                        done(tt(t["den"][:], t["d"][:], t["is0"][:], ALU.add))
                        done(nc.vector.reciprocal(t["den"][:], t["den"][:]))
                        dve.wait_ge(ln_done, 1)
                        done(tt(t["num"][:], t["ln"][:], t["is0"][:], ALU.add))
                        done(tt(t["num"][:], t["num"][:], t["e"][:], ALU.mult))
                        done(tt(t["l1p"][:], t["num"][:], t["den"][:], ALU.mult))
                        done(ts(t["neg"][:], logits, 0.0, None, ALU.min))
                        tt(t["logf"][:], t["neg"][:], t["l1p"][:], ALU.subtract).then_inc(logf_done, 1)
                        nc.vector.memset(cq[:, 2:4, :].bitcast(F32), 1.0).then_inc(rows_done, 1)
                        nc.vector.memset(ck[:, 0:2, :].bitcast(F32), 1.0).then_inc(rows_done, 1)
                        for half in range(2):
                            cols = slice(half * BANK, (half + 1) * BANK)
                            dve.wait_ge(c_act, half + 1)
                            tt(cq[:, 1, cols], psum[0:FOX_H, half, :], cq[:, 0, cols].bitcast(F32), ALU.subtract).then_inc(rows_done, 1)
                            dve.wait_ge(rows_done, 3 + 3 * half)
                            ts(ck[:, 3, cols], cq[:, 1, cols].bitcast(F32), -1.0, None, ALU.mult).then_inc(rows_done, 1)
                            ts(ck[:, 2, cols], cq[:, 0, cols].bitcast(F32), -1.0, None, ALU.mult).then_inc(rows_done, 1)

                    @block.scalar
                    def _(act):
                        act.wait_ge(e_done, 1)
                        nc.scalar.activation(t["e"][:], t["mag"][:], ACT.Exp, scale=-1.0).then_inc(e_done, 1)
                        act.wait_ge(u_done, 1)
                        nc.scalar.activation(t["ln"][:], t["u"][:], ACT.Ln).then_inc(ln_done, 1)
                        for half in range(2):
                            act.wait_ge(summed, half + 1)
                            nc.scalar.activation(cq[:, 0, half * BANK:(half + 1) * BANK], psum[0:FOX_H, half, :],
                                                 ACT.Copy).then_inc(c_act, 1)

                    @block.tensor
                    def _(pe):
                        pe.wait_ge(logf_done, 1)
                        pe.wait_ge(upto_done, 1)
                        logf = t["logf"][:].rearrange("p (t h) -> p t h", h=FOX_H)
                        for half in range(2):
                            if half:
                                for j in range(4):
                                    nc.tensor.matmul(psum[0:FOX_H, 1, :], logf[:, j, :], ones[:], start=j == 0, stop=False)
                            for j in range(4):
                                last = nc.tensor.matmul(psum[0:FOX_H, half, j * P:BANK], logf[:, 4 * half + j, :],
                                                        upto[:, 0:BANK - j * P], start=half == 0 and j == 0, stop=j == 3)
                            last.then_inc(summed, 1)

                    @block.sync
                    def _(sp):
                        sp.wait_ge(rows_done, 8)
                        sp.dma_start(c_query, cq[:].bitcast(F32)).then_inc(stored, 16)
                        sp.dma_start(c_key, ck[:].bitcast(F32)).then_inc(stored, 16)
                        sp.wait_ge(stored, 32)

        SCORE, TURN, OUT, PREP = 0, 4, 6, 7

        def pair(slot, width):
            return psum[:, SCORE + 2 * slot:SCORE + 2 * slot + 2, :].rearrange("p b c -> p (b c)")[:, 0:width]

        def attention_block(plan):
            with Scope(plan.name) as sc:
                n = plan.steps
                probs = sc.sb("probs", [P, plan.prob_slots, D])
                ps, plan.probs = plan.prob_slots, probs
                scored, maxed, exped, normed, turned, pt_hi, pt_lo, valued, own = (sc.sem(k) for k in (
                    "scored", "maxed", "exped", "normed", "turned", "pt_hi", "pt_lo", "valued", "dve_own"))
                out_done = [sc.sem(f"out{k}") for k in range(len(plan.out_stages))]
                plan.allocate(sc)
                groups = [plan.turns(s) for s in range(n)]
                first = [sum(len(g) for g in groups[:s]) for s in range(n + 1)]
                ends = [s for s in range(n) if plan.ends_unit(s)]
                unit = [sum(e < s for e in ends) for s in range(n)]

                def out_part(eng, who, s):
                    for k, (engine, fn) in enumerate(plan.out_stages):
                        ended = s - 3 - k // 2
                        if engine == who and ended in ends:
                            u = ends.index(ended)
                            eng.wait_ge(out_done[k - 1] if k else valued, u + 1)
                            if k == 1 and len(out_done) == 4 and u >= plan.slots:
                                eng.wait_ge(out_done[3], u - plan.slots + 1)
                            fn(u).then_inc(out_done[k], 1)

                with nc.Block(no_gpsimd_drain=True) as block:
                    @block.tensor
                    def _(pe):
                        plan.pe_before(pe)
                        for s in range(n + 3):
                            if s < n:
                                plan.pe_inputs(pe, s)
                                if s >= 2:
                                    pe.wait_ge(exped, s - 1)
                                plan.scores(s).then_inc(scored, 1)
                            if s - 3 in ends:
                                u = ends.index(s - 3)
                                pe.wait_ge(pt_lo, first[s - 2])
                                if u:
                                    pe.wait_ge(out_done[plan.out_freed], u)
                                plan.values(u).then_inc(valued, 1)
                            d = s - 2
                            if 0 <= d < n:
                                pe.wait_ge(normed, d + 1)
                                for g, (moves, _, _) in enumerate(groups[d]):
                                    q = first[d] + g
                                    if q >= 2:
                                        pe.wait_ge(pt_lo, q - 1)
                                    for src, dst in moves:
                                        last = nc.tensor.transpose(psum[:, TURN + q % 2, dst:dst + P],
                                                                   probs[:, d % ps, src:src + P], ident[:])
                                    last.then_inc(turned, 1)
                            plan.pe_extra(pe, s)

                    @block.vector
                    def _(dve):
                        done = Chain(dve, own)
                        plan.dve_before(dve)
                        for s in range(n + 4):
                            if s < n:
                                dve.wait_ge(scored, s + 1)
                                if plan.max_writes_probs and s >= ps:
                                    dve.wait_ge(turned, first[s - ps + 1])
                                plan.row_max(done, s).then_inc(maxed, 1)
                            if 0 <= s - 1 < n:
                                dve.wait_ge(exped, s)
                                plan.normalize(done, s - 1, probs[:, (s - 1) % ps, :]).then_inc(normed, 1)
                            if 0 <= s - 2 < n:
                                for g, (moves, _, lo) in enumerate(groups[s - 2]):
                                    q = first[s - 2] + g
                                    dve.wait_ge(pt_hi, q + 1)
                                    src = psum[:, TURN + q % 2, 0:len(moves) * P]
                                    hi = groups[s - 2][g][1]
                                    nc.vector.tensor_tensor(lo, src if len(lo.shape) == 2 else src.rearrange(
                                        "p (a b) -> p a b", b=P), hi.bitcast(F32), ALU.subtract).then_inc(pt_lo, 1)
                            out_part(dve, "dve", s)
                            plan.dve_extra(dve, s)

                    @block.scalar
                    def _(act):
                        plan.act_before(act)
                        for s in range(n + 4):
                            if s < n:
                                act.wait_ge(maxed, s + 1)
                                if s >= ps:
                                    act.wait_ge(turned, first[s - ps + 1])
                                plan.exps(s, probs[:, s % ps, :]).then_inc(exped, 1)
                            if 0 <= s - 2 < n:
                                for g, (moves, hi, _) in enumerate(groups[s - 2]):
                                    q = first[s - 2] + g
                                    act.wait_ge(turned, q + 1)
                                    u = unit[s - 2]
                                    if u >= plan.pt_slots:
                                        act.wait_ge(valued, u - plan.pt_slots + 1)
                                    src = psum[:, TURN + q % 2, 0:len(moves) * P]
                                    nc.scalar.activation(hi, src if len(hi.shape) == 2 else src.rearrange(
                                        "p (a b) -> p a b", b=P), ACT.Copy).then_inc(pt_hi, 1)
                            out_part(act, "act", s)
                            plan.act_extra(act, s)

                    @block.sync
                    def _(sp):
                        plan.sync(sp)

        class HalfHeads:
            out_stages = ()
            out_freed = 1

            def allocate_out(self, sc, width, slots):
                self.slots = slots
                self.part = sc.sb("part", [P, slots, width])
                self.total = sc.sb("total", [P, slots, width])

            @staticmethod
            def value_product(out, values_tile, p_hi, p_lo, start, stop):
                if not start:
                    nc.tensor.matmul(out[0:HD], values_tile[:, 0:HD], p_lo, start=False, stop=False)
                last = nc.tensor.matmul(out, values_tile, p_hi, start=start, stop=stop and not start)
                if start and not stop:
                    last = nc.tensor.matmul(out[0:HD], values_tile[:, 0:HD], p_lo, start=False, stop=False)
                if start and stop:
                    last = nc.tensor.matmul(out, values_tile, p_lo, start=False, stop=True)
                return last

        class Fox(HalfHeads):
            steps = GROUP * NT
            pt_slots, prob_slots = 1, 2
            max_writes_probs = False
            JOBS = (1, 2, 4, 6)
            AUG = HD + 4

            def __init__(self, grp, qk, values, out_hi, out_lo):
                self.name, self.grp, self.qk, self.v, self.out_hi, self.out_lo = f"foxattn{grp}", grp, qk, values, out_hi, out_lo
                self.out_stages = (("act", self.out_part), ("dve", self.out_sum), ("act", self.out_round), ("dve", self.out_rest))

            def allocate(self, sc):
                self.q1 = sc.sb("q1", [P, 2, S], F32R)
                self.k1 = sc.sb("k1", [P, 2, S], F32R)
                self.q2 = sc.sb("q2", [P, 2, S], F32R)
                self.k2 = sc.sb("k2", [P, 2, S], F32R)
                self.pt_hi = sc.sb("pt_hi", [P, NT, BANK], F32R)
                self.pt_lo = sc.sb("pt_lo", [P, NT, BANK], F32R)
                self.stat = sc.sb("stat", [P, 3, 3])
                self.allocate_out(sc, BANK, 1)
                self.rows_landed = [sc.sem(f"rows_landed{b}") for b in range(2)]
                self.prep_turned, self.prep_act, self.prep_done = (sc.sem(k) for k in ("prep_turned", "prep_act", "prep_done"))
                self.scored_heads = sc.sem("scored_heads")

            def pe_job(self, pe, head, job):
                n = 4 * head + job
                if n:
                    pe.wait_ge(self.prep_done, n)
                col = (job // 2) * GROUP * HD + head * HD
                for t in range(4):
                    last = nc.tensor.transpose(psum[0:HD, PREP, t * P:(t + 1) * P],
                                               self.qk[:, 4 * (job % 2) + t, col:col + HD], ident[:])
                last.then_inc(self.prep_turned, 1)

            def act_job(self, act, head, job):
                n, b, cols = 4 * head + job, head % 2, slice((job % 2) * BANK, (job % 2 + 1) * BANK)
                gain = vecs[0:HD, QN_F:QN_F + 1] if job < 2 else vecs[0:HD, KN_F:KN_F + 1]
                act.wait_ge(self.prep_turned, n + 1)
                src = psum[0:HD, PREP, :]
                if job < 2:
                    nc.scalar.activation(self.q1[0:HD, b, cols], src, ACT.Copy, scale=gain).then_inc(self.prep_act, 1)
                    nc.scalar.activation(self.q2[0:HD, b, cols], src, ACT.Copy, scale=gain).then_inc(self.prep_act, 1)
                else:
                    nc.scalar.activation(self.k1[0:HD, b, cols], src, ACT.Copy, scale=gain).then_inc(self.prep_act, 1)
                    nc.scalar.activation(self.k1[HD:P, b, cols], src, ACT.Copy, scale=gain).then_inc(self.prep_act, 1)

            def dve_job(self, dve, head, job):
                n, b, cols = 4 * head + job, head % 2, slice((job % 2) * BANK, (job % 2 + 1) * BANK)
                dve.wait_ge(self.prep_act, 2 * n + 2)
                at = QN_F if job < 2 else KN_F
                lo = self.q1[HD:P, b, cols] if job < 2 else self.k2[0:HD, b, cols]
                hi = (self.q1 if job < 2 else self.k1)[0:HD, b, cols]
                nc.vector.scalar_tensor_tensor(out=lo, in0=psum[0:HD, PREP, :], scalar=vecs[0:HD, at:at + 1],
                                               in1=hi.bitcast(F32), op0=ALU.mult, op1=ALU.subtract).then_inc(self.prep_done, 1)

            def pe_before(self, pe):
                for job in range(4):
                    self.pe_job(pe, 0, job)

            def act_before(self, act):
                for job in range(4):
                    self.act_job(act, 0, job)

            def dve_before(self, dve):
                for job in range(4):
                    self.dve_job(dve, 0, job)

            def pe_extra(self, pe, s):
                head, i = divmod(s, NT)
                if i in self.JOBS and head + 1 < GROUP:
                    self.pe_job(pe, head + 1, self.JOBS.index(i))

            def _evacuated(self, s):
                head, i = divmod(s - 1, NT)
                return (head + 1, self.JOBS.index(i)) if s >= 1 and i in self.JOBS and head + 1 < GROUP else None

            def act_extra(self, act, s):
                if job := self._evacuated(s):
                    self.act_job(act, *job)

            def dve_extra(self, dve, s):
                if job := self._evacuated(s):
                    self.dve_job(dve, *job)

            def sync(self, sp):
                for head in range(GROUP):
                    b = head % 2
                    if head >= 2:
                        sp.wait_ge(self.scored_heads, head - 1)
                    h = self.grp * GROUP + head
                    sp.dma_start(self.q2[HD:self.AUG, b, :].bitcast(F32), c_query[h]).then_inc(self.rows_landed[b], 16)
                    sp.dma_start(self.k2[HD:self.AUG, b, :].bitcast(F32), c_key[h]).then_inc(self.rows_landed[b], 16)

            def pe_inputs(self, pe, s):
                head, i = divmod(s, NT)
                if i == 0:
                    pe.wait_ge(self.prep_done, 4 * head + 4)
                    pe.wait_ge(self.rows_landed[head % 2], 32 * (head // 2 + 1))

            def scores(self, s):
                head, i = divmod(s, NT)
                b, rows, keys = head % 2, slice(i * P, (i + 1) * P), (i + 1) * P
                for half in range((keys + BANK - 1) // BANK):
                    cols = slice(half * BANK, min(keys, (half + 1) * BANK))
                    out = psum[:, SCORE + 2 * (s % 2) + half, 0:cols.stop - cols.start]
                    diagonal = keys <= (half + 1) * BANK
                    nc.tensor.matmul(out, self.q1[:, b, rows], self.k1[:, b, cols], start=True, stop=False)
                    last = nc.tensor.matmul(out, self.q2[0:self.AUG, b, rows], self.k2[0:self.AUG, b, cols],
                                            start=False, stop=not diagonal)
                    if i == NT - 1 and half == 1:
                        last.then_inc(self.scored_heads, 1)
                    if diagonal:
                        last = nc.tensor.matmul(out[:, i * P - cols.start:], ident_r[:], causal_r[:], start=False, stop=True)
                return last

            def row_max(self, done, s):
                return nc.vector.tensor_reduce(self.stat[:, s % 3, 0:1], pair(s % 2, (s % NT + 1) * P), AX.X, ALU.max, negate=True)

            def exps(self, s, probs):
                keys = (s % NT + 1) * P
                return nc.scalar.activation(probs[:, 0:keys], pair(s % 2, keys), ACT.Exp, bias=self.stat[:, s % 3, 0:1],
                                            accum_out=self.stat[:, s % 3, 1:2])

            def normalize(self, done, s, probs):
                keys, st = (s % NT + 1) * P, self.stat
                done(nc.vector.reciprocal(st[:, s % 3, 2:3], st[:, s % 3, 1:2]))
                return nc.vector.tensor_scalar(probs[:, 0:keys], probs[:, 0:keys], st[:, s % 3, 2:3], None, ALU.mult)

            def turns(self, s):
                i = s % NT
                cols = slice((i % 4) * P, (i % 4 + 1) * P)
                out = []
                for k0 in range(0, i + 1, 4):
                    k1 = min(k0 + 4, i + 1)
                    out.append(([(k * P, (k - k0) * P) for k in range(k0, k1)],
                                self.pt_hi[:, k0:k1, cols], self.pt_lo[:, k0:k1, cols]))
                return out

            def ends_unit(self, s):
                return s % 4 == 3

            def values(self, u):
                head, sb = divmod(u, 2)
                last_key = 4 * sb + 3
                for k in range(last_key + 1):
                    c0 = max(0, k - 4 * sb) * P
                    last = self.value_product(psum[:, OUT, c0:BANK], self.v[:, k, head, :], self.pt_hi[:, k, c0:BANK],
                                              self.pt_lo[:, k, c0:BANK], k == 0, k == last_key)
                return last

            def _place(self, u):
                head, sb = divmod(u, 2)
                h = self.grp * GROUP + head
                return slice((h % 2) * HD, (h % 2 + 1) * HD), h // 2, slice(sb * BANK, (sb + 1) * BANK), u % self.slots

            def out_part(self, u):
                rows, _, _, slot = self._place(u)
                return nc.scalar.activation(self.part[rows, slot, :], psum[HD:P, OUT, :], ACT.Copy)

            def out_sum(self, u):
                rows, _, _, slot = self._place(u)
                return nc.vector.tensor_tensor(self.total[rows, slot, :], psum[0:HD, OUT, :], self.part[rows, slot, :], ALU.add)

            def out_round(self, u):
                rows, kt, cols, slot = self._place(u)
                return nc.scalar.activation(self.out_hi[rows, kt, cols], self.total[rows, slot, :], ACT.Copy)

            def out_rest(self, u):
                rows, kt, cols, slot = self._place(u)
                return nc.vector.tensor_tensor(self.out_lo[rows, kt, cols], self.total[rows, slot, :],
                                               self.out_hi[rows, kt, cols].bitcast(F32), ALU.subtract)

        class Mem:
            name = "memattn"
            steps = MEM_H * 2
            pt_slots, prob_slots = 2, 3
            max_writes_probs = False
            out_freed = 1
            SCALE = MEM_D ** -0.5

            def __init__(self, q, k, v_hi, v_lo, out_hi, out_lo):
                self.q, self.k, self.v_hi, self.v_lo, self.out_hi, self.out_lo = q, k, v_hi, v_lo, out_hi, out_lo
                self.out_stages = (("act", self.out_round), ("dve", self.out_rest))

            def allocate(self, sc):
                self.q_t = [sc.sb(f"q_{h}", [P, MEM_H, S], F32R) for h in ("hi", "lo")]
                self.k_t = [sc.sb(f"k_{h}", [P, MEM_H, M], F32R) for h in ("hi", "lo")]
                self.pt = [sc.sb(f"pt_{h}", [P, 2, 2, BANK], F32R) for h in ("hi", "lo")]
                self.stat = sc.sb("stat", [P, 4, 3, 4])
                self.prep_turned, self.prep_act, self.prep_done = (sc.sem(k) for k in ("prep_turned", "prep_act", "prep_done"))

            def _job(self, head, job):
                tok = self.q if job < 2 else self.k
                tiles = range(4 * job, 4 * job + 4) if job < 2 else range(2)
                dst = [t[:, head, job * BANK:(job + 1) * BANK] for t in self.q_t] if job < 2 else [t[:, head, :] for t in self.k_t]
                at = QN_M if job < 2 else KN_M
                return 3 * head + job, tok, tiles, dst, vecs[:, at:at + 1], len(tiles) * P

            def pe_jobs(self, pe, head):
                for job in range(3):
                    n, tok, tiles, _, _, _ = self._job(head, job)
                    if n:
                        pe.wait_ge(self.prep_done, n)
                    for i, t in enumerate(tiles):
                        last = nc.tensor.transpose(psum[:, PREP, i * P:(i + 1) * P], tok[:, t, head * P:(head + 1) * P], ident[:])
                    last.then_inc(self.prep_turned, 1)

            def act_jobs(self, act, head):
                for job in range(3):
                    n, _, _, dst, gain, width = self._job(head, job)
                    act.wait_ge(self.prep_turned, n + 1)
                    nc.scalar.activation(dst[0], psum[:, PREP, 0:width], ACT.Copy, scale=gain).then_inc(self.prep_act, 1)

            def dve_jobs(self, dve, head):
                for job in range(3):
                    n, _, _, dst, gain, width = self._job(head, job)
                    dve.wait_ge(self.prep_act, n + 1)
                    nc.vector.scalar_tensor_tensor(out=dst[1], in0=psum[:, PREP, 0:width], scalar=gain,
                                                   in1=dst[0].bitcast(F32), op0=ALU.mult, op1=ALU.subtract).then_inc(self.prep_done, 1)

            def pe_before(self, pe):
                self.pe_jobs(pe, 0)

            def act_before(self, act):
                self.act_jobs(act, 0)

            def dve_before(self, dve):
                self.dve_jobs(dve, 0)

            def _extra(self, fn, eng, s):
                if s % 2 == 0 and s // 2 + 1 < MEM_H:
                    fn(eng, s // 2 + 1)

            def pe_extra(self, pe, s):
                self._extra(self.pe_jobs, pe, s)

            def act_extra(self, act, s):
                self._extra(self.act_jobs, act, s)

            def dve_extra(self, dve, s):
                self._extra(self.dve_jobs, dve, s)

            def sync(self, sp):
                pass

            def pe_inputs(self, pe, s):
                if s % 2 == 0:
                    pe.wait_ge(self.prep_done, 3 * (s // 2 + 1))

            def scores(self, s):
                head, half = divmod(s, 2)
                for j in range(4):
                    rows = slice((4 * half + j) * P, (4 * half + j + 1) * P)
                    out = psum[:, SCORE + 2 * (s % 2) + j // 2, (j % 2) * M:(j % 2 + 1) * M]
                    last = three(out, self.q_t[0][:, head, rows], self.q_t[1][:, head, rows],
                                 self.k_t[0][:, head, :], self.k_t[1][:, head, :], True, True)
                return last

            def row_max(self, done, s):
                b = s % 3
                done(nc.vector.tensor_reduce(self.stat[:, 0, b, :], pair(s % 2, S).rearrange("p (j m) -> p j m", m=M), AX.X, ALU.max))
                return nc.vector.tensor_scalar(self.stat[:, 1, b, :], self.stat[:, 0, b, :], -self.SCALE, None, ALU.mult)

            def exps(self, s, probs):
                for j in range(4):
                    cols = slice(j * M, (j + 1) * M)
                    last = nc.scalar.activation(probs[:, cols], pair(s % 2, S)[:, cols], ACT.Exp, scale=self.SCALE,
                                                bias=self.stat[:, 1, s % 3, j:j + 1], accum_out=self.stat[:, 2, s % 3, j:j + 1])
                return last

            def normalize(self, done, s, probs):
                st = self.stat
                done(nc.vector.reciprocal(st[:, 3, s % 3, :], st[:, 2, s % 3, :]))
                for j in range(4):
                    cols = slice(j * M, (j + 1) * M)
                    last = nc.vector.tensor_scalar(probs[:, cols], probs[:, cols], st[:, 3, s % 3, j:j + 1], None, ALU.mult)
                return last

            def turns(self, s):
                return [([(j * M + m * P, j * P) for j in range(4)], self.pt[0][:, s % 2, m, :], self.pt[1][:, s % 2, m, :])
                        for m in range(2)]

            def ends_unit(self, s):
                return True

            def values(self, u):
                head = u // 2
                cols = slice(head * MEM_D, (head + 1) * MEM_D)
                for m in range(2):
                    last = three(psum[:, OUT, :], self.v_hi[:, m, cols], self.v_lo[:, m, cols],
                                 self.pt[0][:, u % 2, m, :], self.pt[1][:, u % 2, m, :], m == 0, m == 1)
                return last

            def _dst(self, t, u):
                return t[:, u // 2, (u % 2) * BANK:(u % 2 + 1) * BANK]

            def out_round(self, u):
                return nc.scalar.activation(self._dst(self.out_hi, u), psum[:, OUT, :], ACT.Copy)

            def out_rest(self, u):
                return nc.vector.tensor_tensor(self._dst(self.out_lo, u), psum[:, OUT, :],
                                               self._dst(self.out_hi, u).bitcast(F32), ALU.subtract)

        class Swa(HalfHeads):
            name = "swaattn"
            steps = SWA_KV * NT
            pt_slots, prob_slots = 1, 3
            max_writes_probs = True
            KW = 2 * P

            def __init__(self, q, k, values, out_hi, out_lo):
                self.q, self.k, self.v, self.out_hi, self.out_lo = q, k, values, out_hi, out_lo
                self.out_stages = (("act", self.out_part), ("dve", self.out_sum), ("act", self.out_round), ("dve", self.out_rest))

            def allocate(self, sc):
                self.q1 = sc.sb("q1", [P, SWA_H, S], F32R)
                self.k1 = sc.sb("k1", [P, SWA_KV, S], F32R)
                self.k2 = sc.sb("k2", [HD, SWA_KV, S], F32R)
                self.pt = [sc.sb(f"pt_{h}", [P, 2, BANK], F32R) for h in ("hi", "lo")]
                self.bias = sc.sb("bias", [P, SWA_H, self.KW])
                self.stat = sc.sb("stat", [P, 6, 3, GROUP])
                self.allocate_out(sc, 2 * P, 2)
                self.bias_landed = sc.sem("bias_landed")
                self.prep_turned, self.prep_act, self.prep_done = (sc.sem(k) for k in ("prep_turned", "prep_act", "prep_done"))

            def _job(self, g, job):
                n, half = 10 * g + job, job % 2
                cols = slice(half * BANK, (half + 1) * BANK)
                if job < 2:
                    return n, self.k, g * HD, half, cols, self.k1[0:HD, g, cols], self.k1[HD:P, g, cols], self.k2[:, g, cols], KN_A
                h = GROUP * g + (job - 2) // 2
                return n, self.q, h * HD, half, cols, self.q1[0:HD, h, cols], None, self.q1[HD:P, h, cols], QN_A

            def pe_job(self, pe, g, job):
                n, tok, col, half, *_ = self._job(g, job)
                if n:
                    pe.wait_ge(self.prep_done, n)
                for t in range(4):
                    last = nc.tensor.transpose(psum[0:HD, PREP, t * P:(t + 1) * P], tok[:, 4 * half + t, col:col + HD], ident[:])
                last.then_inc(self.prep_turned, 1)

            def act_job(self, act, g, job):
                n, *_, hi, again, _, at = self._job(g, job)
                act.wait_ge(self.prep_turned, n + 1)
                gain = vecs[0:HD, at:at + 1]
                if again is not None:
                    nc.scalar.activation(again, psum[0:HD, PREP, :], ACT.Copy, scale=gain)
                nc.scalar.activation(hi, psum[0:HD, PREP, :], ACT.Copy, scale=gain).then_inc(self.prep_act, 1)

            def dve_job(self, dve, g, job):
                n, *_, hi, _, lo, at = self._job(g, job)
                dve.wait_ge(self.prep_act, n + 1)
                nc.vector.scalar_tensor_tensor(out=lo, in0=psum[0:HD, PREP, :], scalar=vecs[0:HD, at:at + 1],
                                               in1=hi.bitcast(F32), op0=ALU.mult, op1=ALU.subtract).then_inc(self.prep_done, 1)

            def pe_before(self, pe):
                for job in range(10):
                    self.pe_job(pe, 0, job)

            def act_before(self, act):
                for job in range(10):
                    self.act_job(act, 0, job)

            def dve_before(self, dve):
                for job in range(10):
                    self.dve_job(dve, 0, job)
                dve.wait_ge(self.bias_landed, 16)

            JOBS = ((0, 1), (2,), (3,), (4,), (5,), (6,), (7,), (8, 9))

            def _extra(self, fn, eng, s):
                for job in (self.JOBS[s] if s < NT else ()):
                    fn(eng, 1, job)

            def pe_extra(self, pe, s):
                self._extra(self.pe_job, pe, s)

            def act_extra(self, act, s):
                self._extra(self.act_job, act, s)

            def dve_extra(self, dve, s):
                self._extra(self.dve_job, dve, s)

            def sync(self, sp):
                sp.dma_start(self.bias[:], bass.AP(diagonals.tensor, P - 1, [[SWA_H * (DIAGS + 1) - 1, P], [DIAGS + 1, SWA_H], [1, self.KW]])
                             ).then_inc(self.bias_landed, 16)

            def pe_inputs(self, pe, s):
                if s % NT == 0:
                    pe.wait_ge(self.prep_done, 10 * (s // NT + 1))

            def _cols(self, s, j):
                return slice(j * self.KW + (P if s % NT == 0 else 0), (j + 1) * self.KW)

            def scores(self, s):
                g, n = divmod(s, NT)
                keys = slice(max(n - 1, 0) * P, (n + 1) * P)
                rows = slice(n * P, (n + 1) * P)
                for j in range(GROUP):
                    h, out = GROUP * g + j, pair(s % 2, S)[:, self._cols(s, j)]
                    nc.tensor.matmul(out, self.q1[:, h, rows], self.k1[:, g, keys], start=True, stop=False)
                    last = nc.tensor.matmul(out, self.q1[0:HD, h, rows], self.k2[:, g, keys], start=False, stop=True)
                return last

            def row_max(self, done, s):
                g, b, st = s // NT, s % 3, self.stat
                for j in range(GROUP):
                    h, cols = GROUP * g + j, self._cols(s, j)
                    done(nc.vector.tensor_tensor_reduce(
                        out=self.probs[:, b, cols], in0=pair(s % 2, S)[:, cols],
                        in1=self.bias[:, h, cols.start - j * self.KW:], scale=1.0, scalar=sinks[:, h:h + 1],
                        op0=ALU.add, op1=ALU.max, accum_out=st[:, 0, b, j:j + 1]))
                nc.vector.tensor_scalar(st[:, 1, b, :], st[:, 0, b, :], -1.0, None, ALU.mult)
                return nc.vector.tensor_tensor(st[:, 2, b, :], sinks[:, GROUP * g:GROUP * (g + 1)], st[:, 0, b, :], ALU.subtract)

            def exps(self, s, probs):
                st, b = self.stat, s % 3
                nc.scalar.activation(st[:, 3, b, :], st[:, 2, b, :], ACT.Exp)
                for j in range(GROUP):
                    cols = self._cols(s, j)
                    last = nc.scalar.activation(probs[:, cols], probs[:, cols], ACT.Exp, bias=st[:, 1, b, j:j + 1],
                                                accum_out=st[:, 4, b, j:j + 1])
                return last

            def normalize(self, done, s, probs):
                st, b = self.stat, s % 3
                done(nc.vector.tensor_tensor(st[:, 5, b, :], st[:, 4, b, :], st[:, 3, b, :], ALU.add))
                done(nc.vector.reciprocal(st[:, 5, b, :], st[:, 5, b, :]))
                for j in range(GROUP):
                    cols = self._cols(s, j)
                    last = nc.vector.tensor_scalar(probs[:, cols], probs[:, cols], st[:, 5, b, j:j + 1], None, ALU.mult)
                return last

            def turns(self, s):
                return [([(j * self.KW + kb * P, j * P) for j in range(GROUP)], self.pt[0][:, kb, :], self.pt[1][:, kb, :])
                        for kb in ((1,) if s % NT == 0 else (0, 1))]

            def ends_unit(self, s):
                return True

            def values(self, u):
                g, n = divmod(u, NT)
                kbs = (1,) if n == 0 else (0, 1)
                for kb in kbs:
                    last = self.value_product(psum[:, OUT, :], self.v[:, n - 1 + kb, g, :], self.pt[0][:, kb, :],
                                              self.pt[1][:, kb, :], kb == kbs[0], kb == 1)
                return last

            def _heads(self, ap, parity):
                return ap.rearrange("p (a b c) -> p a b c", b=2, c=P)[:, :, parity, :]

            def out_part(self, u):
                for parity in range(2):
                    rows = slice(parity * HD, (parity + 1) * HD)
                    last = nc.scalar.activation(self.part[rows, u % 2, :].rearrange("p (a c) -> p a c", c=P),
                                                self._heads(psum[HD:P, OUT, :], parity), ACT.Copy)
                return last

            def out_sum(self, u):
                for parity in range(2):
                    rows = slice(parity * HD, (parity + 1) * HD)
                    last = nc.vector.tensor_tensor(self.total[rows, u % 2, :].rearrange("p (a c) -> p a c", c=P),
                                                   self._heads(psum[0:HD, OUT, :], parity),
                                                   self.part[rows, u % 2, :].rearrange("p (a c) -> p a c", c=P), ALU.add)
                return last

            def _dst(self, t, u):
                g, n = divmod(u, NT)
                return t[:, 2 * g:2 * g + 2, n * P:(n + 1) * P]

            def out_round(self, u):
                return nc.scalar.activation(self._dst(self.out_hi, u), self.total[:, u % 2, :].rearrange("p (a c) -> p a c", c=P), ACT.Copy)

            def out_rest(self, u):
                return nc.vector.tensor_tensor(self._dst(self.out_lo, u), self.total[:, u % 2, :].rearrange("p (a c) -> p a c", c=P),
                                               self._dst(self.out_hi, u).bitcast(F32), ALU.subtract)

        def mem_norm_block(mem_hi, mem_lo):
            with Scope("memnorm") as sc:
                raw = sc.sb("raw", [P, 2, D])
                landed = [sc.sem(f"landed{t}") for t in range(2)]
                act_stats, pool_stats, pe_turn, act_hi_half, dve_part = norm_to_features(
                    sc, raw, 2, G_MEM, mem_hi, mem_lo, lambda e, t: e.wait_ge(landed[t], 16))
                with nc.Block(no_gpsimd_drain=True) as block:
                    @block.sync
                    def _(sp):
                        for t in range(2):
                            sp.dma_start(raw[:, t, :], io["mem"][0, t * P:(t + 1) * P, :]).then_inc(landed[t], 16)

                    @block.gpsimd
                    def _(pool):
                        pool_stats(pool)

                    @block.scalar
                    def _(act):
                        act_stats(act)
                        act_hi_half(act)

                    @block.tensor
                    def _(pe):
                        pe_turn(pe)

                    @block.vector
                    def _(dve):
                        dve_part(dve)

        merged_dram = nc.dram_tensor("merged", [KD, P, S], F32).ap()

        def merge_block(name, branch, w_o, out_hi, out_lo, first):
            with Scope(name) as sc:
                w = Weights(sc, 6, stages=3, slots=6)
                gate = sc.sb("gate", [P, 2, 2, BANK])
                merged = sc.sb("merged", [P, 2, S])
                before = sc.sb("before", [P, 2, S])
                gated, product, merged_done = sc.sem("gated"), sc.sem("product"), sc.sem("merged_done")
                before_landed = [sc.sem(f"before_landed{j}") for j in range(2)]
                stored = [sc.sem(f"stored{j}") for j in range(2)]
                w_gate = io["w_in"][0].rearrange("(k p) n -> p k n", p=P)
                w_branch = w_o[0].rearrange("(k p) n -> p k n", p=P)
                turns = KD // 2

                with nc.Block(no_gpsimd_drain=True) as block:
                    @block.sync
                    def _(sp):
                        with sp.Fori(0, turns) as i:
                            for j in range(2):
                                gate_col = sp.snap(i * (2 * P) + (C_G + branch * D + j * P))
                                out_col = sp.snap(i * (2 * P) + j * P)
                                for h in range(2):
                                    w.load(sp, i, 3 * j + h, w_gate[:, 4 * h:4 * h + 4, bass.ds(gate_col, P)])
                                w.load(sp, i, 3 * j + 2, w_branch[:, :, bass.ds(out_col, P)])

                    @block.gpsimd
                    def _(pool):
                        w.start_pool(pool)
                        with pool.Fori(0, turns) as i:
                            for n in range(6):
                                w.split_piece(pool, i, n)

                    @block.tensor
                    def _(pe):
                        w.start_pe(pe)
                        with pe.Fori(0, turns) as i:
                            for j in range(2):
                                pe.wait_ge(merged_done, i * 4 + 2 * j + 2)
                                for piece in range(3):
                                    n = 3 * j + piece
                                    w.ready(pe, i, n)
                                    for kk in range(4):
                                        for half in range(2):
                                            cols = slice(half * BANK, (half + 1) * BANK)
                                            k = 4 * piece + kk if piece < 2 else kk
                                            b_hi, b_lo = (act_hi, act_lo) if piece < 2 else (out_hi, out_lo)
                                            wc = slice(kk * P, (kk + 1) * P)
                                            last = three(psum[:, 4 * j + (2 if piece == 2 else 0) + half, :],
                                                         w.hi[:, n, wc], w.lo[:, n, wc], b_hi[:, k, cols], b_lo[:, k, cols],
                                                         piece != 1 and kk == 0, piece > 0 and kk == 3)
                                    last.then_inc(w.used, 1)

                    @block.scalar
                    def _(act):
                        for j in range(2):
                            act.sem_inc(stored[j], 16)
                        with act.Fori(0, turns) as i:
                            for j in range(2):
                                if not first:
                                    act.wait_ge(merged_done, i * 4 + 2 * j + 2)
                                    act.dma_start(before[:, j, :], merged_dram[bass.ds(i * 2 + j, 1), :, :].rearrange("a p n -> (a p) n")
                                                  ).then_inc(before_landed[j], 16)
                                act.wait_ge(w.used, i * 6 + (3 * j + 2 + w.slots))
                                for half in range(2):
                                    nc.scalar.activation(gate[:, j, half, :], psum[:, 4 * j + half, :], ACT.Sigmoid,
                                                         bias=vecs[:, bass.ds(i * 2 + (B_GATE + branch * KD + j), 1)]).then_inc(gated, 1)
                                act.wait_ge(merged_done, i * 4 + 2 * j + 2 + 4)
                                act.dma_start(merged_dram[bass.ds(i * 2 + j, 1), :, :].rearrange("a p n -> (a p) n"),
                                              merged[:, j, :]).then_inc(stored[j], 16)
                        for j in range(2):
                            act.wait_ge(stored[j], 16 * (turns + 1))

                    @block.vector
                    def _(dve):
                        dve.sem_inc(merged_done, 4)
                        with dve.Fori(0, turns) as i:
                            for j in range(2):
                                dve.wait_ge(w.used, i * 6 + (3 * j + 3 + w.slots))
                                dve.wait_ge(stored[j], i * 16 + 16)
                                for half in range(2):
                                    cols = slice(half * BANK, (half + 1) * BANK)
                                    dve.wait_ge(gated, i * 4 + 2 * j + half + 1)
                                    ins = nc.vector.tensor_tensor(merged[:, j, cols], psum[:, 4 * j + 2 + half, :], gate[:, j, half, :], ALU.mult)
                                    if first:
                                        ins.then_inc(merged_done, 1)
                                    else:
                                        ins.then_inc(product, 1)
                                        dve.wait_ge(product, i * 4 + 2 * j + half + 1)
                                        dve.wait_ge(before_landed[j], i * 16 + 16)
                                        nc.vector.tensor_tensor(merged[:, j, cols], merged[:, j, cols], before[:, j, cols],
                                                                ALU.add).then_inc(merged_done, 1)

        def out_block(x2):
            with Scope("wout") as sc:
                w = Weights(sc, 2 * KD)
                merged = sc.sb("merged", [P, KD, S])
                landed = [sc.sem(f"landed{k}") for k in range(KD)]
                x_landed = [sc.sem(f"x_landed{t}") for t in range(NT)]
                hi_done, lo_done, filled, added = (sc.sem(k) for k in ("hi_done", "lo_done", "filled", "added"))
                with nc.Block(no_gpsimd_drain=True) as block:
                    @block.sync
                    def _(sp):
                        for k in range(KD):
                            w.load(sp, 0, k, w_rows(io["w_out"], k, 0, BANK))
                        for k in range(KD):
                            w.load(sp, 0, KD + k, w_rows(io["w_out"], k, BANK, D))

                    @block.gpsimd
                    def _(pool):
                        w.start_pool(pool)
                        for n in range(2 * KD):
                            w.split_piece(pool, 0, n)

                    @block.scalar
                    def _(act):
                        for k in range(KD):
                            act.dma_start(merged[:, k, :], merged_dram[k]).then_inc(landed[k], 16)
                        for t in range(NT):
                            act.dma_start(x2[:, t, :], io["x"][0, t * P:(t + 1) * P, :]).then_inc(x_landed[t], 16)
                        for k in range(KD):
                            act.wait_ge(landed[k], 16)
                            nc.scalar.activation(act_hi[:, k, :], merged[:, k, :], ACT.Copy).then_inc(hi_done, 1)

                    @block.tensor
                    def _(pe):
                        w.start_pe(pe)
                        for c in range(2):
                            for k in range(KD):
                                n = c * KD + k
                                w.ready(pe, 0, n)
                                pe.wait_ge(lo_done, k + 1)
                                for t in range(NT):
                                    if c and k == 0:
                                        pe.wait_ge(added, t + 1)
                                    rows = slice(t * P, (t + 1) * P)
                                    last = three(psum[:, t, :], act_hi[:, k, rows], act_lo[:, k, rows], w.hi[:, n % w.slots, :],
                                                 w.lo[:, n % w.slots, :], k == 0, k == KD - 1)
                                    if k == KD - 1 and t < NT - 1:
                                        last.then_inc(filled, 1)
                                last.then_inc(w.used, 1)

                    @block.vector
                    def _(dve):
                        for k in range(KD):
                            dve.wait_ge(hi_done, k + 1)
                            nc.vector.tensor_tensor(act_lo[:, k, :], merged[:, k, :], act_hi[:, k, :].bitcast(F32),
                                                    ALU.subtract).then_inc(lo_done, 1)
                        for c in range(2):
                            for t in range(NT):
                                if t < NT - 1:
                                    dve.wait_ge(filled, c * (NT - 1) + t + 1)
                                else:
                                    dve.wait_ge(w.used, w.slots + (c + 1) * KD)
                                dve.wait_ge(x_landed[t], 16)
                                cols = slice(c * BANK, (c + 1) * BANK)
                                nc.vector.tensor_tensor(x2[:, t, cols], x2[:, t, cols], psum[:, t, :], ALU.add).then_inc(added, 1)

        def mlp_norm_block(x2):
            with Scope("mlpnorm") as sc:
                act_stats, pool_stats, pe_turn, act_hi_half, dve_part = norm_to_features(
                    sc, x2, NT, G_MLP, act_hi, act_lo, lambda e, t: None)
                with nc.Block(no_gpsimd_drain=True) as block:
                    @block.gpsimd
                    def _(pool):
                        pool_stats(pool)

                    @block.scalar
                    def _(act):
                        act_stats(act)
                        act_hi_half(act)

                    @block.tensor
                    def _(pe):
                        pe_turn(pe)

                    @block.vector
                    def _(dve):
                        dve_part(dve)

        def mlp_block(x2):
            FB = 8
            TURNS = FF // (FB * P)
            UP, DOWN = 2 * FB, 2 * FB
            OUTS = 2 * NT
            with Scope("mlp") as sc:
                w = Weights(sc, UP + DOWN, slots=4)
                u_hi = sc.sb("u_hi", [P, FB, S], F32R)
                u_lo = sc.sb("u_lo", [P, FB, S], F32R)
                relu = sc.sb("relu", [P, 2, BANK])
                square = sc.sb("square", [P, 2, BANK])
                relu_done, square_done, hi_done, lo_done, filled, added = (sc.sem(k) for k in (
                    "relu_done", "square_done", "hi_done", "lo_done", "filled", "added"))
                out_stored = sc.sem("out_stored")
                w_up = io["w_mlp_up"][0].rearrange("(k p) n -> p k n", p=P)
                w_down = io["w_mlp_down"][0].rearrange("(t k p) n -> p t k n", p=P, k=FB)

                with nc.Block(no_gpsimd_drain=True) as block:
                    @block.sync
                    def _(sp):
                        with sp.Fori(0, TURNS) as i:
                            for fb in range(FB):
                                for h in range(2):
                                    w.load(sp, i, 2 * fb + h, w_up[:, 4 * h:4 * h + 4, bass.ds(i * (FB * P) + fb * P, P)])
                            for c in range(2):
                                for k in range(FB):
                                    w.load(sp, i, UP + c * FB + k,
                                           w_down[:, bass.ds(i, 1), k, c * BANK:(c + 1) * BANK].rearrange("p a n -> p (a n)"))
                        for t in range(NT):
                            sp.wait_ge(added, OUTS * TURNS + NT + t + 1)
                            sp.dma_start(io["out"][0, t * P:(t + 1) * P, :], x2[:, t, :]).then_inc(out_stored, 16)
                        sp.wait_ge(out_stored, 16 * NT)

                    @block.gpsimd
                    def _(pool):
                        w.start_pool(pool)
                        with pool.Fori(0, TURNS) as i:
                            for n in range(UP + DOWN):
                                w.split_piece(pool, i, n)

                    @block.tensor
                    def _(pe):
                        w.start_pe(pe)
                        with pe.Fori(0, TURNS) as i:
                            for fb in range(FB):
                                for h in range(2):
                                    n = 2 * fb + h
                                    w.ready(pe, i, n)
                                    if h == 0 and fb < 2:
                                        pe.wait_ge(added, i * OUTS + OUTS - 2 + 2 * fb)
                                    elif h == 0:
                                        pe.wait_ge(relu_done, i * (2 * FB) + 2 * fb - 2)
                                    for kk in range(4):
                                        for half in range(2):
                                            cols = slice(half * BANK, (half + 1) * BANK)
                                            wc = slice(kk * P, (kk + 1) * P)
                                            k = 4 * h + kk
                                            last = three(psum[:, 2 * (fb % 2) + half, :], w.hi[:, n % w.slots, wc], w.lo[:, n % w.slots, wc],
                                                         act_hi[:, k, cols], act_lo[:, k, cols], k == 0, k == KD - 1)
                                    last.then_inc(w.used, 1)
                            for c in range(2):
                                for k in range(FB):
                                    n = UP + c * FB + k
                                    w.ready(pe, i, n)
                                    if c == 0:
                                        pe.wait_ge(lo_done, i * (2 * FB) + 2 * k + 4)
                                    for t in range(NT):
                                        bank = (t + 4) % 8
                                        if k == 0 and c == 0 and bank < 4:
                                            pe.wait_ge(relu_done, i * (2 * FB) + 2 * FB - 3 + bank)
                                        if k == 0 and c == 1:
                                            pe.wait_ge(added, i * OUTS + OUTS + t + 1)
                                        rows = slice(t * P, (t + 1) * P)
                                        last = three(psum[:, bank, :], u_hi[:, k, rows], u_lo[:, k, rows],
                                                     w.hi[:, n % w.slots, :], w.lo[:, n % w.slots, :], k == 0, k == FB - 1)
                                        if k == FB - 1 and t < NT - 1:
                                            last.then_inc(filled, 1)
                                    last.then_inc(w.used, 1)

                    @block.scalar
                    def _(act):
                        with act.Fori(0, TURNS) as i:
                            for fb in range(FB):
                                act.wait_ge(w.used, i * w.per + 2 * fb + 2 + w.slots)
                                for half in range(2):
                                    n = 2 * fb + half
                                    nc.scalar.activation(relu[:, half, :], psum[:, 2 * (fb % 2) + half, :], ACT.Relu).then_inc(relu_done, 1)
                                    act.wait_ge(relu_done, i * (2 * FB) + n + 1)
                                    act.wait_ge(lo_done, i * (2 * FB) + n + 1)
                                    nc.scalar.activation(square[:, half, :], relu[:, half, :], ACT.Square).then_inc(square_done, 1)

                    @block.vector
                    def _(dve):
                        dve.sem_inc(lo_done, 2)
                        dve.sem_inc(added, OUTS)
                        with dve.Fori(0, TURNS) as i:
                            dve.wait_ge(w.used, i * w.per + w.slots)
                            for n in range(2 * FB):
                                cols = slice((n % 2) * BANK, (n % 2 + 1) * BANK)
                                dve.wait_ge(square_done, i * (2 * FB) + n + 1)
                                nc.vector.tensor_copy(u_hi[:, n // 2, cols], square[:, n % 2, :]).then_inc(hi_done, 1)
                                dve.wait_ge(hi_done, i * (2 * FB) + n + 1)
                                nc.vector.tensor_tensor(u_lo[:, n // 2, cols], square[:, n % 2, :],
                                                        u_hi[:, n // 2, cols].bitcast(F32), ALU.subtract).then_inc(lo_done, 1)
                            for c in range(2):
                                for t in range(NT):
                                    if t < NT - 1:
                                        dve.wait_ge(filled, i * (2 * NT - 2) + c * (NT - 1) + t + 1)
                                    else:
                                        dve.wait_ge(w.used, i * w.per + UP + (c + 1) * FB + w.slots)
                                    cols = slice(c * BANK, (c + 1) * BANK)
                                    nc.vector.tensor_tensor(x2[:, t, cols], x2[:, t, cols], psum[:, (t + 4) % 8, :], ALU.add).then_inc(added, 1)

        def w_rows(weights, k, lo, hi):
            return weights[0, k * P:(k + 1) * P, lo:hi]

        stop = io.get("stop")
        w_in = io["w_in"]

        def columns(weights, lo, width):
            return lambda k: [w_rows(weights, k, lo, lo + width)]

        setup_block()
        with ExitStack() as outs:
            out_hi = tensor(outs, "out_hi", [P, 4, S], F32R)
            out_lo = tensor(outs, "out_lo", [P, 4, S], F32R)

            for grp in range(FOX_H // GROUP):
                with Scope(f"fox{grp}") as fx:
                    gw = GROUP * HD
                    qk = fx.sb("qk", [P, NT, BANK])
                    values = fx.sb("values", [P, NT, GROUP, 2 * HD], F32R)
                    logits = fx.sb("logits", [P, NT, FOX_H]) if grp == 0 else None

                    def qk_source(k):
                        first = w_rows(w_in, k, C_QF + grp * gw, C_QF + grp * gw + 1)
                        return [bass.AP(w_in.tensor, first.offset, [[w_in.shape[2], P], [C_KF - C_QF, 2], [1, gw]])]

                    def v_source(k):
                        v = w_rows(w_in, k, C_VF + grp * gw, C_VF + (grp + 1) * gw)
                        return [v] + ([w_rows(w_in, k, C_FL, C_FL + FOX_H)] if grp == 0 else [])

                    v_chunk = {"kind": "value", "width": gw + (FOX_H if grp == 0 else 0), "src": v_source,
                               "view": lambda ps: ps[:, 0:gw].rearrange("p (h d) -> p h d", d=HD),
                               "hi": lambda t: values[:, t, :, 0:HD], "lo": lambda t: values[:, t, :, HD:2 * HD]}
                    if grp == 0:
                        v_chunk["logits"] = lambda t: logits[:, t, :]
                    project_block(f"foxproj{grp}", act_hi, act_lo, NT, [
                        {"kind": "norm", "width": BANK, "heads": 2 * GROUP, "hd": HD, "src": qk_source, "dst": qk}, v_chunk])
                    if grp == 0:
                        decay_block(logits[:].rearrange("p t h -> p (t h)"))
                    if stop == "decay":
                        return
                    attention_block(Fox(grp, qk, values, out_hi, out_lo))
                if stop == f"fox{grp}":
                    return
            merge_block("merge_fox", 1, io["w_o_fox"], out_hi, out_lo, True)
            if stop == "mergefox":
                return

            with Scope("mem") as ms:
                q = ms.sb("q", [P, NT, BANK])
                k_tok = ms.sb("k_tok", [P, 2, BANK])
                v_hi = ms.sb("v_hi", [P, 2, BANK], F32R)
                v_lo = ms.sb("v_lo", [P, 2, BANK], F32R)
                with Scope("memtok") as mt:
                    mem_hi = mt.sb("mem_hi", [P, KD, M], F32R)
                    mem_lo = mt.sb("mem_lo", [P, KD, M], F32R)
                    mem_norm_block(mem_hi, mem_lo)
                    project_block("memkv", mem_hi, mem_lo, 2, [
                        {"kind": "norm", "width": BANK, "heads": MEM_H, "hd": MEM_D, "src": columns(io["w_mem_kv"], 0, BANK), "dst": k_tok},
                        {"kind": "value", "width": BANK, "src": columns(io["w_mem_kv"], BANK, BANK), "view": lambda ps: ps,
                         "hi": lambda t: v_hi[:, t, :], "lo": lambda t: v_lo[:, t, :]}])
                project_block("memq", act_hi, act_lo, NT, [
                    {"kind": "norm", "width": BANK, "heads": MEM_H, "hd": MEM_D, "src": columns(w_in, C_QM, BANK), "dst": q}])
                attention_block(Mem(q, k_tok, v_hi, v_lo, out_hi, out_lo))
            if stop == "mem":
                return
            merge_block("merge_mem", 2, io["w_o_mem"], out_hi, out_lo, False)

            with Scope("swa") as ss:
                q = ss.sb("q", [P, NT, BANK])
                k_tok = ss.sb("k_tok", [P, NT, SWA_KV * HD])
                values = ss.sb("values", [P, NT, SWA_KV, 2 * HD], F32R)
                kvw = SWA_KV * HD
                project_block("swaproj", act_hi, act_lo, NT, [
                    {"kind": "norm", "width": BANK, "heads": SWA_H, "hd": HD, "src": columns(w_in, C_QA, BANK), "dst": q},
                    {"kind": "norm", "width": kvw, "heads": SWA_KV, "hd": HD, "src": columns(w_in, C_KA, kvw), "dst": k_tok},
                    {"kind": "value", "width": kvw, "src": columns(w_in, C_VA, kvw),
                     "view": lambda ps: ps[:, 0:kvw].rearrange("p (h d) -> p h d", d=HD),
                     "hi": lambda t: values[:, t, :, 0:HD], "lo": lambda t: values[:, t, :, HD:2 * HD]}])
                attention_block(Swa(q, k_tok, values, out_hi, out_lo))
            if stop == "swa":
                return
            merge_block("merge_swa", 0, io["w_o_swa"], out_hi, out_lo, False)

        with ExitStack() as rest:
            x2 = tensor(rest, "x2", [P, NT, D])
            out_block(x2)
            if stop == "x2":
                return
            mlp_norm_block(x2)
            mlp_block(x2)


def kernel(**inputs):
    import concourse.bacc as bacc
    from concourse.bass_utils import run_bass_kernel_spmd

    nc = bacc.Bacc("TRN2", target_bir_lowering=False, num_devices=1)
    arrays = {name: np.ascontiguousarray(a) for name, a in inputs.items()}
    arrays["bucket_table"] = bucket_table()
    io = {name: nc.dram_tensor(f"in_{name}", a.shape, mybir.dt.from_np(a.dtype), kind="ExternalInput").ap()
          for name, a in arrays.items()}
    io["out"] = nc.dram_tensor("out", (1, S, D), F32, kind="ExternalOutput").ap()
    block_program(nc, io)
    done = run_bass_kernel_spmd(nc, [{f"in_{name}": a for name, a in arrays.items()}], core_ids=[0])
    return done.results[0]["out"]
```

```python
from contextlib import ExitStack

import numpy as np

import concourse.bass as bass
from concourse import mybir
from concourse.alu_op_type import AluOpType as ALU

ACT = mybir.ActivationFunctionType
AX = mybir.AxisListType
F32 = mybir.dt.float32
F32R = mybir.dt.float32r

P = 128
D = 1024
S = 1024
M = 256
KD = D // P
NT = S // P
BANK = 512
SWA_H, SWA_KV, HD = 8, 2, 64
FOX_H = 8
MEM_H, MEM_D = 4, 128
GROUP = 4
FF = 4 * D
WINDOW = 128
BUCKETS, MAX_DIST = 32, 128
EPS = 1e-6
NEG = -1e30
C_QA, C_KA, C_VA, C_QF, C_KF, C_VF, C_FL, C_QM, C_G = 0, 512, 640, 768, 1280, 1792, 2304, 2312, 2824
G_MIX, G_MEM, G_MLP, B_GATE, QN_A, KN_A, QN_F, KN_F, QN_M, KN_M, N_VEC = 0, 8, 16, 24, 48, 49, 50, 51, 52, 53, 54
DIAGS = 383


def bucket_table():
    table = np.zeros((BUCKETS + 1, DIAGS + 1), np.float32)
    exact = BUCKETS // 2
    for j in range(DIAGS):
        dist = 255 - j
        if 0 <= dist < WINDOW:
            if dist < exact:
                b = dist
            else:
                b = exact + int(np.float32(np.log(np.float32(dist / exact))) / np.float32(np.log(MAX_DIST / exact)) * (BUCKETS - exact))
            table[min(b, BUCKETS - 1), j] = 1.0
        else:
            table[BUCKETS, j] = NEG
    table[BUCKETS, DIAGS] = NEG
    return table


def block_program(nc, io):
    top = ExitStack()
    with top:
        def tensor(ctx, name, shape, dt=F32):
            return ctx.enter_context(nc.sbuf_tensor(name, shape, dt))

        class Scope:
            retired, cleared = [], []

            def __init__(self, name):
                self.name, self.ctx, self.sem_ctx, self.sems = name, ExitStack(), ExitStack(), []

            def __enter__(self):
                for _, context in Scope.cleared:
                    context.close()
                Scope.cleared = []
                self.ctx.__enter__()
                return self

            def sem(self, name):
                s = self.sem_ctx.enter_context(nc.semaphore(f"{self.name}_{name}"))
                self.sems.append(s)
                return s

            def sb(self, name, shape, dt=F32):
                return tensor(self.ctx, f"{self.name}_{name}", shape, dt)

            def __exit__(self, *e):
                Scope.retired.append((self.sems, self.sem_ctx))
                return self.ctx.__exit__(*e)

        def clear_retired(sp):
            for sems, _ in Scope.retired:
                for s in sems:
                    sp.sem_clear(s)
            Scope.cleared, Scope.retired = Scope.cleared + Scope.retired, []

        psum = top.enter_context(nc.psum_tensor("psum", [P, 8, BANK], F32))
        ident = tensor(top, "ident", [P, P])
        ident_r = tensor(top, "ident_r", [P, P], F32R)
        causal_r = tensor(top, "causal_r", [P, P], F32R)
        vecs = tensor(top, "vecs", [P, 64])
        sinks = tensor(top, "sinks", [P, SWA_H])
        b_forget = tensor(top, "b_forget", [P, FOX_H])
        minus_half = tensor(top, "minus_half", [P, 64])
        zeros = tensor(top, "zeros", [P, BANK])
        act_hi = tensor(top, "act_hi", [P, KD, S], F32R)
        act_lo = tensor(top, "act_lo", [P, KD, S], F32R)
        c_query = nc.dram_tensor("c_query", [FOX_H, 4, S], F32).ap()
        c_key = nc.dram_tensor("c_key", [FOX_H, 4, S], F32).ap()
        diagonals = nc.dram_tensor("diagonals", [P, SWA_H, DIAGS + 1], F32).ap()

        gate_logits = nc.dram_tensor("gate_logits", [3 * KD, P, S], F32).ap()
        branch_out = {b: nc.dram_tensor(f"branch_out{b}", [2, P, 4, S], F32).ap() for b in (1, 2)}

        class Weights:

            def __init__(self, sc, per, stages=4, slots=8, loads=None):
                loads = loads or [1] * per
                self.at = [16 * sum(loads[j % stages:j + 1:stages]) for j in range(per)]
                self.turn = [16 * sum(loads[s::stages]) for s in range(stages)]
                self.per, self.stages, self.slots = per, stages, slots
                self.stage = sc.sb("w_stage", [P, stages, BANK])
                self.hi = sc.sb("w_hi", [P, slots, BANK], F32R)
                self.lo = sc.sb("w_lo", [P, slots, BANK], F32R)
                self.landed = [sc.sem(f"w_landed{s}") for s in range(stages)]
                self.hi_done = sc.sem("w_hi_done")
                self.act_hi_done = sc.sem("w_act_hi_done")
                self.by_act = []
                self.split = sc.sem("w_split")
                self.used = sc.sem("w_used")
                self.asked = sc.sem("w_asked")

            def load(self, sp, i, j, *sources):
                sp.wait_ge(self.split, i * self.per + j + 1)
                if not isinstance(i, int):
                    sp.sem_inc(self.asked, 1)
                at = 0
                for src in sources:
                    width = src.shape[-1] * (src.shape[1] if len(src.shape) == 3 else 1)
                    dst = self.stage[:, j % self.stages, at:at + width]
                    if len(src.shape) == 3:
                        dst = dst.rearrange("p (a b) -> p a b", a=src.shape[1])
                    sp.dma_start(dst, src).then_inc(self.landed[j % self.stages], 16)
                    at += width

            def start_pool(self, pool):
                pool.sem_inc(self.split, self.stages)

            def start_pe(self, pe):
                pe.sem_inc(self.used, self.slots)

            def split_piece(self, pool, i, j, width=BANK):
                s, r = j % self.stages, j % self.slots
                pool.wait_ge(self.landed[s], i * self.turn[s] + self.at[j])
                if j in self.by_act:
                    pool.wait_ge(self.act_hi_done, self.by_act.index(j) + 1)
                    nc.gpsimd.tensor_tensor(self.lo[:, r, 0:width], self.stage[:, s, 0:width],
                                            self.hi[:, r, 0:width].bitcast(F32), ALU.subtract).then_inc(self.split, 1)
                    return
                pool.wait_ge(self.used, i * self.per + j + 1)
                nc.gpsimd.tensor_tensor(self.hi[:, r, 0:width], self.stage[:, s, 0:width], zeros[:, 0:width],
                                        ALU.add).then_inc(self.hi_done, 1)
                pool.wait_ge(self.hi_done, i * self.per + j + 1 - sum(n < j for n in self.by_act))
                nc.gpsimd.tensor_tensor(self.lo[:, r, 0:width], self.stage[:, s, 0:width],
                                        self.hi[:, r, 0:width].bitcast(F32), ALU.subtract).then_inc(self.split, 1)

            def act_hi(self, act, j, width=BANK):
                act.wait_ge(self.landed[j % self.stages], self.at[j])
                act.wait_ge(self.used, j + 1)
                nc.scalar.activation(self.hi[:, j % self.slots, 0:width], self.stage[:, j % self.stages, 0:width],
                                     ACT.Copy).then_inc(self.act_hi_done, 1)

            def ready(self, pe, i, j):
                pe.wait_ge(self.split, i * self.per + j + 1 + self.stages)

        def three(out, a_hi, a_lo, b_hi, b_lo, first, last):
            nc.tensor.matmul(out, a_hi, b_hi, start=first, stop=False)
            nc.tensor.matmul(out, a_hi, b_lo, start=False, stop=False)
            return nc.tensor.matmul(out, a_lo, b_hi, start=False, stop=last)

        def norm_to_features(sc, raw, n_tiles, gain, dst_hi, dst_lo, raw_ready):
            per = min(4, n_tiles)
            width = per * P
            normed = sc.sb("normed", [P, n_tiles, D])
            ssq = sc.sb("row_ssq", [P, n_tiles])
            rstd = sc.sb("row_rstd", [P, n_tiles])
            squared, stat, scaled = sc.sem("row_squared"), sc.sem("row_stat"), sc.sem("row_scaled")
            turned, hi_done, lo_done = sc.sem("row_turned"), sc.sem("nt_hi"), sc.sem("nt_lo")
            groups = n_tiles // per

            def act_stats(act):
                for t in range(n_tiles):
                    raw_ready(act, t)
                    nc.scalar.activation(normed[:, t, :], raw[:, t, :], ACT.Square,
                                         accum_out=ssq[:, t:t + 1]).then_inc(squared, 1)

            def pool(pool):
                for g in range(groups):
                    r = slice(g * per, (g + 1) * per)
                    pool.wait_ge(squared, (g + 1) * per)
                    nc.gpsimd.tensor_scalar(rstd[:, r], ssq[:, r], 1.0 / D, EPS, ALU.mult, ALU.add).then_inc(stat, 1)
                    pool.wait_ge(stat, 2 * g + 1)
                    nc.gpsimd.tensor_tensor(rstd[:, r], rstd[:, r], minus_half[:, r], ALU.pow).then_inc(stat, 1)

            def dve_scale(dve, g):
                dve.wait_ge(stat, 2 * g + 2)
                for t in range(g * per, (g + 1) * per):
                    raw_ready(dve, t)
                    nc.vector.tensor_scalar(normed[:, t, :], raw[:, t, :], rstd[:, t:t + 1], None,
                                            ALU.mult).then_inc(scaled, 1)

            def pe(pe, bank_free=lambda pe, n: None):
                for g in range(groups):
                    pe.wait_ge(scaled, (g + 1) * per)
                    for k in range(KD):
                        n = g * KD + k
                        bank_free(pe, n)
                        if n >= 8:
                            pe.wait_ge(lo_done, n - 7)
                        for t in range(per):
                            last = nc.tensor.transpose(psum[:, n % 8, t * P:(t + 1) * P],
                                                       normed[:, g * per + t, k * P:(k + 1) * P], ident[:])
                        last.then_inc(turned, 1)

            def act_hi_half(act):
                for g in range(groups):
                    for k in range(KD):
                        n = g * KD + k
                        act.wait_ge(turned, n + 1)
                        nc.scalar.activation(dst_hi[:, k, g * width:(g + 1) * width], psum[:, n % 8, 0:width], ACT.Copy,
                                             scale=vecs[:, gain + k:gain + k + 1]).then_inc(hi_done, 1)

            def dve(dve, scale=True):
                for g in range(groups):
                    if scale:
                        dve_scale(dve, g)
                    for k in range(KD):
                        n = g * KD + k
                        cols = slice(g * width, (g + 1) * width)
                        dve.wait_ge(hi_done, n + 1)
                        nc.vector.scalar_tensor_tensor(
                            out=dst_lo[:, k, cols], in0=psum[:, n % 8, 0:width], scalar=vecs[:, gain + k:gain + k + 1],
                            in1=dst_hi[:, k, cols].bitcast(F32), op0=ALU.mult, op1=ALU.subtract).then_inc(lo_done, 1)

            return act_stats, pool, pe, act_hi_half, dve, dve_scale, lo_done

        def setup_block():
            with Scope("setup") as sc:
                rows = sc.sb("rows", [64, P])
                rel = sc.sb("rel", [BUCKETS + 1, SWA_H])
                hot = sc.sb("hot", [BUCKETS + 1, DIAGS + 1])
                rel_wide = sc.sb("rel_wide", [BUCKETS + 1, SWA_H, P])
                diag = sc.sb("diag", [P, SWA_H, DIAGS + 1])
                causal = sc.sb("causal", [P, P])
                x_raw = sc.sb("x_raw", [P, NT, D])
                x_landed = [sc.sem(f"x_landed{t}") for t in range(NT)]
                small = sc.sem("small_landed")
                made, ident_ready, causal_ready, rel_made, rel_ready, diag_copied, vec_t, diag_t, copied, stored = (sc.sem(n) for n in (
                    "made", "ident_ready", "causal_ready", "rel_made", "rel_ready", "diag_copied", "vec_turned", "diag_made", "copied", "diag_stored"))
                act_stats, pool_stats, pe_turn, act_hi_half, dve_part, _, _ = norm_to_features(
                    sc, x_raw, NT, G_MIX, act_hi, act_lo, lambda e, t: e.wait_ge(x_landed[t], 16))

                with nc.Block() as block:
                    @block.sync
                    def _(sp):
                        for t in range(NT):
                            sp.dma_start(x_raw[:, t, :], io["x"][0, t * P:(t + 1) * P, :]).then_inc(x_landed[t], 16)
                        sp.wait_ge(diag_copied, SWA_H)
                        sp.dma_start(diagonals, diag[:]).then_inc(stored, 16)
                        sp.wait_ge(stored, 16)
                        clear_retired(sp)

                    @block.gpsimd
                    def _(pool):
                        nc.gpsimd.memset(ident[:], 0.0).then_inc(made, 1)
                        nc.gpsimd.memset(causal[:], 0.0).then_inc(made, 1)
                        nc.gpsimd.memset(minus_half[:], -0.5).then_inc(made, 1)
                        nc.gpsimd.memset(zeros[:], 0.0).then_inc(made, 1)
                        pool.wait_ge(made, 4)
                        nc.gpsimd.affine_select(out=ident[:], in_=ident[:], compare_op=ALU.not_equal, fill=1.0, base=0,
                                                pattern=[[-1, P]], channel_multiplier=1).then_inc(ident_ready, 1)
                        nc.gpsimd.affine_select(out=causal[:], in_=causal[:], compare_op=ALU.is_ge, fill=NEG, base=0,
                                                pattern=[[-1, P]], channel_multiplier=1).then_inc(causal_ready, 1)
                        pool_stats(pool)

                    @block.scalar
                    def _(act):
                        for at, name, n in ((G_MIX, "g_mix", 8), (G_MEM, "g_mem", 8), (G_MLP, "g_mlp", 8), (B_GATE, "b_gate", 24)):
                            act.dma_start(rows[at:at + n, :], io[name].rearrange("a (r c) -> (a r) c", c=P)).then_inc(small, 16)
                        for at, name in ((QN_A, "qn_swa"), (KN_A, "kn_swa"), (QN_F, "qn_fox"), (KN_F, "kn_fox")):
                            for half in range(2):
                                act.dma_start(rows[at:at + 1, half * HD:(half + 1) * HD], io[name]).then_inc(small, 16)
                        act.dma_start(rows[QN_M:QN_M + 1, :], io["qn_mem"]).then_inc(small, 16)
                        act.dma_start(rows[KN_M:KN_M + 1, :], io["kn_mem"]).then_inc(small, 16)
                        act.dma_start(sinks[:], bass.AP(io["sink_swa"].tensor, 0, [[0, P], [1, SWA_H]])).then_inc(small, 16)
                        act.dma_start(b_forget[:], bass.AP(io["b_forget"].tensor, 0, [[0, P], [1, FOX_H]])).then_inc(small, 16)
                        act.dma_start(hot[:], io["bucket_table"]).then_inc(small, 16)
                        act.dma_start(rel[0:BUCKETS, :], io["rel_bias"]).then_inc(small, 16)
                        act_stats(act)
                        act_hi_half(act)

                    @block.tensor
                    def _(pe):
                        pe.wait_ge(ident_ready, 1)
                        pe.wait_ge(small, 18 * 16)
                        nc.tensor.transpose(psum[:, 0, 0:N_VEC], rows[0:N_VEC, :], ident[0:N_VEC, 0:N_VEC]).then_inc(vec_t, 1)
                        pe.wait_ge(rel_ready, 1)
                        for h in range(SWA_H):
                            if h >= 7:
                                pe.wait_ge(diag_copied, h - 6)
                            nc.tensor.matmul(psum[:, 1 + h % 7, 0:DIAGS + 1], rel_wide[:, h, :], hot[:], start=True,
                                             stop=True).then_inc(diag_t, 1)
                        pe.wait_ge(diag_copied, SWA_H)
                        pe.wait_ge(copied, 1)
                        pe_turn(pe)

                    @block.vector
                    def _(dve):
                        nc.vector.memset(rel[BUCKETS:BUCKETS + 1, :], 1.0).then_inc(rel_made, 1)
                        dve.wait_ge(rel_made, 1)
                        dve.wait_ge(small, 18 * 16)
                        nc.vector.tensor_copy(rel_wide[:], rel[:].unsqueeze(2).to_broadcast([BUCKETS + 1, SWA_H, P])).then_inc(rel_ready, 1)
                        dve.wait_ge(vec_t, 1)
                        nc.vector.tensor_copy(vecs[:, 0:N_VEC], psum[:, 0, 0:N_VEC]).then_inc(copied, 1)
                        for h in range(SWA_H):
                            dve.wait_ge(diag_t, h + 1)
                            nc.vector.tensor_copy(diag[:, h, :], psum[:, 1 + h % 7, 0:DIAGS + 1]).then_inc(diag_copied, 1)
                        dve.wait_ge(ident_ready, 1)
                        dve.wait_ge(causal_ready, 1)
                        nc.vector.tensor_copy(ident_r[:], ident[:]).then_inc(copied, 1)
                        nc.vector.tensor_copy(causal_r[:], causal[:]).then_inc(copied, 1)
                        dve.wait_ge(copied, 1)
                        for at in (QN_A, QN_F):
                            nc.vector.tensor_scalar(vecs[:, at:at + 1], vecs[:, at:at + 1], HD ** -0.5, None,
                                                    ALU.mult).then_inc(copied, 1)
                        dve_part(dve)

        class Chain:

            def __init__(self, eng, sem):
                self.eng, self.sem, self.n = eng, sem, 0

            def count(self, instruction):
                self.n += 1
                instruction.then_inc(self.sem, 1)

            def wait(self):
                self.eng.wait_ge(self.sem, self.n)

            def __call__(self, instruction):
                self.count(instruction)
                self.wait()

        def project_block(name, chunks, stores=(), mem=None):
            n_pieces = KD * len(chunks)
            with Scope(name) as sc:
                w = Weights(sc, n_pieces, loads=[len(c["src"](0)) for c in chunks for _ in range(KD)])
                tiles = [chunk["rows"][2] for chunk in chunks]
                start = [sum(tiles[:c]) for c in range(len(chunks))]
                full = [sum(t - 1 for t in tiles[:c]) for c in range(len(chunks))]
                w.by_act = [c * KD + k for c in range(len(chunks)) for k in range(KD) if tiles[c] < 4]
                squares = sc.sb("squares", [P, 2, BANK])
                filled, raw_done, squared, v_hi_done, freed_value = (sc.sem(n) for n in (
                    "filled", "raw_done", "squared", "v_hi_done", "freed_value"))
                reduced, stat, logits_done, scaled, stored = (sc.sem(n) for n in ("reduced", "stat", "logits_done", "scaled", "stored"))
                total = [(c, t) for c in range(len(chunks)) for t in range(tiles[c])]
                order = {kind: [q for q, (c, _) in enumerate(total) if kind in chunks[c]] for kind in ("norm", "value")}
                norms = [c for c in range(len(chunks)) if "norm" in chunks[c]]
                norm_at = [sum(tiles[d] for d in norms if d < c) for c in range(len(chunks))]
                ssq = sc.sb("ssq", [P, max(len(norms), 1), 64])
                if mem:
                    raw = sc.sb("raw", [P, 2, D])
                    mem_landed = [sc.sem(f"mem_landed{t}") for t in range(2)]
                    mem_stats, mem_pool, mem_turn, mem_hi, mem_lo, mem_scale, mem_done = norm_to_features(
                        sc, raw, 2, G_MEM, mem[0], mem[1], lambda e, t: e.wait_ge(mem_landed[t], 16))

                with nc.Block(no_gpsimd_drain=True) as block:
                    @block.sync
                    def _(sp):
                        for c, chunk in enumerate(chunks):
                            for k in range(KD):
                                w.load(sp, 0, c * KD + k, *chunk["src"](k))
                                for t in range(2 if mem and c == 0 and k == 3 else 0):
                                    sp.dma_start(raw[:, t, :], io["mem"][0, t * P:(t + 1) * P, :]).then_inc(mem_landed[t], 16)
                            for dst, src in (stores if c == 0 else ()):
                                sp.dma_start(dst, src).then_inc(stored, 16)
                        if stores:
                            sp.wait_ge(stored, 16 * len(stores))
                        clear_retired(sp)

                    @block.gpsimd
                    def _(pool):
                        w.start_pool(pool)

                        def stats(c):
                            n, part = norms.index(c), chunks[c]["norm"]
                            r = slice(0, tiles[c] * part["heads"])
                            pool.wait_ge(reduced, norm_at[c] + tiles[c])
                            nc.gpsimd.tensor_scalar(ssq[:, n, r], ssq[:, n, r], 1.0 / part["hd"], EPS,
                                                    ALU.mult, ALU.add).then_inc(stat, 1)
                            pool.wait_ge(stat, 2 * n + 1)
                            nc.gpsimd.tensor_tensor(ssq[:, n, r], ssq[:, n, r], minus_half[:, r], ALU.pow).then_inc(stat, 1)

                        for c, chunk in enumerate(chunks):
                            for k in range(KD):
                                w.split_piece(pool, 0, c * KD + k, chunk["width"])
                            if c == 0 and mem:
                                mem_pool(pool)
                            if c - 1 in norms:
                                stats(c - 1)
                        if len(chunks) - 1 in norms:
                            stats(len(chunks) - 1)

                    @block.tensor
                    def _(pe):
                        w.start_pe(pe)
                        for c, chunk in enumerate(chunks):
                            for k in range(KD):
                                w.ready(pe, 0, c * KD + k)
                                for t in range(tiles[c]):
                                    q = start[c] + t
                                    if k == 0 and c == 1 and mem and t == 0:
                                        pe.wait_ge(mem_done, KD)
                                    if k == 0 and q >= 8:
                                        if "value" in chunks[total[q - 8][0]]:
                                            pe.wait_ge(freed_value, order["value"].index(q - 8) + 1)
                                        else:
                                            pe.wait_ge(raw_done, order["norm"].index(q - 8) + 1)
                                    rows = slice(t * P, (t + 1) * P)
                                    r = (c * KD + k) % w.slots
                                    wd = chunk["width"]
                                    src_hi, src_lo, _ = chunk["rows"]
                                    last = three(psum[:, q % 8, 0:wd], src_hi[:, k, rows], src_lo[:, k, rows],
                                                 w.hi[:, r, 0:wd], w.lo[:, r, 0:wd], k == 0, k == KD - 1)
                                    if k == KD - 1 and t < tiles[c] - 1:
                                        last.then_inc(filled, 1)
                                last.then_inc(w.used, 1)
                            if mem and c == 0:
                                mem_turn(pe, lambda pe, n: pe.wait_ge(raw_done, n + 1))

                    @block.scalar
                    def _(act):
                        if mem:
                            mem_stats(act)

                        def split(c):
                            for k in range(KD):
                                if c < len(chunks) and c * KD + k in w.by_act:
                                    w.act_hi(act, c * KD + k, chunks[c]["width"])

                        split(0)
                        split(1)
                        for c, chunk in enumerate(chunks):
                            for t in range(tiles[c]):
                                q = start[c] + t
                                if t < tiles[c] - 1:
                                    act.wait_ge(filled, full[c] + t + 1)
                                else:
                                    act.wait_ge(w.used, w.slots + (c + 1) * KD)
                                if "value" in chunk:
                                    part = chunk["value"]
                                    nc.scalar.activation(part["hi"](t), part["view"](psum[:, q % 8, :]), ACT.Copy).then_inc(v_hi_done, 1)
                                if "norm" in chunk:
                                    part = chunk["norm"]
                                    nc.scalar.activation(part["dst"][:, t, :], psum[:, q % 8, 0:part["heads"] * part["hd"]],
                                                         ACT.Copy).then_inc(raw_done, 1)
                            if mem and c == 0:
                                mem_hi(act)
                            if "norm" in chunk:
                                part = chunk["norm"]
                                for t in range(tiles[c]):
                                    n = norm_at[c] + t
                                    act.wait_ge(raw_done, n + 1)
                                    if n >= 2:
                                        act.wait_ge(reduced, n - 1)
                                    nc.scalar.activation(squares[:, n % 2, 0:part["heads"] * part["hd"]], part["dst"][:, t, :],
                                                         ACT.Square).then_inc(squared, 1)
                            split(c + 2)

                    @block.vector
                    def _(dve):
                        if mem:
                            mem_scale(dve, 0)
                        for c, chunk in enumerate(chunks):
                            if "value" in chunk:
                                part = chunk["value"]
                                for t in range(tiles[c]):
                                    q = start[c] + t
                                    dve.wait_ge(v_hi_done, order["value"].index(q) + 1)
                                    if "norm" in chunk:
                                        dve.wait_ge(raw_done, order["norm"].index(q) + 1)
                                    if "logits" in part:
                                        nc.vector.tensor_tensor(part["logits"](t), psum[:, q % 8, chunk["width"] - FOX_H:chunk["width"]],
                                                                b_forget[:], ALU.add).then_inc(logits_done, 1)
                                    nc.vector.tensor_tensor(part["lo"](t), part["view"](psum[:, q % 8, :]),
                                                            part["hi"](t).bitcast(F32), ALU.subtract).then_inc(freed_value, 1)
                            if mem and c == 0:
                                mem_lo(dve, scale=False)
                            if "norm" in chunk:
                                part, n = chunk["norm"], norms.index(c)
                                heads, hd = part["heads"], part["hd"]
                                for t in range(tiles[c]):
                                    m = norm_at[c] + t
                                    dve.wait_ge(squared, m + 1)
                                    nc.vector.tensor_reduce(
                                        ssq[:, n, t * heads:(t + 1) * heads],
                                        squares[:, m % 2, 0:heads * hd].rearrange("p (h d) -> p h d", h=heads),
                                        AX.X, ALU.add).then_inc(reduced, 1)
                                dve.wait_ge(stat, 2 * n + 2)
                                for t in range(tiles[c]):
                                    tok = part["dst"][:, t, :].rearrange("p (h d) -> p h d", h=heads)
                                    r = ssq[:, n, t * heads:(t + 1) * heads]
                                    nc.vector.tensor_tensor(
                                        tok, tok, r.unsqueeze(2).to_broadcast([P, heads, hd]), ALU.mult).then_inc(scaled, 1)

        def decay_block(logits):
            with Scope("decay") as sc:
                n = NT * FOX_H
                names = ("neg", "mag", "e", "u", "d", "ln", "is0", "num", "den", "l1p", "logf")
                t = {k: sc.sb(k, [P, n]) for k in names}
                upto = sc.sb("upto", [P, BANK])
                ones = sc.sb("ones", [P, BANK])
                cq = sc.sb("cq", [FOX_H, 4, S], F32R)
                ck = sc.sb("ck", [FOX_H, 4, S], F32R)
                own, e_done, u_done, ln_done, logf_done, made, upto_done, summed, c_act, rows_done, stored = (sc.sem(k) for k in (
                    "own", "e_done", "u_done", "ln_done", "logf_done", "made", "upto_done", "summed", "c_act", "rows_done", "stored"))
                with nc.Block(no_gpsimd_drain=True) as block:
                    @block.gpsimd
                    def _(pool):
                        nc.gpsimd.memset(ones[:], 1.0).then_inc(made, 1)
                        pool.wait_ge(made, 1)
                        nc.gpsimd.affine_select(out=upto[:], in_=ones[:], compare_op=ALU.is_ge, fill=0.0, base=0,
                                                pattern=[[1, BANK]], channel_multiplier=-1).then_inc(upto_done, 1)

                    @block.vector
                    def _(dve):
                        done = Chain(dve, own)
                        ts, tt = nc.vector.tensor_scalar, nc.vector.tensor_tensor
                        done(ts(t["neg"][:], logits, -1.0, None, ALU.mult))
                        tt(t["mag"][:], t["neg"][:], logits, ALU.max).then_inc(e_done, 1)
                        dve.wait_ge(e_done, 2)
                        ts(t["u"][:], t["e"][:], 1.0, None, ALU.add).then_inc(u_done, 1)
                        dve.wait_ge(u_done, 1)
                        done(ts(t["d"][:], t["u"][:], -1.0, None, ALU.add))
                        done(ts(t["is0"][:], t["d"][:], 0.0, None, ALU.is_equal))
                        done(tt(t["den"][:], t["d"][:], t["is0"][:], ALU.add))
                        done(nc.vector.reciprocal(t["den"][:], t["den"][:]))
                        dve.wait_ge(ln_done, 1)
                        done(tt(t["num"][:], t["ln"][:], t["is0"][:], ALU.add))
                        done(tt(t["num"][:], t["num"][:], t["e"][:], ALU.mult))
                        done(tt(t["l1p"][:], t["num"][:], t["den"][:], ALU.mult))
                        done(ts(t["neg"][:], logits, 0.0, None, ALU.min))
                        tt(t["logf"][:], t["neg"][:], t["l1p"][:], ALU.subtract).then_inc(logf_done, 1)
                        nc.vector.memset(cq[:, 2:4, :].bitcast(F32), 1.0).then_inc(rows_done, 1)
                        nc.vector.memset(ck[:, 0:2, :].bitcast(F32), 1.0).then_inc(rows_done, 1)
                        for half in range(2):
                            cols = slice(half * BANK, (half + 1) * BANK)
                            dve.wait_ge(c_act, half + 1)
                            tt(cq[:, 1, cols], psum[0:FOX_H, half, :], cq[:, 0, cols].bitcast(F32), ALU.subtract).then_inc(rows_done, 1)
                            dve.wait_ge(rows_done, 3 + 3 * half)
                            ts(ck[:, 3, cols], cq[:, 1, cols].bitcast(F32), -1.0, None, ALU.mult).then_inc(rows_done, 1)
                            ts(ck[:, 2, cols], cq[:, 0, cols].bitcast(F32), -1.0, None, ALU.mult).then_inc(rows_done, 1)

                    @block.scalar
                    def _(act):
                        act.wait_ge(e_done, 1)
                        nc.scalar.activation(t["e"][:], t["mag"][:], ACT.Exp, scale=-1.0).then_inc(e_done, 1)
                        act.wait_ge(u_done, 1)
                        nc.scalar.activation(t["ln"][:], t["u"][:], ACT.Ln).then_inc(ln_done, 1)
                        for half in range(2):
                            act.wait_ge(summed, half + 1)
                            nc.scalar.activation(cq[:, 0, half * BANK:(half + 1) * BANK], psum[0:FOX_H, half, :],
                                                 ACT.Copy).then_inc(c_act, 1)

                    @block.tensor
                    def _(pe):
                        pe.wait_ge(logf_done, 1)
                        pe.wait_ge(upto_done, 1)
                        logf = t["logf"][:].rearrange("p (t h) -> p t h", h=FOX_H)
                        for half in range(2):
                            if half:
                                for j in range(4):
                                    nc.tensor.matmul(psum[0:FOX_H, 1, :], logf[:, j, :], ones[:], start=j == 0, stop=False)
                            for j in range(4):
                                last = nc.tensor.matmul(psum[0:FOX_H, half, j * P:BANK], logf[:, 4 * half + j, :],
                                                        upto[:, 0:BANK - j * P], start=half == 0 and j == 0, stop=j == 3)
                            last.then_inc(summed, 1)

                    @block.sync
                    def _(sp):
                        sp.wait_ge(rows_done, 8)
                        sp.dma_start(c_query, cq[:].bitcast(F32)).then_inc(stored, 16)
                        sp.dma_start(c_key, ck[:].bitcast(F32)).then_inc(stored, 16)
                        sp.wait_ge(stored, 32)
                        clear_retired(sp)

        SCORE, TURN, OUT, GATE = 0, 4, 6, 7

        def pair(slot, width):
            return psum[:, SCORE + 2 * slot:SCORE + 2 * slot + 2, :].rearrange("p b c -> p (b c)")[:, 0:width]

        class GateLogits:

            def __init__(self, sc, tiles):
                self.tiles = tiles
                self.w = Weights(sc, 2 * len(tiles), stages=2, slots=2)
                self.out = sc.sb("logits_out", [P, BANK])
                self.product, self.copied, self.stored = (sc.sem(k) for k in ("logits_product", "logits_copied", "logits_stored"))
                self.w_gate = io["w_in"][0].rearrange("(k p) n -> p k n", p=P)
                self.unstored = None

            def load(self, sp, n):
                col = C_G + self.tiles[n // 2] * P
                self.w.load(sp, 0, n, self.w_gate[:, 4 * (n % 2):4 * (n % 2) + 4, col:col + P])

            def pe_unit(self, pe, u):
                w, tile, tokens, h = self.w, u // 4, (u // 2) % 2, u % 2
                cols = slice(tokens * BANK, (tokens + 1) * BANK)
                if tokens == 0:
                    w.ready(pe, 0, 2 * tile + h)
                if h == 0 and u:
                    pe.wait_ge(self.copied, u // 2)
                for kk in range(4):
                    wc = slice(kk * P, (kk + 1) * P)
                    last = three(psum[:, GATE, :], w.hi[:, h, wc], w.lo[:, h, wc], act_hi[:, 4 * h + kk, cols],
                                 act_lo[:, 4 * h + kk, cols], h == 0 and kk == 0, h == 1 and kk == 3)
                if tokens == 1:
                    last.then_inc(w.used, 1)
                elif h == 1:
                    last.then_inc(self.product, 1)

            def act_copy(self, act, u):
                tile, tokens = u // 4, (u // 2) % 2
                self.act_store(act)
                if tokens == 0:
                    act.wait_ge(self.product, tile + 1)
                else:
                    act.wait_ge(self.w.used, self.w.slots + 2 * tile + 2)
                if u > 1:
                    act.wait_ge(self.stored, 16 * (u // 2))
                nc.scalar.activation(self.out[:], psum[:, GATE, :], ACT.Copy).then_inc(self.copied, 1)
                self.unstored = u

            def act_store(self, act):
                if self.unstored is not None:
                    u, self.unstored = self.unstored, None
                    tile, tokens = u // 4, (u // 2) % 2
                    act.wait_ge(self.copied, u // 2 + 1)
                    act.dma_start(gate_logits[self.tiles[tile], :, tokens * BANK:(tokens + 1) * BANK], self.out[:]).then_inc(self.stored, 16)

        def attention_block(plan, gate_tiles):
            with Scope(plan.name) as sc:
                n = plan.steps
                probs = sc.sb("probs", [P, plan.prob_slots, D])
                ps, plan.probs = plan.prob_slots, probs
                scored, maxed, exped, normed, turned, hi_done, lo_done, valued, own = (sc.sem(k) for k in (
                    "scored", "maxed", "exped", "normed", "turned", "hi_done", "lo_done", "valued", "dve_own"))
                out_done = [sc.sem(f"out{k}") for k in range(len(plan.out_stages))]
                plan.allocate(sc)
                gates = GateLogits(sc, gate_tiles)
                items, turn_end, prepared, n_units = [], [], {}, 0
                step_items = {}
                for s in range(-1, n + 2):
                    here = [("turn", s - 2, g) for g in plan.turns(s - 2)] if s >= 2 else []
                    for job in (plan.preps(s) if s < n else ()):
                        prepared[job] = len(items) + len(here) + 1
                        here.append(("prep", job))
                    units = list(range(n_units, n_units + plan.gate_units(s)))
                    n_units += len(units)
                    work = []
                    for j, item in enumerate(here):
                        work.append((len(items) + j, item))
                        if j % 2 == 1 and units:
                            work.append((units.pop(0), ("unit",)))
                    step_items[s] = work + [(u, ("unit",)) for u in units]
                    items += here
                    if s >= 2:
                        turn_end.append(len(items) - sum(kind == "prep" for kind, *_ in here))
                assert n_units == 4 * len(gate_tiles)
                ends = [s for s in range(n) if plan.ends_unit(s)]
                unit = [sum(e < s for e in ends) for s in range(n)]

                def out_part(eng, who, s):
                    for k, (engine, fn) in reversed(list(enumerate(plan.out_stages))):
                        ended = s - 3 - k // 2
                        if engine == who and ended in ends:
                            u = ends.index(ended)
                            eng.wait_ge(out_done[k - 1] if k else valued, u + 1)
                            if k == 1 and len(out_done) == 4 and u >= plan.slots:
                                eng.wait_ge(out_done[3], u - plan.slots + 1)
                            fn(u).then_inc(out_done[k], 1)

                with nc.Block(no_gpsimd_drain=True) as block:
                    @block.tensor
                    def _(pe):
                        gates.w.start_pe(pe)

                        def transposes(s):
                            for q, (kind, *arg) in step_items[s]:
                                if kind == "unit":
                                    gates.pe_unit(pe, q)
                                    continue
                                at, *group = arg
                                if q >= 2:
                                    pe.wait_ge(lo_done, q - 1)
                                if kind == "turn":
                                    pe.wait_ge(normed, at + 1)
                                    for src, dst in group[0][0]:
                                        last = nc.tensor.transpose(psum[:, TURN + q % 2, dst:dst + P],
                                                                   probs[:, at % ps, src:src + P], ident[:])
                                else:
                                    last = plan.prep_pe(at, TURN + q % 2)
                                last.then_inc(turned, 1)

                        transposes(-1)
                        for s in range(n + 3):
                            if s < n:
                                if needed := plan.needs(s):
                                    pe.wait_ge(lo_done, prepared[needed])
                                plan.pe_inputs(pe, s)
                                if s >= 2:
                                    pe.wait_ge(exped, s - 1)
                                plan.scores(s).then_inc(scored, 1)
                            if s - 3 in ends:
                                u = ends.index(s - 3)
                                pe.wait_ge(lo_done, turn_end[s - 3])
                                if u:
                                    pe.wait_ge(out_done[plan.out_freed], u)
                                plan.values(u).then_inc(valued, 1)
                            if s < n + 2:
                                transposes(s)

                    @block.vector
                    def _(dve):
                        done = Chain(dve, own)

                        def lo_halves(s):
                            for q, (kind, *arg) in step_items[s]:
                                if kind == "unit":
                                    continue
                                at, *group = arg
                                dve.wait_ge(hi_done, q + 1)
                                if kind == "turn":
                                    moves, hi, lo = group[0]
                                    src = psum[:, TURN + q % 2, 0:len(moves) * P]
                                    last = nc.vector.tensor_tensor(lo, src if len(lo.shape) == 2 else src.rearrange(
                                        "p (a b) -> p a b", b=P), hi.bitcast(F32), ALU.subtract)
                                else:
                                    last = plan.prep_dve(at, TURN + q % 2)
                                last.then_inc(lo_done, 1)

                        lo_halves(-1)
                        plan.dve_before(dve)
                        for s in range(n + 4):
                            if s < n:
                                dve.wait_ge(scored, s + 1)
                                if plan.max_writes_probs and s >= ps:
                                    dve.wait_ge(turned, turn_end[s - ps])
                                plan.row_max(done, s).then_inc(maxed, 1)
                            if 0 <= s - 1 < n:
                                dve.wait_ge(exped, s)
                                plan.normalize(done, s - 1, probs[:, (s - 1) % ps, :]).then_inc(normed, 1)
                            if s < n + 2:
                                lo_halves(s)
                            out_part(dve, "dve", s)

                    @block.scalar
                    def _(act):
                        def hi_halves(s):
                            for q, (kind, *arg) in step_items[s]:
                                if kind == "unit":
                                    if q % 2:
                                        gates.act_copy(act, q)
                                    continue
                                at, *group = arg
                                act.wait_ge(turned, q + 1)
                                if kind == "turn":
                                    moves, hi, _ = group[0]
                                    if unit[at] >= plan.pt_slots:
                                        act.wait_ge(valued, unit[at] - plan.pt_slots + 1)
                                    src = psum[:, TURN + q % 2, 0:len(moves) * P]
                                    last = nc.scalar.activation(hi, src if len(hi.shape) == 2 else src.rearrange(
                                        "p (a b) -> p a b", b=P), ACT.Copy)
                                else:
                                    last = plan.prep_act(at, TURN + q % 2)
                                last.then_inc(hi_done, 1)

                        hi_halves(-1)
                        for s in range(n + 4):
                            if s < n:
                                act.wait_ge(maxed, s + 1)
                                if s >= ps:
                                    act.wait_ge(turned, turn_end[s - ps])
                                plan.exps(s, probs[:, s % ps, :]).then_inc(exped, 1)
                            gates.act_store(act)
                            if s < n + 2:
                                hi_halves(s)
                            out_part(act, "act", s)
                        gates.act_store(act)
                        act.wait_ge(gates.stored, 16 * 2 * len(gate_tiles))

                    @block.gpsimd
                    def _(pool):
                        gates.w.start_pool(pool)
                        for piece in range(2 * len(gate_tiles)):
                            gates.w.split_piece(pool, 0, piece)

                    @block.sync
                    def _(sp):
                        for piece in range(2 * len(gate_tiles)):
                            plan.sync(sp, piece)
                            gates.load(sp, piece)
                        clear_retired(sp)

        class HalfHeads:
            out_stages = ()
            out_freed = 1

            def allocate_out(self, sc, width, slots):
                self.slots = slots
                self.part = sc.sb("part", [P, slots, width])
                self.total = sc.sb("total", [P, slots, width])

            @staticmethod
            def value_product(out, values_tile, p_hi, p_lo, start, stop):
                if not start:
                    nc.tensor.matmul(out[0:HD], values_tile[:, 0:HD], p_lo, start=False, stop=False)
                last = nc.tensor.matmul(out, values_tile, p_hi, start=start, stop=stop and not start)
                if start and not stop:
                    last = nc.tensor.matmul(out[0:HD], values_tile[:, 0:HD], p_lo, start=False, stop=False)
                if start and stop:
                    last = nc.tensor.matmul(out, values_tile, p_lo, start=False, stop=True)
                return last

        class Fox(HalfHeads):
            steps = GROUP * NT
            pt_slots, prob_slots = 1, 2
            max_writes_probs = False
            JOBS = (1, 2, 4, 6)
            AUG = HD + 4
            UNIT = 2 * P

            def __init__(self, grp, qk, values, out_hi, out_lo):
                self.name, self.grp, self.qk, self.v, self.out_hi, self.out_lo = f"foxattn{grp}", grp, qk, values, out_hi, out_lo
                self.out_stages = (("act", self.out_part), ("dve", self.out_sum), ("act", self.out_round), ("dve", self.out_rest))

            def allocate(self, sc):
                self.q1 = sc.sb("q1", [P, 2, S], F32R)
                self.k1 = sc.sb("k1", [P, 2, S], F32R)
                self.q2 = sc.sb("q2", [P, 2, S], F32R)
                self.k2 = sc.sb("k2", [P, 2, S], F32R)
                self.pt_hi = sc.sb("pt_hi", [P, NT, self.UNIT], F32R)
                self.pt_lo = sc.sb("pt_lo", [P, NT, self.UNIT], F32R)
                self.stat = sc.sb("stat", [P, 3, 3])
                self.allocate_out(sc, self.UNIT, 1)
                self.rows_landed = [sc.sem(f"rows_landed{b}") for b in range(2)]
                self.scored_heads = sc.sem("scored_heads")

            def preps(self, s):
                head, i = divmod(s, NT)
                if s < 0:
                    return [(0, part) for part in range(4)]
                return [(head + 1, self.JOBS.index(i))] if i in self.JOBS and head + 1 < GROUP else []

            def needs(self, s):
                return (s // NT, 3) if s % NT == 0 else None

            def gate_units(self, s):
                return 1 if 1 <= s <= self.steps else 0

            def prep_pe(self, job, bank):
                head, part = job
                col = (part // 2) * GROUP * HD + head * HD
                for t in range(4):
                    last = nc.tensor.transpose(psum[0:HD, bank, t * P:(t + 1) * P],
                                               self.qk[:, 4 * (part % 2) + t, col:col + HD], ident[:])
                return last

            def prep_act(self, job, bank):
                head, part = job
                b, cols = head % 2, slice((part % 2) * BANK, (part % 2 + 1) * BANK)
                gain = vecs[0:HD, QN_F:QN_F + 1] if part < 2 else vecs[0:HD, KN_F:KN_F + 1]
                src = psum[0:HD, bank, :]
                again = self.q2[0:HD, b, cols] if part < 2 else self.k1[HD:P, b, cols]
                nc.scalar.activation(again, src, ACT.Copy, scale=gain)
                return nc.scalar.activation((self.q1 if part < 2 else self.k1)[0:HD, b, cols], src, ACT.Copy, scale=gain)

            def prep_dve(self, job, bank):
                head, part = job
                b, cols = head % 2, slice((part % 2) * BANK, (part % 2 + 1) * BANK)
                at = QN_F if part < 2 else KN_F
                lo = self.q1[HD:P, b, cols] if part < 2 else self.k2[0:HD, b, cols]
                hi = (self.q1 if part < 2 else self.k1)[0:HD, b, cols]
                return nc.vector.scalar_tensor_tensor(out=lo, in0=psum[0:HD, bank, :], scalar=vecs[0:HD, at:at + 1],
                                                      in1=hi.bitcast(F32), op0=ALU.mult, op1=ALU.subtract)

            def dve_before(self, dve):
                pass

            def sync(self, sp, piece):
                for head in {0: (0, 1), 8: (2,), 12: (3,)}.get(piece, ()):
                    b = head % 2
                    if head >= 2:
                        sp.wait_ge(self.scored_heads, head - 1)
                    h = self.grp * GROUP + head
                    sp.dma_start(self.q2[HD:self.AUG, b, :].bitcast(F32), c_query[h]).then_inc(self.rows_landed[b], 16)
                    sp.dma_start(self.k2[HD:self.AUG, b, :].bitcast(F32), c_key[h]).then_inc(self.rows_landed[b], 16)

            def pe_inputs(self, pe, s):
                head, i = divmod(s, NT)
                if i == 0:
                    pe.wait_ge(self.rows_landed[head % 2], 32 * (head // 2 + 1))

            def scores(self, s):
                head, i = divmod(s, NT)
                b, rows, keys = head % 2, slice(i * P, (i + 1) * P), (i + 1) * P
                for half in range((keys + BANK - 1) // BANK):
                    cols = slice(half * BANK, min(keys, (half + 1) * BANK))
                    out = psum[:, SCORE + 2 * (s % 2) + half, 0:cols.stop - cols.start]
                    diagonal = keys <= (half + 1) * BANK
                    nc.tensor.matmul(out, self.q1[:, b, rows], self.k1[:, b, cols], start=True, stop=False)
                    last = nc.tensor.matmul(out, self.q2[0:self.AUG, b, rows], self.k2[0:self.AUG, b, cols],
                                            start=False, stop=not diagonal)
                    if i == NT - 1 and half == 1:
                        last.then_inc(self.scored_heads, 1)
                    if diagonal:
                        last = nc.tensor.matmul(out[:, i * P - cols.start:], ident_r[:], causal_r[:], start=False, stop=True)
                return last

            def row_max(self, done, s):
                return nc.vector.tensor_reduce(self.stat[:, s % 3, 0:1], pair(s % 2, (s % NT + 1) * P), AX.X, ALU.max, negate=True)

            def exps(self, s, probs):
                keys = (s % NT + 1) * P
                return nc.scalar.activation(probs[:, 0:keys], pair(s % 2, keys), ACT.Exp, bias=self.stat[:, s % 3, 0:1],
                                            accum_out=self.stat[:, s % 3, 1:2])

            def normalize(self, done, s, probs):
                keys, st = (s % NT + 1) * P, self.stat
                done(nc.vector.reciprocal(st[:, s % 3, 2:3], st[:, s % 3, 1:2]))
                return nc.vector.tensor_scalar(probs[:, 0:keys], probs[:, 0:keys], st[:, s % 3, 2:3], None, ALU.mult)

            def turns(self, s):
                i = s % NT
                cols = slice((i % 2) * P, (i % 2 + 1) * P)
                out = []
                for k0 in range(0, i + 1, 4):
                    k1 = min(k0 + 4, i + 1)
                    out.append(([(k * P, (k - k0) * P) for k in range(k0, k1)],
                                self.pt_hi[:, k0:k1, cols], self.pt_lo[:, k0:k1, cols]))
                return out

            def ends_unit(self, s):
                return s % 2 == 1

            def values(self, u):
                head, sb = divmod(u, NT // 2)
                last_key = 2 * sb + 1
                for k in range(last_key + 1):
                    c0 = max(0, k - 2 * sb) * P
                    last = self.value_product(psum[:, OUT, c0:self.UNIT], self.v[:, k, head, :], self.pt_hi[:, k, c0:self.UNIT],
                                              self.pt_lo[:, k, c0:self.UNIT], k == 0, k == last_key)
                return last

            def _place(self, u):
                head, sb = divmod(u, NT // 2)
                h = self.grp * GROUP + head
                return slice((h % 2) * HD, (h % 2 + 1) * HD), h // 2, slice(sb * self.UNIT, (sb + 1) * self.UNIT), u % self.slots

            def out_part(self, u):
                rows, _, _, slot = self._place(u)
                return nc.scalar.activation(self.part[rows, slot, :], psum[HD:P, OUT, 0:self.UNIT], ACT.Copy)

            def out_sum(self, u):
                rows, _, _, slot = self._place(u)
                return nc.vector.tensor_tensor(self.total[rows, slot, :], psum[0:HD, OUT, 0:self.UNIT], self.part[rows, slot, :], ALU.add)

            def out_round(self, u):
                rows, kt, cols, slot = self._place(u)
                return nc.scalar.activation(self.out_hi[rows, kt, cols], self.total[rows, slot, :], ACT.Copy)

            def out_rest(self, u):
                rows, kt, cols, slot = self._place(u)
                return nc.vector.tensor_tensor(self.out_lo[rows, kt, cols], self.total[rows, slot, :],
                                               self.out_hi[rows, kt, cols].bitcast(F32), ALU.subtract)

        class Mem:
            name = "memattn"
            steps = MEM_H * 2
            pt_slots, prob_slots = 2, 3
            max_writes_probs = False
            out_freed = 1
            SCALE = MEM_D ** -0.5

            def __init__(self, q, k, v_hi, v_lo, out_hi, out_lo):
                self.q, self.k, self.v_hi, self.v_lo, self.out_hi, self.out_lo = q, k, v_hi, v_lo, out_hi, out_lo
                self.out_stages = (("act", self.out_round), ("dve", self.out_rest))

            def allocate(self, sc):
                self.q_t = [sc.sb(f"q_{h}", [P, 2, S], F32R) for h in ("hi", "lo")]
                self.k_t = [sc.sb(f"k_{h}", [P, 2, M], F32R) for h in ("hi", "lo")]
                self.pt = [sc.sb(f"pt_{h}", [P, 2, 2, BANK], F32R) for h in ("hi", "lo")]
                self.stat = sc.sb("stat", [P, 4, 3, 4])

            def preps(self, s):
                head = s // 2 + 1
                return [(head, part) for part in range(3)] if s % 2 == (s < 0) and head < MEM_H else []

            def needs(self, s):
                return (s // 2, 2) if s % 2 == 0 else None

            def gate_units(self, s):
                return 1 if 1 <= s <= self.steps else 0

            def _job(self, job):
                head, part = job
                if part == 0:
                    return self.k, range(2), [t[:, head % 2, :] for t in self.k_t], vecs[:, KN_M:KN_M + 1]
                return (self.q, range(4 * part - 4, 4 * part), [t[:, head % 2, (part - 1) * BANK:part * BANK] for t in self.q_t],
                        vecs[:, QN_M:QN_M + 1])

            def prep_pe(self, job, bank):
                tok, tiles, _, _ = self._job(job)
                for i, t in enumerate(tiles):
                    last = nc.tensor.transpose(psum[:, bank, i * P:(i + 1) * P], tok[:, t, job[0] * P:(job[0] + 1) * P], ident[:])
                return last

            def prep_act(self, job, bank):
                _, tiles, dst, gain = self._job(job)
                return nc.scalar.activation(dst[0], psum[:, bank, 0:len(tiles) * P], ACT.Copy, scale=gain)

            def prep_dve(self, job, bank):
                _, tiles, dst, gain = self._job(job)
                return nc.vector.scalar_tensor_tensor(out=dst[1], in0=psum[:, bank, 0:len(tiles) * P], scalar=gain,
                                                      in1=dst[0].bitcast(F32), op0=ALU.mult, op1=ALU.subtract)

            def dve_before(self, dve):
                pass

            def sync(self, sp, piece):
                pass

            def pe_inputs(self, pe, s):
                pass

            def scores(self, s):
                head, half = divmod(s, 2)
                for j in range(4):
                    rows = slice((4 * half + j) * P, (4 * half + j + 1) * P)
                    out = psum[:, SCORE + 2 * (s % 2) + j // 2, (j % 2) * M:(j % 2 + 1) * M]
                    last = three(out, self.q_t[0][:, head % 2, rows], self.q_t[1][:, head % 2, rows],
                                 self.k_t[0][:, head % 2, :], self.k_t[1][:, head % 2, :], True, True)
                return last

            def row_max(self, done, s):
                b = s % 3
                done(nc.vector.tensor_reduce(self.stat[:, 0, b, :], pair(s % 2, S).rearrange("p (j m) -> p j m", m=M), AX.X, ALU.max))
                return nc.vector.tensor_scalar(self.stat[:, 1, b, :], self.stat[:, 0, b, :], -self.SCALE, None, ALU.mult)

            def exps(self, s, probs):
                for j in range(4):
                    cols = slice(j * M, (j + 1) * M)
                    last = nc.scalar.activation(probs[:, cols], pair(s % 2, S)[:, cols], ACT.Exp, scale=self.SCALE,
                                                bias=self.stat[:, 1, s % 3, j:j + 1], accum_out=self.stat[:, 2, s % 3, j:j + 1])
                return last

            def normalize(self, done, s, probs):
                st = self.stat
                done(nc.vector.reciprocal(st[:, 3, s % 3, :], st[:, 2, s % 3, :]))
                for j in range(4):
                    cols = slice(j * M, (j + 1) * M)
                    last = nc.vector.tensor_scalar(probs[:, cols], probs[:, cols], st[:, 3, s % 3, j:j + 1], None, ALU.mult)
                return last

            def turns(self, s):
                return [([(j * M + m * P, j * P) for j in range(4)], self.pt[0][:, s % 2, m, :], self.pt[1][:, s % 2, m, :])
                        for m in range(2)]

            def ends_unit(self, s):
                return True

            def values(self, u):
                head = u // 2
                cols = slice(head * MEM_D, (head + 1) * MEM_D)
                for m in range(2):
                    last = three(psum[:, OUT, :], self.v_hi[:, m, cols], self.v_lo[:, m, cols],
                                 self.pt[0][:, u % 2, m, :], self.pt[1][:, u % 2, m, :], m == 0, m == 1)
                return last

            def _dst(self, t, u):
                return t[:, u // 2, (u % 2) * BANK:(u % 2 + 1) * BANK]

            def out_round(self, u):
                return nc.scalar.activation(self._dst(self.out_hi, u), psum[:, OUT, :], ACT.Copy)

            def out_rest(self, u):
                return nc.vector.tensor_tensor(self._dst(self.out_lo, u), psum[:, OUT, :],
                                               self._dst(self.out_hi, u).bitcast(F32), ALU.subtract)

        class Swa(HalfHeads):
            name = "swaattn"
            steps = SWA_KV * NT
            pt_slots, prob_slots = 1, 3
            max_writes_probs = True
            KW = 2 * P

            def __init__(self, q, k, values, out_hi, out_lo):
                self.q, self.k, self.v, self.out_hi, self.out_lo = q, k, values, out_hi, out_lo
                self.out_stages = (("act", self.out_part), ("dve", self.out_sum), ("act", self.out_round), ("dve", self.out_rest))

            def allocate(self, sc):
                self.q1 = sc.sb("q1", [P, 2, GROUP, BANK], F32R)
                self.k1 = sc.sb("k1", [P, SWA_KV, S], F32R)
                self.k2 = sc.sb("k2", [HD, SWA_KV, S], F32R)
                self.pt = [sc.sb(f"pt_{h}", [P, 2, BANK], F32R) for h in ("hi", "lo")]
                self.bias = sc.sb("bias", [P, SWA_H, self.KW])
                self.stat = sc.sb("stat", [P, 6, 3, GROUP])
                self.allocate_out(sc, 2 * P, 1)
                self.bias_landed = sc.sem("bias_landed")

            def preps(self, s):
                if s < 0:
                    return [("k", 0, 0), ("k", 0, 1)] + [("q", 0, j) for j in range(GROUP)]
                jobs = [("q", s // 4 + 1, s % 4)] if s // 4 + 1 < self.steps // 4 else []
                return jobs + {3: [("k", 1, 0)], 5: [("k", 1, 1)]}.get(s, [])

            def needs(self, s):
                return ("q", s // 4, GROUP - 1) if s % 4 == 0 else None

            def gate_units(self, s):
                return 1 + s % 2 if 1 <= s <= self.steps else 0

            def _job(self, job):
                kind, at, j = job
                if kind == "k":
                    cols = slice(j * BANK, (j + 1) * BANK)
                    return self.k, at * HD, j, self.k1[0:HD, at, cols], self.k1[HD:P, at, cols], self.k2[:, at, cols], KN_A
                g, half = divmod(at, 2)
                return self.q, (GROUP * g + j) * HD, half, self.q1[0:HD, at % 2, j, :], None, self.q1[HD:P, at % 2, j, :], QN_A

            def prep_pe(self, job, bank):
                tok, col, half, *_ = self._job(job)
                for t in range(4):
                    last = nc.tensor.transpose(psum[0:HD, bank, t * P:(t + 1) * P], tok[:, 4 * half + t, col:col + HD], ident[:])
                return last

            def prep_act(self, job, bank):
                *_, hi, again, _, at = self._job(job)
                gain = vecs[0:HD, at:at + 1]
                if again is not None:
                    nc.scalar.activation(again, psum[0:HD, bank, :], ACT.Copy, scale=gain)
                return nc.scalar.activation(hi, psum[0:HD, bank, :], ACT.Copy, scale=gain)

            def prep_dve(self, job, bank):
                *_, hi, _, lo, at = self._job(job)
                return nc.vector.scalar_tensor_tensor(out=lo, in0=psum[0:HD, bank, :], scalar=vecs[0:HD, at:at + 1],
                                                      in1=hi.bitcast(F32), op0=ALU.mult, op1=ALU.subtract)

            def dve_before(self, dve):
                dve.wait_ge(self.bias_landed, 16)

            def sync(self, sp, piece):
                if piece == 0:
                    sp.dma_start(self.bias[:], bass.AP(diagonals.tensor, P - 1, [[SWA_H * (DIAGS + 1) - 1, P], [DIAGS + 1, SWA_H], [1, self.KW]])
                                 ).then_inc(self.bias_landed, 16)

            def pe_inputs(self, pe, s):
                pass

            def _cols(self, s, j):
                return slice(j * self.KW + (P if s % NT == 0 else 0), (j + 1) * self.KW)

            def scores(self, s):
                g, n = divmod(s, NT)
                keys = slice(max(n - 1, 0) * P, (n + 1) * P)
                rows, chunk = slice(n % 4 * P, (n % 4 + 1) * P), s // 4 % 2
                for j in range(GROUP):
                    out = pair(s % 2, S)[:, self._cols(s, j)]
                    nc.tensor.matmul(out, self.q1[:, chunk, j, rows], self.k1[:, g, keys], start=True, stop=False)
                    last = nc.tensor.matmul(out, self.q1[0:HD, chunk, j, rows], self.k2[:, g, keys], start=False, stop=True)
                return last

            def row_max(self, done, s):
                g, b, st = s // NT, s % 3, self.stat
                for j in range(GROUP):
                    h, cols = GROUP * g + j, self._cols(s, j)
                    done.count(nc.vector.tensor_tensor_reduce(
                        out=self.probs[:, b, cols], in0=pair(s % 2, S)[:, cols],
                        in1=self.bias[:, h, cols.start - j * self.KW:], scale=1.0, scalar=sinks[:, h:h + 1],
                        op0=ALU.add, op1=ALU.max, accum_out=st[:, 0, b, j:j + 1]))
                done.wait()
                nc.vector.tensor_scalar(st[:, 1, b, :], st[:, 0, b, :], -1.0, None, ALU.mult)
                return nc.vector.tensor_tensor(st[:, 2, b, :], sinks[:, GROUP * g:GROUP * (g + 1)], st[:, 0, b, :], ALU.subtract)

            def exps(self, s, probs):
                st, b = self.stat, s % 3
                nc.scalar.activation(st[:, 3, b, :], st[:, 2, b, :], ACT.Exp)
                for j in range(GROUP):
                    cols = self._cols(s, j)
                    last = nc.scalar.activation(probs[:, cols], probs[:, cols], ACT.Exp, bias=st[:, 1, b, j:j + 1],
                                                accum_out=st[:, 4, b, j:j + 1])
                return last

            def normalize(self, done, s, probs):
                st, b = self.stat, s % 3
                done(nc.vector.tensor_tensor(st[:, 5, b, :], st[:, 4, b, :], st[:, 3, b, :], ALU.add))
                done(nc.vector.reciprocal(st[:, 5, b, :], st[:, 5, b, :]))
                for j in range(GROUP):
                    cols = self._cols(s, j)
                    last = nc.vector.tensor_scalar(probs[:, cols], probs[:, cols], st[:, 5, b, j:j + 1], None, ALU.mult)
                return last

            def turns(self, s):
                return [([(j * self.KW + kb * P, j * P) for j in range(GROUP)], self.pt[0][:, kb, :], self.pt[1][:, kb, :])
                        for kb in ((1,) if s % NT == 0 else (0, 1))]

            def ends_unit(self, s):
                return True

            def values(self, u):
                g, n = divmod(u, NT)
                kbs = (1,) if n == 0 else (0, 1)
                for kb in kbs:
                    last = self.value_product(psum[:, OUT, :], self.v[:, n - 1 + kb, g, :], self.pt[0][:, kb, :],
                                              self.pt[1][:, kb, :], kb == kbs[0], kb == 1)
                return last

            def _heads(self, ap, parity):
                return ap.rearrange("p (a b c) -> p a b c", b=2, c=P)[:, :, parity, :]

            def out_part(self, u):
                for parity in range(2):
                    rows = slice(parity * HD, (parity + 1) * HD)
                    last = nc.scalar.activation(self.part[rows, 0, :].rearrange("p (a c) -> p a c", c=P),
                                                self._heads(psum[HD:P, OUT, :], parity), ACT.Copy)
                return last

            def out_sum(self, u):
                for parity in range(2):
                    rows = slice(parity * HD, (parity + 1) * HD)
                    last = nc.vector.tensor_tensor(self.total[rows, 0, :].rearrange("p (a c) -> p a c", c=P),
                                                   self._heads(psum[0:HD, OUT, :], parity),
                                                   self.part[rows, 0, :].rearrange("p (a c) -> p a c", c=P), ALU.add)
                return last

            def _dst(self, t, u):
                g, n = divmod(u, NT)
                return t[:, 2 * g:2 * g + 2, n * P:(n + 1) * P]

            def out_round(self, u):
                return nc.scalar.activation(self._dst(self.out_hi, u), self.total[:, 0, :].rearrange("p (a c) -> p a c", c=P), ACT.Copy)

            def out_rest(self, u):
                return nc.vector.tensor_tensor(self._dst(self.out_lo, u), self.total[:, 0, :].rearrange("p (a c) -> p a c", c=P),
                                               self._dst(self.out_hi, u).bitcast(F32), ALU.subtract)

        def merge_block(swa_hi, swa_lo):
            weights = [io["w_o_swa"], io["w_o_fox"], io["w_o_mem"]]
            with Scope("merge") as sc:
                w = Weights(sc, 3, stages=3, slots=3)
                halves = {0: (swa_hi, swa_lo)}
                for b in (1, 2):
                    halves[b] = tuple(sc.sb(f"branch{b}_{h}", [P, 4, S], F32R) for h in ("hi", "lo"))
                branch_landed = {b: sc.sem(f"branch{b}_landed") for b in (1, 2)}
                gate = sc.sb("gate", [P, 3, S])
                gate_landed = [sc.sem(f"gate_landed{b}") for b in range(3)]
                merged = sc.sb("merged", [P, 2, BANK])
                product = sc.sb("product", [P, 2, BANK])
                gated, multiplied, added, hi_done, lo_done = (sc.sem(k) for k in ("gated", "multiplied", "added", "hi_done", "lo_done"))
                w_branch = [wo[0].rearrange("(k p) n -> p k n", p=P) for wo in weights]

                with nc.Block(no_gpsimd_drain=True) as block:
                    @block.sync
                    def _(sp):
                        with sp.Fori(0, KD) as i:
                            for b in range(3):
                                w.load(sp, i, b, w_branch[b][:, :, bass.ds(i * P, P)])
                                sp.wait_ge(multiplied, i * 6 + 2 * b + 2)
                                sp.sem_inc(w.asked, 1)
                                sp.dma_start(gate[:, b, :], gate_logits[bass.ds(i + b * KD, 1), :, :].rearrange("a p n -> (a p) n")
                                             ).then_inc(gate_landed[b], 16)
                        clear_retired(sp)

                    @block.gpsimd
                    def _(pool):
                        w.start_pool(pool)
                        with pool.Fori(0, KD) as i:
                            for n in range(3):
                                w.split_piece(pool, i, n)

                    @block.tensor
                    def _(pe):
                        w.start_pe(pe)
                        with pe.Fori(0, KD) as i:
                            for b in range(3):
                                w.ready(pe, i, b)
                                if b:
                                    pe.wait_ge(branch_landed[b], 32)
                                pe.wait_ge(multiplied, i * 6 + 2 * b + 2)
                                o_hi, o_lo = halves[b]
                                for kk in range(4):
                                    for half in range(2):
                                        cols, wc = slice(half * BANK, (half + 1) * BANK), slice(kk * P, (kk + 1) * P)
                                        last = three(psum[:, 2 * b + half, :], w.hi[:, b, wc], w.lo[:, b, wc],
                                                     o_hi[:, kk, cols], o_lo[:, kk, cols], kk == 0, kk == 3)
                                last.then_inc(w.used, 1)

                    @block.scalar
                    def _(act):
                        for b in (1, 2):
                            for h in range(2):
                                act.dma_start(halves[b][h][:].bitcast(F32), branch_out[b][h]).then_inc(branch_landed[b], 16)
                        with act.Fori(0, KD) as i:
                            for b in range(3):
                                act.wait_ge(gate_landed[b], i * 16 + 16)
                                nc.scalar.activation(gate[:, b, :], gate[:, b, :], ACT.Sigmoid,
                                                     bias=vecs[:, bass.ds(i + (B_GATE + b * KD), 1)]).then_inc(gated, 1)
                            for half in range(2):
                                act.wait_ge(added, i * 4 + (half + 5))
                                cols = slice(half * BANK, (half + 1) * BANK)
                                nc.scalar.activation(act_hi[:, bass.ds(i, 1), cols].rearrange("p a n -> p (a n)"), merged[:, half, :],
                                                     ACT.Copy).then_inc(hi_done, 1)

                    @block.vector
                    def _(dve):
                        dve.sem_inc(multiplied, 6)
                        dve.sem_inc(added, 2)
                        dve.sem_inc(lo_done, 2)
                        with dve.Fori(0, KD) as i:
                            for b in range(3):
                                dve.wait_ge(w.used, i * 3 + (b + 1 + w.slots))
                                dve.wait_ge(gated, i * 3 + (b + 1))
                                for half in range(2):
                                    cols = slice(half * BANK, (half + 1) * BANK)
                                    if b:
                                        dst = product
                                        dve.wait_ge(added, i * 4 + (2 * b + half - 1))
                                    else:
                                        dst = merged
                                        dve.wait_ge(lo_done, i * 2 + (half + 1))
                                    nc.vector.tensor_tensor(dst[:, half, :], psum[:, 2 * b + half, :], gate[:, b, cols],
                                                            ALU.mult).then_inc(multiplied, 1)
                                if b:
                                    for half in range(2):
                                        dve.wait_ge(multiplied, i * 6 + (2 * b + half + 1 + 6))
                                        nc.vector.tensor_tensor(merged[:, half, :], merged[:, half, :], product[:, half, :],
                                                                ALU.add).then_inc(added, 1)
                            for half in range(2):
                                cols = slice(half * BANK, (half + 1) * BANK)
                                dve.wait_ge(hi_done, i * 2 + (half + 1))
                                nc.vector.tensor_tensor(act_lo[:, bass.ds(i, 1), cols].rearrange("p a n -> p (a n)"), merged[:, half, :],
                                                        act_hi[:, bass.ds(i, 1), cols].rearrange("p a n -> p (a n)").bitcast(F32),
                                                        ALU.subtract).then_inc(lo_done, 1)

        def out_block(x2):
            with Scope("wout") as sc:
                w = Weights(sc, 2 * KD)
                x_landed = [sc.sem(f"x_landed{t}") for t in range(NT)]
                filled, added = sc.sem("filled"), sc.sem("added")
                with nc.Block(no_gpsimd_drain=True) as block:
                    @block.sync
                    def _(sp):
                        for k in range(KD):
                            w.load(sp, 0, k, w_rows(io["w_out"], k, 0, BANK))
                        for k in range(KD):
                            w.load(sp, 0, KD + k, w_rows(io["w_out"], k, BANK, D))
                        clear_retired(sp)

                    @block.gpsimd
                    def _(pool):
                        w.start_pool(pool)
                        for n in range(2 * KD):
                            w.split_piece(pool, 0, n)

                    @block.scalar
                    def _(act):
                        for t in range(NT):
                            act.dma_start(x2[:, t, :], io["x"][0, t * P:(t + 1) * P, :]).then_inc(x_landed[t], 16)

                    @block.tensor
                    def _(pe):
                        w.start_pe(pe)
                        for c in range(2):
                            for k in range(KD):
                                n = c * KD + k
                                w.ready(pe, 0, n)
                                for t in range(NT):
                                    if c and k == 0:
                                        pe.wait_ge(added, t + 1)
                                    rows = slice(t * P, (t + 1) * P)
                                    last = three(psum[:, t, :], act_hi[:, k, rows], act_lo[:, k, rows], w.hi[:, n % w.slots, :],
                                                 w.lo[:, n % w.slots, :], k == 0, k == KD - 1)
                                    if k == KD - 1 and t < NT - 1:
                                        last.then_inc(filled, 1)
                                last.then_inc(w.used, 1)

                    @block.vector
                    def _(dve):
                        for c in range(2):
                            for t in range(NT):
                                if t < NT - 1:
                                    dve.wait_ge(filled, c * (NT - 1) + t + 1)
                                else:
                                    dve.wait_ge(w.used, w.slots + (c + 1) * KD)
                                dve.wait_ge(x_landed[t], 16)
                                cols = slice(c * BANK, (c + 1) * BANK)
                                nc.vector.tensor_tensor(x2[:, t, cols], x2[:, t, cols], psum[:, t, :], ALU.add).then_inc(added, 1)

        def mlp_norm_block(x2):
            with Scope("mlpnorm") as sc:
                act_stats, pool_stats, pe_turn, act_hi_half, dve_part, _, _ = norm_to_features(
                    sc, x2, NT, G_MLP, act_hi, act_lo, lambda e, t: None)
                with nc.Block(no_gpsimd_drain=True) as block:
                    @block.sync
                    def _(sp):
                        clear_retired(sp)

                    @block.gpsimd
                    def _(pool):
                        pool_stats(pool)

                    @block.scalar
                    def _(act):
                        act_stats(act)
                        act_hi_half(act)

                    @block.tensor
                    def _(pe):
                        pe_turn(pe)

                    @block.vector
                    def _(dve):
                        dve_part(dve)

        def mlp_block(x2):
            FB = 8
            TURNS = FF // (FB * P)
            UP, DOWN = 2 * FB, 2 * FB
            OUTS = 2 * NT
            with Scope("mlp") as sc:
                w = Weights(sc, UP + DOWN, slots=4)
                u_hi = sc.sb("u_hi", [P, FB, S], F32R)
                u_lo = sc.sb("u_lo", [P, FB, S], F32R)
                relu = sc.sb("relu", [P, 2, BANK])
                square = sc.sb("square", [P, 2, BANK])
                relu_done, square_done, hi_done, lo_done, filled, added = (sc.sem(k) for k in (
                    "relu_done", "square_done", "hi_done", "lo_done", "filled", "added"))
                out_stored = sc.sem("out_stored")
                w_up = io["w_mlp_up"][0].rearrange("(k p) n -> p k n", p=P)
                w_down = io["w_mlp_down"][0].rearrange("(t k p) n -> p t k n", p=P, k=FB)

                with nc.Block(no_gpsimd_drain=True) as block:
                    @block.sync
                    def _(sp):
                        with sp.Fori(0, TURNS) as i:
                            for fb in range(FB):
                                for h in range(2):
                                    w.load(sp, i, 2 * fb + h, w_up[:, 4 * h:4 * h + 4, bass.ds(i * (FB * P) + fb * P, P)])
                            for c in range(2):
                                for k in range(FB):
                                    w.load(sp, i, UP + c * FB + k,
                                           w_down[:, bass.ds(i, 1), k, c * BANK:(c + 1) * BANK].rearrange("p a n -> p (a n)"))
                        for c in range(2):
                            for t in range(NT):
                                cols = slice(c * BANK, (c + 1) * BANK)
                                sp.wait_ge(added, OUTS * TURNS + c * NT + t + 1)
                                sp.dma_start(io["out"][0, t * P:(t + 1) * P, cols], x2[:, t, cols]).then_inc(out_stored, 16)
                        sp.wait_ge(out_stored, 16 * 2 * NT)
                        clear_retired(sp)

                    @block.gpsimd
                    def _(pool):
                        w.start_pool(pool)
                        with pool.Fori(0, TURNS) as i:
                            for n in range(UP + DOWN):
                                w.split_piece(pool, i, n)

                    @block.tensor
                    def _(pe):
                        w.start_pe(pe)
                        with pe.Fori(0, TURNS) as i:
                            for fb in range(FB):
                                for h in range(2):
                                    n = 2 * fb + h
                                    w.ready(pe, i, n)
                                    if h == 0 and fb < 2:
                                        pe.wait_ge(added, i * OUTS + OUTS - 2 + 2 * fb)
                                    elif h == 0:
                                        pe.wait_ge(relu_done, i * (2 * FB) + 2 * fb - 2)
                                    for kk in range(4):
                                        for half in range(2):
                                            cols = slice(half * BANK, (half + 1) * BANK)
                                            wc = slice(kk * P, (kk + 1) * P)
                                            k = 4 * h + kk
                                            last = three(psum[:, 2 * (fb % 2) + half, :], w.hi[:, n % w.slots, wc], w.lo[:, n % w.slots, wc],
                                                         act_hi[:, k, cols], act_lo[:, k, cols], k == 0, k == KD - 1)
                                    last.then_inc(w.used, 1)
                            for c in range(2):
                                for k in range(FB):
                                    n = UP + c * FB + k
                                    w.ready(pe, i, n)
                                    if c == 0:
                                        pe.wait_ge(lo_done, i * (2 * FB) + 2 * k + 4)
                                    for t in range(NT):
                                        bank = (t + 4) % 8
                                        if k == 0 and c == 0 and bank < 4:
                                            pe.wait_ge(relu_done, i * (2 * FB) + 2 * FB - 3 + bank)
                                        if k == 0 and c == 1:
                                            pe.wait_ge(added, i * OUTS + OUTS + t + 1)
                                        rows = slice(t * P, (t + 1) * P)
                                        last = three(psum[:, bank, :], u_hi[:, k, rows], u_lo[:, k, rows],
                                                     w.hi[:, n % w.slots, :], w.lo[:, n % w.slots, :], k == 0, k == FB - 1)
                                        if k == FB - 1 and t < NT - 1:
                                            last.then_inc(filled, 1)
                                    last.then_inc(w.used, 1)

                    @block.scalar
                    def _(act):
                        with act.Fori(0, TURNS) as i:
                            for fb in range(FB):
                                act.wait_ge(w.used, i * w.per + 2 * fb + 2 + w.slots)
                                for half in range(2):
                                    n = 2 * fb + half
                                    nc.scalar.activation(relu[:, half, :], psum[:, 2 * (fb % 2) + half, :], ACT.Relu).then_inc(relu_done, 1)
                                    act.wait_ge(relu_done, i * (2 * FB) + n + 1)
                                    act.wait_ge(lo_done, i * (2 * FB) + n + 1)
                                    nc.scalar.activation(square[:, half, :], relu[:, half, :], ACT.Square).then_inc(square_done, 1)

                    @block.vector
                    def _(dve):
                        dve.sem_inc(lo_done, 2)
                        dve.sem_inc(added, OUTS)
                        with dve.Fori(0, TURNS) as i:
                            dve.wait_ge(w.used, i * w.per + w.slots)
                            for n in range(2 * FB):
                                cols = slice((n % 2) * BANK, (n % 2 + 1) * BANK)
                                dve.wait_ge(square_done, i * (2 * FB) + n + 1)
                                nc.vector.tensor_copy(u_hi[:, n // 2, cols], square[:, n % 2, :]).then_inc(hi_done, 1)
                                dve.wait_ge(hi_done, i * (2 * FB) + n + 1)
                                nc.vector.tensor_tensor(u_lo[:, n // 2, cols], square[:, n % 2, :],
                                                        u_hi[:, n // 2, cols].bitcast(F32), ALU.subtract).then_inc(lo_done, 1)
                            for c in range(2):
                                for t in range(NT):
                                    if t < NT - 1:
                                        dve.wait_ge(filled, i * (2 * NT - 2) + c * (NT - 1) + t + 1)
                                    else:
                                        dve.wait_ge(w.used, i * w.per + UP + (c + 1) * FB + w.slots)
                                    cols = slice(c * BANK, (c + 1) * BANK)
                                    nc.vector.tensor_tensor(x2[:, t, cols], x2[:, t, cols], psum[:, (t + 4) % 8, :], ALU.add).then_inc(added, 1)

        def w_rows(weights, k, lo, hi):
            return weights[0, k * P:(k + 1) * P, lo:hi]

        stop = io.get("stop")
        w_in = io["w_in"]

        def columns(weights, lo, width):
            return lambda k: [w_rows(weights, k, lo, lo + width)]

        tokens = (act_hi, act_lo, NT)
        setup_block()
        with ExitStack() as outs:
            out_hi = tensor(outs, "out_hi", [P, 4, S], F32R)
            out_lo = tensor(outs, "out_lo", [P, 4, S], F32R)

            for grp in range(FOX_H // GROUP):
                with Scope(f"fox{grp}") as fx:
                    gw = GROUP * HD
                    qk = fx.sb("qk", [P, NT, BANK])
                    values = fx.sb("values", [P, NT, GROUP, 2 * HD], F32R)
                    logits = fx.sb("logits", [P, NT, FOX_H]) if grp == 0 else None

                    def qk_source(k):
                        first = w_rows(w_in, k, C_QF + grp * gw, C_QF + grp * gw + 1)
                        return [bass.AP(w_in.tensor, first.offset, [[w_in.shape[2], P], [C_KF - C_QF, 2], [1, gw]])]

                    def v_source(k):
                        v = w_rows(w_in, k, C_VF + grp * gw, C_VF + (grp + 1) * gw)
                        return [v] + ([w_rows(w_in, k, C_FL, C_FL + FOX_H)] if grp == 0 else [])

                    value = {"view": lambda ps: ps[:, 0:gw].rearrange("p (h d) -> p h d", d=HD),
                             "hi": lambda t: values[:, t, :, 0:HD], "lo": lambda t: values[:, t, :, HD:2 * HD]}
                    if grp == 0:
                        value["logits"] = lambda t: logits[:, t, :]
                    project_block(f"foxproj{grp}", [
                        {"rows": tokens, "width": BANK, "src": qk_source, "norm": {"heads": 2 * GROUP, "hd": HD, "dst": qk}},
                        {"rows": tokens, "width": gw + (FOX_H if grp == 0 else 0), "src": v_source, "value": value}])
                    if grp == 0:
                        decay_block(logits[:].rearrange("p t h -> p (t h)"))
                    if stop == "decay":
                        return
                    attention_block(Fox(grp, qk, values, out_hi, out_lo), range(grp * KD, (grp + 1) * KD))
                if stop == f"fox{grp}":
                    return

            def out_stores(branch):
                return [(branch_out[branch][h], t[:].bitcast(F32)) for h, t in enumerate((out_hi, out_lo))]

            with Scope("mem") as ms:
                q = ms.sb("q", [P, NT, BANK])
                k_tok = ms.sb("k_tok", [P, 2, BANK])
                v_hi = ms.sb("v_hi", [P, 2, BANK], F32R)
                v_lo = ms.sb("v_lo", [P, 2, BANK], F32R)
                with Scope("memtok") as mt:
                    mem_hi = mt.sb("mem_hi", [P, KD, M], F32R)
                    mem_lo = mt.sb("mem_lo", [P, KD, M], F32R)
                    memory = (mem_hi, mem_lo, 2)
                    project_block("memproj", [
                        {"rows": tokens, "width": BANK, "src": columns(w_in, C_QM, BANK), "norm": {"heads": MEM_H, "hd": MEM_D, "dst": q}},
                        {"rows": memory, "width": BANK, "src": columns(io["w_mem_kv"], 0, BANK),
                         "norm": {"heads": MEM_H, "hd": MEM_D, "dst": k_tok}},
                        {"rows": memory, "width": BANK, "src": columns(io["w_mem_kv"], BANK, BANK),
                         "value": {"view": lambda ps: ps, "hi": lambda t: v_hi[:, t, :], "lo": lambda t: v_lo[:, t, :]}}],
                        stores=out_stores(1), mem=(mem_hi, mem_lo))
                attention_block(Mem(q, k_tok, v_hi, v_lo, out_hi, out_lo), range(2 * KD, 2 * KD + 2))
            if stop == "mem":
                return

            with Scope("swa") as ss:
                q = ss.sb("q", [P, NT, BANK])
                k_tok = ss.sb("k_tok", [P, NT, SWA_KV * HD])
                values = ss.sb("values", [P, NT, SWA_KV, 2 * HD], F32R)
                kvw = SWA_KV * HD
                project_block("swaproj", [
                    {"rows": tokens, "width": BANK, "src": columns(w_in, C_QA, BANK), "norm": {"heads": SWA_H, "hd": HD, "dst": q}},
                    {"rows": tokens, "width": 2 * kvw, "src": columns(w_in, C_KA, 2 * kvw), "norm": {"heads": SWA_KV, "hd": HD, "dst": k_tok},
                     "value": {"view": lambda ps: ps[:, kvw:2 * kvw].rearrange("p (h d) -> p h d", d=HD),
                               "hi": lambda t: values[:, t, :, 0:HD], "lo": lambda t: values[:, t, :, HD:2 * HD]}}],
                    stores=out_stores(2))
                attention_block(Swa(q, k_tok, values, out_hi, out_lo), range(2 * KD + 2, 3 * KD))
            if stop == "swa":
                return
            merge_block(out_hi, out_lo)

        with ExitStack() as rest:
            x2 = tensor(rest, "x2", [P, NT, D])
            out_block(x2)
            if stop == "x2":
                return
            mlp_norm_block(x2)
            mlp_block(x2)
            with nc.Block(no_gpsimd_drain=True) as block:
                @block.sync
                def _(sp):
                    clear_retired(sp)


def kernel(**inputs):
    import concourse.bacc as bacc
    from concourse.bass_utils import run_bass_kernel_spmd

    nc = bacc.Bacc("TRN2", target_bir_lowering=False, num_devices=1)
    arrays = {name: np.ascontiguousarray(a) for name, a in inputs.items()}
    arrays["bucket_table"] = bucket_table()
    io = {name: nc.dram_tensor(f"in_{name}", a.shape, mybir.dt.from_np(a.dtype), kind="ExternalInput").ap()
          for name, a in arrays.items()}
    io["out"] = nc.dram_tensor("out", (1, S, D), F32, kind="ExternalOutput").ap()
    block_program(nc, io)
    done = run_bass_kernel_spmd(nc, [{f"in_{name}": a for name, a in arrays.items()}], core_ids=[0])
    return done.results[0]["out"]
```

```python
from contextlib import ExitStack

import numpy as np

import concourse.bass as bass
from concourse import mybir
from concourse.alu_op_type import AluOpType as ALU

ACT = mybir.ActivationFunctionType
AX = mybir.AxisListType
F32 = mybir.dt.float32
F32R = mybir.dt.float32r

P = 128
D = 1024
S = 1024
M = 256
KD = D // P
NT = S // P
BANK = 512
SWA_H, SWA_KV, HD = 8, 2, 64
FOX_H = 8
MEM_H, MEM_D = 4, 128
GROUP = 4
FF = 4 * D
WINDOW = 128
BUCKETS, MAX_DIST = 32, 128
EPS = 1e-6
NEG = -1e30
C_QA, C_KA, C_VA, C_QF, C_KF, C_VF, C_FL, C_QM, C_G = 0, 512, 640, 768, 1280, 1792, 2304, 2312, 2824
G_MIX, G_MEM, G_MLP, B_GATE, QN_A, KN_A, QN_F, KN_F, QN_M, KN_M, N_VEC = 0, 8, 16, 24, 48, 49, 50, 51, 52, 53, 54
DIAGS = 383


def bucket_table():
    table = np.zeros((BUCKETS + 1, DIAGS + 1), np.float32)
    exact = BUCKETS // 2
    for j in range(DIAGS):
        dist = 255 - j
        if 0 <= dist < WINDOW:
            if dist < exact:
                b = dist
            else:
                b = exact + int(np.float32(np.log(np.float32(dist / exact))) / np.float32(np.log(MAX_DIST / exact)) * (BUCKETS - exact))
            table[min(b, BUCKETS - 1), j] = 1.0
        else:
            table[BUCKETS, j] = NEG
    table[BUCKETS, DIAGS] = NEG
    return table


def block_program(nc, io):
    top = ExitStack()
    with top:
        def tensor(ctx, name, shape, dt=F32):
            return ctx.enter_context(nc.sbuf_tensor(name, shape, dt))

        class Scope:
            retired, cleared = [], []

            def __init__(self, name):
                self.name, self.ctx, self.sem_ctx, self.sems = name, ExitStack(), ExitStack(), []

            def __enter__(self):
                for _, context in Scope.cleared:
                    context.close()
                Scope.cleared = []
                self.ctx.__enter__()
                return self

            def sem(self, name):
                s = self.sem_ctx.enter_context(nc.semaphore(f"{self.name}_{name}"))
                self.sems.append(s)
                return s

            def sb(self, name, shape, dt=F32):
                return tensor(self.ctx, f"{self.name}_{name}", shape, dt)

            def __exit__(self, *e):
                Scope.retired.append((self.sems, self.sem_ctx))
                return self.ctx.__exit__(*e)

        def clear_retired(sp):
            for sems, _ in Scope.retired:
                for s in sems:
                    sp.sem_clear(s)
            Scope.cleared, Scope.retired = Scope.cleared + Scope.retired, []

        psum = top.enter_context(nc.psum_tensor("psum", [P, 8, BANK], F32))
        ident = tensor(top, "ident", [P, P])
        ident_r = tensor(top, "ident_r", [P, P], F32R)
        causal_r = tensor(top, "causal_r", [P, P], F32R)
        vecs = tensor(top, "vecs", [P, 64])
        sinks = tensor(top, "sinks", [P, SWA_H])
        b_forget = tensor(top, "b_forget", [P, FOX_H])
        minus_half = tensor(top, "minus_half", [P, 64])
        zeros = tensor(top, "zeros", [P, 1])
        act_hi = tensor(top, "act_hi", [P, KD, S], F32R)
        act_lo = tensor(top, "act_lo", [P, KD, S], F32R)
        c_query = nc.dram_tensor("c_query", [FOX_H, 4, S], F32).ap()
        c_key = nc.dram_tensor("c_key", [FOX_H, 4, S], F32).ap()
        diagonals = nc.dram_tensor("diagonals", [P, SWA_H, DIAGS + 1], F32).ap()

        gate_logits = nc.dram_tensor("gate_logits", [3 * KD, P, S], F32).ap()
        branch_out = {b: nc.dram_tensor(f"branch_out{b}", [4, P, S], F32).ap() for b in (1, 2)}

        class Weights:

            def __init__(self, sc, per, stages=4, slots=8, loads=None):
                loads = loads or [1] * per
                self.at = [16 * sum(loads[j % stages:j + 1:stages]) for j in range(per)]
                self.turn = [16 * sum(loads[s::stages]) for s in range(stages)]
                self.per, self.stages, self.slots = per, stages, slots
                self.stage = sc.sb("w_stage", [P, stages, BANK])
                self.hi = sc.sb("w_hi", [P, slots, BANK], F32R)
                self.lo = sc.sb("w_lo", [P, slots, BANK], F32R)
                self.landed = [sc.sem(f"w_landed{s}") for s in range(stages)]
                self.hi_done = sc.sem("w_hi_done")
                self.act_hi_done = sc.sem("w_act_hi_done")
                self.by_act = []
                self.split = sc.sem("w_split")
                self.used = sc.sem("w_used")
                self.asked = sc.sem("w_asked")

            def load(self, sp, i, j, *sources):
                sp.wait_ge(self.split, i * self.per + j + 1)
                if not isinstance(i, int):
                    sp.sem_inc(self.asked, 1)
                at = 0
                for src in sources:
                    width = src.shape[-1] * (src.shape[1] if len(src.shape) == 3 else 1)
                    dst = self.stage[:, j % self.stages, at:at + width]
                    if len(src.shape) == 3:
                        dst = dst.rearrange("p (a b) -> p a b", a=src.shape[1])
                    sp.dma_start(dst, src).then_inc(self.landed[j % self.stages], 16)
                    at += width

            def start_pool(self, pool):
                pool.sem_inc(self.split, self.stages)

            def start_pe(self, pe):
                pe.sem_inc(self.used, self.slots)

            def split_piece(self, pool, i, j, width=BANK):
                s, r = j % self.stages, j % self.slots
                pool.wait_ge(self.landed[s], i * self.turn[s] + self.at[j])
                if j in self.by_act:
                    pool.wait_ge(self.act_hi_done, self.by_act.index(j) + 1)
                    nc.gpsimd.tensor_tensor(self.lo[:, r, 0:width], self.stage[:, s, 0:width],
                                            self.hi[:, r, 0:width].bitcast(F32), ALU.subtract).then_inc(self.split, 1)
                    return
                pool.wait_ge(self.used, i * self.per + j + 1)
                nc.gpsimd.tensor_tensor(self.hi[:, r, 0:width], self.stage[:, s, 0:width], zeros[:].to_broadcast([P, width]),
                                        ALU.add).then_inc(self.hi_done, 1)
                pool.wait_ge(self.hi_done, i * self.per + j + 1 - sum(n < j for n in self.by_act))
                nc.gpsimd.tensor_tensor(self.lo[:, r, 0:width], self.stage[:, s, 0:width],
                                        self.hi[:, r, 0:width].bitcast(F32), ALU.subtract).then_inc(self.split, 1)

            def act_hi(self, act, j, width=BANK):
                act.wait_ge(self.landed[j % self.stages], self.at[j])
                act.wait_ge(self.used, j + 1)
                nc.scalar.activation(self.hi[:, j % self.slots, 0:width], self.stage[:, j % self.stages, 0:width],
                                     ACT.Copy).then_inc(self.act_hi_done, 1)

            def ready(self, pe, i, j):
                pe.wait_ge(self.split, i * self.per + j + 1 + self.stages)

        def three(out, a_hi, a_lo, b_hi, b_lo, first, last):
            nc.tensor.matmul(out, a_hi, b_hi, start=first, stop=False)
            nc.tensor.matmul(out, a_hi, b_lo, start=False, stop=False)
            return nc.tensor.matmul(out, a_lo, b_hi, start=False, stop=last)

        def norm_to_features(sc, raw, n_tiles, gain, dst_hi, dst_lo, raw_ready, spare=None):
            per = min(4, n_tiles)
            width = per * P
            normed = raw if spare is not None else sc.sb("normed", [P, n_tiles, D])
            ssq = sc.sb("row_ssq", [P, n_tiles])
            rstd = sc.sb("row_rstd", [P, n_tiles])
            squared, stat, scaled = sc.sem("row_squared"), sc.sem("row_stat"), sc.sem("row_scaled")
            turned, hi_done, lo_done = sc.sem("row_turned"), sc.sem("nt_hi"), sc.sem("nt_lo")
            groups = n_tiles // per

            def act_stats(act):
                for t in range(n_tiles):
                    raw_ready(act, t)
                    if spare is not None and t:
                        act.wait_ge(squared, t)
                    nc.scalar.activation(normed[:, t, :] if spare is None else spare, raw[:, t, :], ACT.Square,
                                         accum_out=ssq[:, t:t + 1]).then_inc(squared, 1)

            def pool(pool):
                for g in range(groups):
                    r = slice(g * per, (g + 1) * per)
                    pool.wait_ge(squared, (g + 1) * per)
                    nc.gpsimd.tensor_scalar(rstd[:, r], ssq[:, r], 1.0 / D, EPS, ALU.mult, ALU.add).then_inc(stat, 1)
                    pool.wait_ge(stat, 2 * g + 1)
                    nc.gpsimd.tensor_tensor(rstd[:, r], rstd[:, r], minus_half[:, r], ALU.pow).then_inc(stat, 1)

            def dve_scale(dve, g):
                dve.wait_ge(stat, 2 * g + 2)
                for t in range(g * per, (g + 1) * per):
                    raw_ready(dve, t)
                    nc.vector.tensor_scalar(normed[:, t, :], raw[:, t, :], rstd[:, t:t + 1], None,
                                            ALU.mult).then_inc(scaled, 1)

            def pe(pe, bank_free=lambda pe, n: None):
                for g in range(groups):
                    pe.wait_ge(scaled, (g + 1) * per)
                    for k in range(KD):
                        n = g * KD + k
                        bank_free(pe, n)
                        if n >= 8:
                            pe.wait_ge(lo_done, n - 7)
                        for t in range(per):
                            last = nc.tensor.transpose(psum[:, n % 8, t * P:(t + 1) * P],
                                                       normed[:, g * per + t, k * P:(k + 1) * P], ident[:])
                        last.then_inc(turned, 1)

            def act_hi_half(act):
                for g in range(groups):
                    for k in range(KD):
                        n = g * KD + k
                        act.wait_ge(turned, n + 1)
                        nc.scalar.activation(dst_hi[:, k, g * width:(g + 1) * width], psum[:, n % 8, 0:width], ACT.Copy,
                                             scale=vecs[:, gain + k:gain + k + 1]).then_inc(hi_done, 1)

            def dve(dve, scale=True):
                for g in range(groups):
                    if scale:
                        dve_scale(dve, g)
                    for k in range(KD):
                        n = g * KD + k
                        cols = slice(g * width, (g + 1) * width)
                        dve.wait_ge(hi_done, n + 1)
                        nc.vector.scalar_tensor_tensor(
                            out=dst_lo[:, k, cols], in0=psum[:, n % 8, 0:width], scalar=vecs[:, gain + k:gain + k + 1],
                            in1=dst_hi[:, k, cols].bitcast(F32), op0=ALU.mult, op1=ALU.subtract).then_inc(lo_done, 1)

            return act_stats, pool, pe, act_hi_half, dve, dve_scale, lo_done

        def setup_block():
            with Scope("setup") as sc:
                rows = sc.sb("rows", [64, P])
                rel = sc.sb("rel", [BUCKETS + 1, SWA_H])
                hot = sc.sb("hot", [BUCKETS + 1, DIAGS + 1])
                hot_r = sc.sb("hot_r", [BUCKETS + 1, DIAGS + 1], F32R)
                rel_wide = [sc.sb(f"rel_wide_{h}", [BUCKETS + 1, SWA_H, P], F32R) for h in ("hi", "lo")]
                diag = sc.sb("diag", [P, SWA_H, DIAGS + 1])
                causal = sc.sb("causal", [P, P])
                x_raw = sc.sb("x_raw", [P, NT, D])
                x_landed = [sc.sem(f"x_landed{t}") for t in range(NT)]
                small = sc.sem("small_landed")
                made, ident_ready, causal_ready, rel_made, rel_ready, diag_copied, vec_t, diag_t, copied, stored = (sc.sem(n) for n in (
                    "made", "ident_ready", "causal_ready", "rel_made", "rel_ready", "diag_copied", "vec_turned", "diag_made", "copied", "diag_stored"))
                act_stats, pool_stats, pe_turn, act_hi_half, dve_part, _, _ = norm_to_features(
                    sc, x_raw, NT, G_MIX, act_hi, act_lo, lambda e, t: e.wait_ge(x_landed[t], 16))

                with nc.Block() as block:
                    @block.sync
                    def _(sp):
                        for at, name, n in ((G_MIX, "g_mix", 8), (G_MEM, "g_mem", 8), (G_MLP, "g_mlp", 8), (B_GATE, "b_gate", 24)):
                            sp.dma_start(rows[at:at + n, :], io[name].rearrange("a (r c) -> (a r) c", c=P)).then_inc(small, 16)
                        for at, name in ((QN_A, "qn_swa"), (KN_A, "kn_swa"), (QN_F, "qn_fox"), (KN_F, "kn_fox")):
                            for half in range(2):
                                sp.dma_start(rows[at:at + 1, half * HD:(half + 1) * HD], io[name]).then_inc(small, 16)
                        sp.dma_start(rows[QN_M:QN_M + 1, :], io["qn_mem"]).then_inc(small, 16)
                        sp.dma_start(rows[KN_M:KN_M + 1, :], io["kn_mem"]).then_inc(small, 16)
                        sp.dma_start(sinks[:], bass.AP(io["sink_swa"].tensor, 0, [[0, P], [1, SWA_H]])).then_inc(small, 16)
                        sp.dma_start(b_forget[:], bass.AP(io["b_forget"].tensor, 0, [[0, P], [1, FOX_H]])).then_inc(small, 16)
                        sp.dma_start(hot[:], io["bucket_table"]).then_inc(small, 16)
                        sp.dma_start(rel[0:BUCKETS, :], io["rel_bias"]).then_inc(small, 16)
                        for t in range(NT):
                            sp.dma_start(x_raw[:, t, :], io["x"][0, t * P:(t + 1) * P, :]).then_inc(x_landed[t], 16)
                        sp.wait_ge(diag_copied, SWA_H)
                        sp.dma_start(diagonals, diag[:]).then_inc(stored, 16)
                        sp.wait_ge(stored, 16)
                        clear_retired(sp)

                    @block.gpsimd
                    def _(pool):
                        nc.gpsimd.memset(ident[:], 0.0).then_inc(made, 1)
                        nc.gpsimd.memset(causal[:], 0.0).then_inc(made, 1)
                        nc.gpsimd.memset(minus_half[:], -0.5).then_inc(made, 1)
                        nc.gpsimd.memset(zeros[:], 0.0).then_inc(made, 1)
                        pool.wait_ge(made, 4)
                        nc.gpsimd.affine_select(out=ident[:], in_=ident[:], compare_op=ALU.not_equal, fill=1.0, base=0,
                                                pattern=[[-1, P]], channel_multiplier=1).then_inc(ident_ready, 1)
                        nc.gpsimd.affine_select(out=causal[:], in_=causal[:], compare_op=ALU.is_ge, fill=NEG, base=0,
                                                pattern=[[-1, P]], channel_multiplier=1).then_inc(causal_ready, 1)
                        pool_stats(pool)

                    @block.scalar
                    def _(act):
                        act_stats(act)
                        act_hi_half(act)

                    @block.tensor
                    def _(pe):
                        pe.wait_ge(ident_ready, 1)
                        pe.wait_ge(small, 18 * 16)
                        nc.tensor.transpose(psum[:, 0, 0:N_VEC], rows[0:N_VEC, :], ident[0:N_VEC, 0:N_VEC]).then_inc(vec_t, 1)
                        pe.wait_ge(rel_ready, 3)
                        for h in range(SWA_H):
                            if h >= 7:
                                pe.wait_ge(diag_copied, h - 6)
                            out = psum[:, 1 + h % 7, 0:DIAGS + 1]
                            nc.tensor.matmul(out, rel_wide[0][:, h, :], hot_r[:], start=True, stop=False)
                            nc.tensor.matmul(out, rel_wide[1][:, h, :], hot_r[:], start=False, stop=True).then_inc(diag_t, 1)
                        pe.wait_ge(diag_copied, SWA_H)
                        pe.wait_ge(copied, 1)
                        pe_turn(pe)

                    @block.vector
                    def _(dve):
                        nc.vector.memset(rel[BUCKETS:BUCKETS + 1, :], 1.0).then_inc(rel_made, 1)
                        dve.wait_ge(rel_made, 1)
                        dve.wait_ge(small, 18 * 16)
                        wide = rel[:].unsqueeze(2).to_broadcast([BUCKETS + 1, SWA_H, P])
                        nc.vector.tensor_copy(rel_wide[0][:], wide).then_inc(rel_ready, 1)
                        nc.vector.tensor_copy(hot_r[:], hot[:]).then_inc(rel_ready, 1)
                        dve.wait_ge(rel_ready, 1)
                        nc.vector.tensor_tensor(rel_wide[1][:], wide, rel_wide[0][:].bitcast(F32), ALU.subtract).then_inc(rel_ready, 1)
                        dve.wait_ge(vec_t, 1)
                        nc.vector.tensor_copy(vecs[:, 0:N_VEC], psum[:, 0, 0:N_VEC]).then_inc(copied, 1)
                        for h in range(SWA_H):
                            dve.wait_ge(diag_t, h + 1)
                            nc.vector.tensor_copy(diag[:, h, :], psum[:, 1 + h % 7, 0:DIAGS + 1]).then_inc(diag_copied, 1)
                        dve.wait_ge(ident_ready, 1)
                        dve.wait_ge(causal_ready, 1)
                        nc.vector.tensor_copy(ident_r[:], ident[:]).then_inc(copied, 1)
                        nc.vector.tensor_copy(causal_r[:], causal[:]).then_inc(copied, 1)
                        dve.wait_ge(copied, 1)
                        for at in (QN_A, QN_F):
                            nc.vector.tensor_scalar(vecs[:, at:at + 1], vecs[:, at:at + 1], HD ** -0.5, None,
                                                    ALU.mult).then_inc(copied, 1)
                        dve_part(dve)

        class Chain:

            def __init__(self, eng, sem):
                self.eng, self.sem, self.n = eng, sem, 0

            def count(self, instruction):
                self.n += 1
                instruction.then_inc(self.sem, 1)

            def wait(self):
                self.eng.wait_ge(self.sem, self.n)

            def __call__(self, instruction):
                self.count(instruction)
                self.wait()

        def project_block(name, chunks, store=None, mem=None):
            n_pieces = KD * len(chunks)
            with Scope(name) as sc:
                w = Weights(sc, n_pieces, loads=[len(c["src"](0)) for c in chunks for _ in range(KD)])
                tiles = [chunk["rows"][2] for chunk in chunks]
                start = [sum(tiles[:c]) for c in range(len(chunks))]
                full = [sum(t - 1 for t in tiles[:c]) for c in range(len(chunks))]
                w.by_act = [c * KD + k for c in range(len(chunks)) for k in range(KD) if tiles[c] < 4 or c + k == 0]
                squares = sc.sb("squares", [P, 2, BANK])
                filled, raw_done, squared, v_hi_done, freed_value = (sc.sem(n) for n in (
                    "filled", "raw_done", "squared", "v_hi_done", "freed_value"))
                reduced, stat_scaled, stat, logits_done, scaled = (sc.sem(n) for n in (
                    "reduced", "stat_scaled", "stat", "logits_done", "scaled"))
                summed, stored = sc.sem("summed"), [sc.sem(f"stored{slot}") for slot in range(2)]
                whole = sc.sb("whole", [P, 2, S]) if store else None
                total = [(c, t) for c in range(len(chunks)) for t in range(tiles[c])]
                order = {kind: [q for q, (c, _) in enumerate(total) if kind in chunks[c]] for kind in ("norm", "value")}
                norms = [c for c in range(len(chunks)) if "norm" in chunks[c]]
                norm_at = [sum(tiles[d] for d in norms if d < c) for c in range(len(chunks))]
                ssq = sc.sb("ssq", [P, max(len(norms), 1), 64])

                def stat_part(c, tile):
                    return sum((tiles[d] + 3) // 4 for d in norms if d < c) + tile // 4

                if mem:
                    raw = sc.sb("raw", [P, 2, D])
                    mem_landed = [sc.sem(f"mem_landed{t}") for t in range(2)]
                    mem_stats, mem_pool, mem_turn, mem_hi, mem_lo, mem_scale, mem_done = norm_to_features(
                        sc, raw, 2, G_MEM, mem[0], mem[1], lambda e, t: e.wait_ge(mem_landed[t], 16), spare=squares[:].rearrange("p a b -> p (a b)"))

                with nc.Block(no_gpsimd_drain=True) as block:
                    @block.sync
                    def _(sp):
                        for c, chunk in enumerate(chunks):
                            for k in range(KD):
                                w.load(sp, 0, c * KD + k, *chunk["src"](k))
                                for t in range(2 if mem and c == 0 and k == 3 else 0):
                                    sp.dma_start(raw[:, t, :], io["mem"][0, t * P:(t + 1) * P, :]).then_inc(mem_landed[t], 16)
                            for kt in range(4 if store and c == 0 else 0):
                                sp.wait_ge(summed, kt + 1)
                                sp.dma_start(store[0][kt], whole[:, kt % 2, :]).then_inc(stored[kt % 2], 16)
                        if store:
                            for slot in range(2):
                                sp.wait_ge(stored[slot], 16 * 2)
                        clear_retired(sp)

                    @block.gpsimd
                    def _(pool):
                        w.start_pool(pool)

                        def stats(c):
                            n, part = norms.index(c), chunks[c]["norm"]
                            for first in range(0, tiles[c], 4):
                                last = min(first + 4, tiles[c])
                                r = slice(first * part["heads"], last * part["heads"])
                                pool.wait_ge(reduced, norm_at[c] + last)
                                nc.gpsimd.tensor_scalar(ssq[:, n, r], ssq[:, n, r], 1.0 / part["hd"], EPS,
                                                        ALU.mult, ALU.add).then_inc(stat_scaled, 1)
                                pool.wait_ge(stat_scaled, stat_part(c, first) + 1)
                                nc.gpsimd.tensor_tensor(ssq[:, n, r], ssq[:, n, r], minus_half[:, r], ALU.pow).then_inc(stat, 1)

                        for c, chunk in enumerate(chunks):
                            for k in range(KD):
                                w.split_piece(pool, 0, c * KD + k, chunk["width"])
                            if c == 0 and mem:
                                mem_pool(pool)
                            if c - 1 in norms:
                                stats(c - 1)
                        if len(chunks) - 1 in norms:
                            stats(len(chunks) - 1)

                    @block.tensor
                    def _(pe):
                        w.start_pe(pe)
                        for c, chunk in enumerate(chunks):
                            for k in range(KD):
                                w.ready(pe, 0, c * KD + k)
                                for t in range(tiles[c]):
                                    q = start[c] + t
                                    if k == 0 and c == 1 and mem and t == 0:
                                        pe.wait_ge(mem_done, KD)
                                    if k == 0 and q >= 8:
                                        if "value" in chunks[total[q - 8][0]]:
                                            pe.wait_ge(freed_value, order["value"].index(q - 8) + 1)
                                        else:
                                            pe.wait_ge(raw_done, order["norm"].index(q - 8) + 1)
                                    rows = slice(t * P, (t + 1) * P)
                                    r = (c * KD + k) % w.slots
                                    wd = chunk["width"]
                                    src_hi, src_lo, _ = chunk["rows"]
                                    last = three(psum[:, q % 8, 0:wd], src_hi[:, k, rows], src_lo[:, k, rows],
                                                 w.hi[:, r, 0:wd], w.lo[:, r, 0:wd], k == 0, k == KD - 1)
                                    if k == KD - 1 and t < tiles[c] - 1:
                                        last.then_inc(filled, 1)
                                last.then_inc(w.used, 1)
                            if mem and c == 0:
                                mem_turn(pe, lambda pe, n: pe.wait_ge(raw_done, n + 1))

                    @block.scalar
                    def _(act):

                        def split(c):
                            for k in range(KD):
                                if c < len(chunks) and c * KD + k in w.by_act:
                                    w.act_hi(act, c * KD + k, chunks[c]["width"])

                        def square(c, t):
                            if "norm" in chunks[c]:
                                part, n = chunks[c]["norm"], norm_at[c] + t
                                act.wait_ge(raw_done, n + 1)
                                if n >= 2:
                                    act.wait_ge(reduced, n - 1)
                                nc.scalar.activation(squares[:, n % 2, 0:part["heads"] * part["hd"]], part["dst"][:, t, :],
                                                     ACT.Square).then_inc(squared, 1)

                        split(0)
                        if mem:
                            mem_stats(act)
                        split(1)
                        for c, chunk in enumerate(chunks):
                            for t in range(tiles[c]):
                                q = start[c] + t
                                if t < tiles[c] - 1:
                                    act.wait_ge(filled, full[c] + t + 1)
                                else:
                                    act.wait_ge(w.used, w.slots + (c + 1) * KD)
                                if "value" in chunk:
                                    part = chunk["value"]
                                    nc.scalar.activation(part["hi"](t), part["view"](psum[:, q % 8, :]), ACT.Copy).then_inc(v_hi_done, 1)
                                if "norm" in chunk:
                                    part = chunk["norm"]
                                    nc.scalar.activation(part["dst"][:, t, :], psum[:, q % 8, 0:part["heads"] * part["hd"]],
                                                         ACT.Copy).then_inc(raw_done, 1)
                                if c == len(chunks) - 1:
                                    square(c, t)
                            if mem and c == 0:
                                mem_hi(act)
                            for t in range(tiles[c] if c < len(chunks) - 1 else 0):
                                square(c, t)
                            split(c + 2)

                    @block.vector
                    def _(dve):
                        for kt in range(4 if store else 0):
                            hi, lo = (t[:, kt, :].bitcast(F32) for t in store[1:])
                            if kt >= 2:
                                dve.wait_ge(stored[kt % 2], 16 * (kt // 2))
                            nc.vector.tensor_tensor(whole[:, kt % 2, :], lo, hi, ALU.add).then_inc(summed, 1)
                        if mem:
                            mem_scale(dve, 0)
                        def lo_half(c, t):
                            if "value" in chunks[c]:
                                part, q = chunks[c]["value"], start[c] + t
                                dve.wait_ge(v_hi_done, order["value"].index(q) + 1)
                                if "norm" in chunks[c]:
                                    dve.wait_ge(raw_done, order["norm"].index(q) + 1)
                                if "logits" in part:
                                    nc.vector.tensor_tensor(part["logits"](t), psum[:, q % 8, chunks[c]["width"] - FOX_H:chunks[c]["width"]],
                                                            b_forget[:], ALU.add).then_inc(logits_done, 1)
                                nc.vector.tensor_tensor(part["lo"](t), part["view"](psum[:, q % 8, :]),
                                                        part["hi"](t).bitcast(F32), ALU.subtract).then_inc(freed_value, 1)

                        def reduce(c, t):
                            if "norm" in chunks[c]:
                                part, n, m = chunks[c]["norm"], norms.index(c), norm_at[c] + t
                                heads, hd = part["heads"], part["hd"]
                                dve.wait_ge(squared, m + 1)
                                nc.vector.tensor_reduce(
                                    ssq[:, n, t * heads:(t + 1) * heads],
                                    squares[:, m % 2, 0:heads * hd].rearrange("p (h d) -> p h d", h=heads),
                                    AX.X, ALU.add).then_inc(reduced, 1)

                        def scale(c, t):
                            part, n = chunks[c]["norm"], norms.index(c)
                            heads, hd = part["heads"], part["hd"]
                            if t % 4 == 0:
                                dve.wait_ge(stat, stat_part(c, t) + 1)
                            tok = part["dst"][:, t, :].rearrange("p (h d) -> p h d", h=heads)
                            r = ssq[:, n, t * heads:(t + 1) * heads]
                            nc.vector.tensor_tensor(
                                tok, tok, r.unsqueeze(2).to_broadcast([P, heads, hd]), ALU.mult).then_inc(scaled, 1)

                        for c, chunk in enumerate(chunks):
                            if c == len(chunks) - 1:
                                for t in range(tiles[c]):
                                    lo_half(c, t)
                                    reduce(c, t)
                            else:
                                for t in range(tiles[c]):
                                    lo_half(c, t)
                                if mem and c == 0:
                                    mem_lo(dve, scale=False)
                                for t in range(tiles[c]):
                                    reduce(c, t)
                            if "norm" in chunk:
                                for t in range(tiles[c]):
                                    scale(c, t)

        def decay_block(logits):
            with Scope("decay") as sc:
                n = NT * FOX_H
                names = ("neg", "mag", "e", "u", "d", "ln", "is0", "num", "den", "l1p", "logf")
                t = {k: sc.sb(k, [P, n]) for k in names}
                upto = sc.sb("upto", [P, BANK])
                ones = sc.sb("ones", [P, BANK])
                upto_r = sc.sb("upto_r", [P, BANK], F32R)
                ones_r = sc.sb("ones_r", [P, BANK], F32R)
                logf = [sc.sb(f"logf_{h}", [P, n], F32R) for h in ("hi", "lo")]
                cq = sc.sb("cq", [FOX_H, 4, S], F32R)
                ck = sc.sb("ck", [FOX_H, 4, S], F32R)
                own, e_done, u_done, ln_done, logf_done, made, upto_done, ones_done, summed, c_act, rows_done, stored = (sc.sem(k) for k in (
                    "own", "e_done", "u_done", "ln_done", "logf_done", "made", "upto_done", "ones_done", "summed", "c_act", "rows_done", "stored"))
                with nc.Block(no_gpsimd_drain=True) as block:
                    @block.gpsimd
                    def _(pool):
                        nc.gpsimd.memset(ones[:], 1.0).then_inc(made, 1)
                        pool.wait_ge(made, 1)
                        nc.gpsimd.affine_select(out=upto[:], in_=ones[:], compare_op=ALU.is_ge, fill=0.0, base=0,
                                                pattern=[[1, BANK]], channel_multiplier=-1).then_inc(upto_done, 1)
                        nc.gpsimd.memset(cq[:, 2:4, :].bitcast(F32), 1.0).then_inc(ones_done, 1)
                        nc.gpsimd.memset(ck[:, 0:2, :].bitcast(F32), 1.0).then_inc(ones_done, 1)

                    @block.vector
                    def _(dve):
                        done = Chain(dve, own)
                        ts, tt = nc.vector.tensor_scalar, nc.vector.tensor_tensor
                        done(ts(t["neg"][:], logits, -1.0, None, ALU.mult))
                        tt(t["mag"][:], t["neg"][:], logits, ALU.max).then_inc(e_done, 1)
                        dve.wait_ge(upto_done, 1)
                        nc.vector.tensor_copy(upto_r[:], upto[:]).then_inc(upto_done, 1)
                        nc.vector.tensor_copy(ones_r[:], ones[:]).then_inc(upto_done, 1)
                        dve.wait_ge(e_done, 2)
                        ts(t["u"][:], t["e"][:], 1.0, None, ALU.add).then_inc(u_done, 1)
                        dve.wait_ge(u_done, 1)
                        done(ts(t["d"][:], t["u"][:], -1.0, None, ALU.add))
                        done(ts(t["is0"][:], t["d"][:], 0.0, None, ALU.is_equal))
                        done(tt(t["den"][:], t["d"][:], t["is0"][:], ALU.add))
                        done(nc.vector.reciprocal(t["den"][:], t["den"][:]))
                        dve.wait_ge(ln_done, 1)
                        done(tt(t["num"][:], t["ln"][:], t["is0"][:], ALU.add))
                        done(tt(t["num"][:], t["num"][:], t["e"][:], ALU.mult))
                        done(tt(t["l1p"][:], t["num"][:], t["den"][:], ALU.mult))
                        done(ts(t["neg"][:], logits, 0.0, None, ALU.min))
                        done(tt(t["logf"][:], t["neg"][:], t["l1p"][:], ALU.subtract))
                        done(nc.vector.tensor_copy(logf[0][:], t["logf"][:]))
                        tt(logf[1][:], t["logf"][:], logf[0][:].bitcast(F32), ALU.subtract).then_inc(logf_done, 1)
                        for half in range(2):
                            cols = slice(half * BANK, (half + 1) * BANK)
                            dve.wait_ge(c_act, half + 1)
                            tt(cq[:, 1, cols], psum[0:FOX_H, half, :], cq[:, 0, cols].bitcast(F32), ALU.subtract).then_inc(rows_done, 1)
                            dve.wait_ge(rows_done, 1 + 3 * half)
                            ts(ck[:, 3, cols], cq[:, 1, cols].bitcast(F32), -1.0, None, ALU.mult).then_inc(rows_done, 1)
                            ts(ck[:, 2, cols], cq[:, 0, cols].bitcast(F32), -1.0, None, ALU.mult).then_inc(rows_done, 1)

                    @block.scalar
                    def _(act):
                        act.wait_ge(e_done, 1)
                        nc.scalar.activation(t["e"][:], t["mag"][:], ACT.Exp, scale=-1.0).then_inc(e_done, 1)
                        act.wait_ge(u_done, 1)
                        nc.scalar.activation(t["ln"][:], t["u"][:], ACT.Ln).then_inc(ln_done, 1)
                        for half in range(2):
                            act.wait_ge(summed, half + 1)
                            nc.scalar.activation(cq[:, 0, half * BANK:(half + 1) * BANK], psum[0:FOX_H, half, :],
                                                 ACT.Copy).then_inc(c_act, 1)

                    @block.tensor
                    def _(pe):
                        pe.wait_ge(logf_done, 1)
                        pe.wait_ge(upto_done, 3)
                        parts = [h[:].rearrange("p (t h) -> p t h", h=FOX_H) for h in logf]
                        for half in range(2):
                            if half:
                                for j in range(4):
                                    for part in parts:
                                        nc.tensor.matmul(psum[0:FOX_H, 1, :], part[:, j, :], ones_r[:],
                                                         start=j == 0 and part is parts[0], stop=False)
                            for j in range(4):
                                for part in parts:
                                    last = nc.tensor.matmul(psum[0:FOX_H, half, j * P:BANK], part[:, 4 * half + j, :],
                                                            upto_r[:, 0:BANK - j * P], start=half == 0 and j == 0 and part is parts[0],
                                                            stop=j == 3 and part is parts[1])
                            last.then_inc(summed, 1)

                    @block.sync
                    def _(sp):
                        sp.wait_ge(rows_done, 6)
                        sp.wait_ge(ones_done, 2)
                        sp.dma_start(c_query, cq[:].bitcast(F32)).then_inc(stored, 16)
                        sp.dma_start(c_key, ck[:].bitcast(F32)).then_inc(stored, 16)
                        sp.wait_ge(stored, 32)
                        clear_retired(sp)

        SCORE, TURN, OUT, GATE = 0, 4, 6, 7

        def pair(slot, width):
            return psum[:, SCORE + 2 * slot:SCORE + 2 * slot + 2, :].rearrange("p b c -> p (b c)")[:, 0:width]

        class GateLogits:

            def __init__(self, sc, tiles):
                self.tiles = tiles
                self.w = Weights(sc, 2 * len(tiles), stages=2, slots=2)
                self.out = sc.sb("logits_out", [P, BANK])
                self.product, self.copied, self.stored = (sc.sem(k) for k in ("logits_product", "logits_copied", "logits_stored"))
                self.w_gate = io["w_in"][0].rearrange("(k p) n -> p k n", p=P)
                self.unstored = None

            def load(self, sp, n):
                col = C_G + self.tiles[n // 2] * P
                self.w.load(sp, 0, n, self.w_gate[:, 4 * (n % 2):4 * (n % 2) + 4, col:col + P])

            def pe_unit(self, pe, u):
                w, tile, tokens, h = self.w, u // 4, (u // 2) % 2, u % 2
                cols = slice(tokens * BANK, (tokens + 1) * BANK)
                if tokens == 0:
                    w.ready(pe, 0, 2 * tile + h)
                if h == 0 and u:
                    pe.wait_ge(self.copied, u // 2)
                for kk in range(4):
                    wc = slice(kk * P, (kk + 1) * P)
                    last = three(psum[:, GATE, :], w.hi[:, h, wc], w.lo[:, h, wc], act_hi[:, 4 * h + kk, cols],
                                 act_lo[:, 4 * h + kk, cols], h == 0 and kk == 0, h == 1 and kk == 3)
                if tokens == 1:
                    last.then_inc(w.used, 1)
                elif h == 1:
                    last.then_inc(self.product, 1)

            def act_copy(self, act, u):
                tile, tokens = u // 4, (u // 2) % 2
                self.act_store(act)
                if tokens == 0:
                    act.wait_ge(self.product, tile + 1)
                else:
                    act.wait_ge(self.w.used, self.w.slots + 2 * tile + 2)
                if u > 1:
                    act.wait_ge(self.stored, 16 * (u // 2))
                nc.scalar.activation(self.out[:], psum[:, GATE, :], ACT.Copy).then_inc(self.copied, 1)
                self.unstored = u

            def act_store(self, act):
                if self.unstored is not None:
                    u, self.unstored = self.unstored, None
                    tile, tokens = u // 4, (u // 2) % 2
                    act.wait_ge(self.copied, u // 2 + 1)
                    act.dma_start(gate_logits[self.tiles[tile], :, tokens * BANK:(tokens + 1) * BANK], self.out[:]).then_inc(self.stored, 16)

        def attention_block(plan, gate_tiles):
            with Scope(plan.name) as sc:
                n = plan.steps
                probs = sc.sb("probs", [P, plan.prob_slots, D])
                ps, plan.probs = plan.prob_slots, probs
                scored, maxed, exped, normed, turned, hi_done, lo_done, valued, own = (sc.sem(k) for k in (
                    "scored", "maxed", "exped", "normed", "turned", "hi_done", "lo_done", "valued", "dve_own"))
                out_done = [sc.sem(f"out{k}") for k in range(len(plan.out_stages))]
                plan.allocate(sc)
                gates = GateLogits(sc, gate_tiles)
                items, turn_end, prepared, n_units = [], [], {}, 0
                step_items = {}
                ends = [s for s in range(n) if plan.ends_unit(s)]
                for s in range(-1, n + 3):
                    here = [("turn", s - 2, g) for g in plan.turns(s - 2)] if 2 <= s < n + 2 else []
                    for job in (plan.preps(s) if s < n else ()):
                        prepared[job] = len(items) + len(here) + 1
                        here.append(("prep", job))
                    units = list(range(n_units, n_units + plan.gate_units(s)))
                    n_units += len(units)
                    work = []
                    for j, item in enumerate(here):
                        work.append((len(items) + j, item))
                        if j % 2 == 1 and units:
                            work.append((units.pop(0), ("unit",)))
                    work += [(u, ("unit",)) for u in units]
                    if s - 3 in ends:
                        work.insert(min(2, len(work)), (ends.index(s - 3), ("values",)))
                    step_items[s] = work
                    items += here
                    if 2 <= s < n + 2:
                        turn_end.append(len(items) - sum(kind == "prep" for kind, *_ in here))
                assert n_units == 4 * len(gate_tiles)
                unit = [sum(e < s for e in ends) for s in range(n)]

                def out_part(eng, who, s):
                    for k, (engine, fn) in reversed(list(enumerate(plan.out_stages))):
                        ended = s - 3 - k // 2
                        if engine == who and ended in ends:
                            u = ends.index(ended)
                            eng.wait_ge(out_done[k - 1] if k else valued, u + 1)
                            if k == 1 and len(out_done) == 4 and u >= plan.slots:
                                eng.wait_ge(out_done[3], u - plan.slots + 1)
                            fn(u).then_inc(out_done[k], 1)

                with nc.Block(no_gpsimd_drain=True) as block:
                    @block.tensor
                    def _(pe):
                        gates.w.start_pe(pe)

                        def transposes(s):
                            for q, (kind, *arg) in step_items[s]:
                                if kind == "unit":
                                    gates.pe_unit(pe, q)
                                    continue
                                if kind == "values":
                                    pe.wait_ge(lo_done, turn_end[s - 3])
                                    if q:
                                        pe.wait_ge(out_done[plan.out_freed], q)
                                    plan.values(q).then_inc(valued, 1)
                                    continue
                                at, *group = arg
                                if q >= 2:
                                    pe.wait_ge(lo_done, q - 1)
                                if kind == "turn":
                                    pe.wait_ge(normed, at + 1)
                                    for src, dst in group[0][0]:
                                        last = nc.tensor.transpose(psum[:, TURN + q % 2, dst:dst + P],
                                                                   probs[:, at % ps, src:src + P], ident[:])
                                else:
                                    last = plan.prep_pe(at, TURN + q % 2)
                                last.then_inc(turned, 1)

                        transposes(-1)
                        for s in range(n + 3):
                            if s < n:
                                if needed := plan.needs(s):
                                    pe.wait_ge(lo_done, prepared[needed])
                                plan.pe_inputs(pe, s)
                                if s >= 2:
                                    pe.wait_ge(exped, s - 1)
                                plan.scores(s).then_inc(scored, 1)
                            transposes(s)

                    @block.vector
                    def _(dve):
                        done = Chain(dve, own)

                        def lo_halves(s, part=slice(None)):
                            for q, (kind, *arg) in [item for item in step_items[s] if item[1][0] in ("turn", "prep")][part]:
                                at, *group = arg
                                dve.wait_ge(hi_done, q + 1)
                                if kind == "turn":
                                    moves, hi, lo = group[0]
                                    if unit[at] >= plan.lo_slots:
                                        dve.wait_ge(valued, unit[at] - plan.lo_slots + 1)
                                    src = psum[:, TURN + q % 2, 0:len(moves) * P]
                                    last = nc.vector.tensor_tensor(lo, src if len(lo.shape) == 2 else src.rearrange(
                                        "p (a b) -> p a b", b=P), hi.bitcast(F32), ALU.subtract)
                                else:
                                    last = plan.prep_dve(at, TURN + q % 2)
                                last.then_inc(lo_done, 1)

                        first, rest = slice(0, 2), slice(2, None)
                        lo_halves(-1)
                        plan.dve_before(dve)
                        for s in range(n + 4):
                            if s < n:
                                dve.wait_ge(scored, s + 1)
                                if plan.max_writes_probs and s >= ps:
                                    dve.wait_ge(turned, turn_end[s - ps])
                                plan.row_max(done, s).then_inc(maxed, 1)
                            if s < n + 2:
                                lo_halves(s, first)
                            if 0 <= s - 1 < n:
                                dve.wait_ge(exped, s)
                                plan.normalize(done, s - 1, probs[:, (s - 1) % ps, :]).then_inc(normed, 1)
                            out_part(dve, "dve", s)
                            if s < n + 2:
                                lo_halves(s, rest)

                    @block.scalar
                    def _(act):
                        def hi_halves(s, part=slice(None)):
                            for q, (kind, *arg) in [item for item in step_items[s] if item[1][0] != "values"][part]:
                                if kind == "unit":
                                    if q % 2:
                                        gates.act_copy(act, q)
                                    continue
                                at, *group = arg
                                act.wait_ge(turned, q + 1)
                                if kind == "turn":
                                    moves, hi, _ = group[0]
                                    if unit[at] >= plan.pt_slots:
                                        act.wait_ge(valued, unit[at] - plan.pt_slots + 1)
                                    src = psum[:, TURN + q % 2, 0:len(moves) * P]
                                    last = nc.scalar.activation(hi, src if len(hi.shape) == 2 else src.rearrange(
                                        "p (a b) -> p a b", b=P), ACT.Copy)
                                else:
                                    last = plan.prep_act(at, TURN + q % 2)
                                last.then_inc(hi_done, 1)

                        hi_halves(-1)
                        first, rest = slice(0, 2), slice(2, None)
                        for s in range(n + 4):
                            if s < n + 2:
                                hi_halves(s, first)
                            if s < n:
                                act.wait_ge(maxed, s + 1)
                                if s >= ps:
                                    act.wait_ge(turned, turn_end[s - ps])
                                plan.exps(s, probs[:, s % ps, :]).then_inc(exped, 1)
                            gates.act_store(act)
                            out_part(act, "act", s)
                            if s < n + 2:
                                hi_halves(s, rest)
                        gates.act_store(act)
                        act.wait_ge(gates.stored, 16 * 2 * len(gate_tiles))

                    @block.gpsimd
                    def _(pool):
                        gates.w.start_pool(pool)
                        for piece in range(2 * len(gate_tiles)):
                            gates.w.split_piece(pool, 0, piece)

                    @block.sync
                    def _(sp):
                        for piece in range(2 * len(gate_tiles)):
                            plan.sync(sp, piece)
                            gates.load(sp, piece)
                        clear_retired(sp)

        class HalfHeads:
            out_stages = ()
            out_freed = 1

            def allocate_out(self, sc, width, slots):
                self.slots = slots
                self.part = sc.sb("part", [P, slots, width])
                self.total = sc.sb("total", [P, slots, width])

            @staticmethod
            def value_product(out, values_tile, p_hi, p_lo, start, stop):
                if not start:
                    nc.tensor.matmul(out[0:HD], values_tile[:, 0:HD], p_lo, start=False, stop=False)
                last = nc.tensor.matmul(out, values_tile, p_hi, start=start, stop=stop and not start)
                if start and not stop:
                    last = nc.tensor.matmul(out[0:HD], values_tile[:, 0:HD], p_lo, start=False, stop=False)
                if start and stop:
                    last = nc.tensor.matmul(out, values_tile, p_lo, start=False, stop=True)
                return last

        class Fox(HalfHeads):
            steps = GROUP * NT
            pt_slots, lo_slots, prob_slots = 1, 1, 2
            max_writes_probs = False
            JOBS = (1, 2, 4, 6)
            AUG = HD + 4
            UNIT = 2 * P

            def __init__(self, grp, qk, values, out_hi, out_lo):
                self.name, self.grp, self.qk, self.v, self.out_hi, self.out_lo = f"foxattn{grp}", grp, qk, values, out_hi, out_lo
                self.out_stages = (("act", self.out_part), ("dve", self.out_sum), ("act", self.out_round), ("dve", self.out_rest))

            def allocate(self, sc):
                self.q1 = sc.sb("q1", [P, 2, S], F32R)
                self.k1 = sc.sb("k1", [P, 2, S], F32R)
                self.q2 = sc.sb("q2", [P, 2, S], F32R)
                self.k2 = sc.sb("k2", [P, 2, S], F32R)
                self.pt_hi = sc.sb("pt_hi", [P, NT, self.UNIT], F32R)
                self.pt_lo = sc.sb("pt_lo", [P, NT, self.UNIT], F32R)
                self.stat = sc.sb("stat", [P, 3, 3])
                self.allocate_out(sc, self.UNIT, 1)
                self.rows_landed = [sc.sem(f"rows_landed{b}") for b in range(2)]
                self.scored_heads = sc.sem("scored_heads")

            def preps(self, s):
                head, i = divmod(s, NT)
                if s < 0:
                    return [(0, part) for part in range(4)]
                return [(head + 1, self.JOBS.index(i))] if i in self.JOBS and head + 1 < GROUP else []

            def needs(self, s):
                return (s // NT, 3) if s % NT == 0 else None

            def gate_units(self, s):
                return 1 if 1 <= s <= self.steps else 0

            def prep_pe(self, job, bank):
                head, part = job
                col = (part // 2) * GROUP * HD + head * HD
                for t in range(4):
                    last = nc.tensor.transpose(psum[0:HD, bank, t * P:(t + 1) * P],
                                               self.qk[:, 4 * (part % 2) + t, col:col + HD], ident[:])
                return last

            def prep_act(self, job, bank):
                head, part = job
                b, cols = head % 2, slice((part % 2) * BANK, (part % 2 + 1) * BANK)
                gain = vecs[0:HD, QN_F:QN_F + 1] if part < 2 else vecs[0:HD, KN_F:KN_F + 1]
                src = psum[0:HD, bank, :]
                again = self.q2[0:HD, b, cols] if part < 2 else self.k1[HD:P, b, cols]
                nc.scalar.activation(again, src, ACT.Copy, scale=gain)
                return nc.scalar.activation((self.q1 if part < 2 else self.k1)[0:HD, b, cols], src, ACT.Copy, scale=gain)

            def prep_dve(self, job, bank):
                head, part = job
                b, cols = head % 2, slice((part % 2) * BANK, (part % 2 + 1) * BANK)
                at = QN_F if part < 2 else KN_F
                lo = self.q1[HD:P, b, cols] if part < 2 else self.k2[0:HD, b, cols]
                hi = (self.q1 if part < 2 else self.k1)[0:HD, b, cols]
                return nc.vector.scalar_tensor_tensor(out=lo, in0=psum[0:HD, bank, :], scalar=vecs[0:HD, at:at + 1],
                                                      in1=hi.bitcast(F32), op0=ALU.mult, op1=ALU.subtract)

            def dve_before(self, dve):
                pass

            def sync(self, sp, piece):
                for head in {0: (0, 1), 8: (2,), 12: (3,)}.get(piece, ()):
                    b = head % 2
                    if head >= 2:
                        sp.wait_ge(self.scored_heads, head - 1)
                    h = self.grp * GROUP + head
                    sp.dma_start(self.q2[HD:self.AUG, b, :].bitcast(F32), c_query[h]).then_inc(self.rows_landed[b], 16)
                    sp.dma_start(self.k2[HD:self.AUG, b, :].bitcast(F32), c_key[h]).then_inc(self.rows_landed[b], 16)

            def pe_inputs(self, pe, s):
                head, i = divmod(s, NT)
                if i == 0:
                    pe.wait_ge(self.rows_landed[head % 2], 32 * (head // 2 + 1))

            def scores(self, s):
                head, i = divmod(s, NT)
                b, rows, keys = head % 2, slice(i * P, (i + 1) * P), (i + 1) * P
                for half in range((keys + BANK - 1) // BANK):
                    cols = slice(half * BANK, min(keys, (half + 1) * BANK))
                    out = psum[:, SCORE + 2 * (s % 2) + half, 0:cols.stop - cols.start]
                    diagonal = keys <= (half + 1) * BANK
                    nc.tensor.matmul(out, self.q1[:, b, rows], self.k1[:, b, cols], start=True, stop=False)
                    last = nc.tensor.matmul(out, self.q2[0:self.AUG, b, rows], self.k2[0:self.AUG, b, cols],
                                            start=False, stop=not diagonal)
                    if i == NT - 1 and half == 1:
                        last.then_inc(self.scored_heads, 1)
                    if diagonal:
                        last = nc.tensor.matmul(out[:, i * P - cols.start:], ident_r[:], causal_r[:], start=False, stop=True)
                return last

            def row_max(self, done, s):
                return nc.vector.tensor_reduce(self.stat[:, s % 3, 0:1], pair(s % 2, (s % NT + 1) * P), AX.X, ALU.max, negate=True)

            def exps(self, s, probs):
                keys = (s % NT + 1) * P
                return nc.scalar.activation(probs[:, 0:keys], pair(s % 2, keys), ACT.Exp, bias=self.stat[:, s % 3, 0:1],
                                            accum_out=self.stat[:, s % 3, 1:2])

            def normalize(self, done, s, probs):
                done(nc.vector.reciprocal(self.stat[:, s % 3, 2:3], self.stat[:, s % 3, 1:2]))
                keys = (s % NT + 1) * P
                return nc.vector.tensor_scalar(probs[:, 0:keys], probs[:, 0:keys], self.stat[:, s % 3, 2:3], None, ALU.mult)

            def turns(self, s):
                i = s % NT
                cols = slice((i % 2) * P, (i % 2 + 1) * P)
                out = []
                for k0 in range(0, i + 1, 4):
                    k1 = min(k0 + 4, i + 1)
                    out.append(([(k * P, (k - k0) * P) for k in range(k0, k1)],
                                self.pt_hi[:, k0:k1, cols], self.pt_lo[:, k0:k1, cols]))
                return out

            def ends_unit(self, s):
                return s % 2 == 1

            def values(self, u):
                head, sb = divmod(u, NT // 2)
                last_key = 2 * sb + 1
                for k in range(last_key + 1):
                    c0 = max(0, k - 2 * sb) * P
                    last = self.value_product(psum[:, OUT, c0:self.UNIT], self.v[:, k, head, :], self.pt_hi[:, k, c0:self.UNIT],
                                              self.pt_lo[:, k, c0:self.UNIT], k == 0, k == last_key)
                return last

            def _place(self, u):
                head, sb = divmod(u, NT // 2)
                h = self.grp * GROUP + head
                return slice((h % 2) * HD, (h % 2 + 1) * HD), h // 2, slice(sb * self.UNIT, (sb + 1) * self.UNIT), u % self.slots

            def out_part(self, u):
                rows, _, _, slot = self._place(u)
                return nc.scalar.activation(self.part[rows, slot, :], psum[HD:P, OUT, 0:self.UNIT], ACT.Copy)

            def out_sum(self, u):
                rows, _, _, slot = self._place(u)
                return nc.vector.tensor_tensor(self.total[rows, slot, :], psum[0:HD, OUT, 0:self.UNIT], self.part[rows, slot, :], ALU.add)

            def out_round(self, u):
                rows, kt, cols, slot = self._place(u)
                return nc.scalar.activation(self.out_hi[rows, kt, cols], self.total[rows, slot, :], ACT.Copy)

            def out_rest(self, u):
                rows, kt, cols, slot = self._place(u)
                return nc.vector.tensor_tensor(self.out_lo[rows, kt, cols], self.total[rows, slot, :],
                                               self.out_hi[rows, kt, cols].bitcast(F32), ALU.subtract)

        class Mem:
            name = "memattn"
            steps = MEM_H * 2
            pt_slots, lo_slots, prob_slots = 2, 2, 3
            max_writes_probs = False
            out_freed = 1
            SCALE = MEM_D ** -0.5

            def __init__(self, q, k, v_hi, v_lo, out_hi, out_lo):
                self.q, self.k, self.v_hi, self.v_lo, self.out_hi, self.out_lo = q, k, v_hi, v_lo, out_hi, out_lo
                self.out_stages = (("act", self.out_round), ("dve", self.out_rest))

            def allocate(self, sc):
                self.q_t = [sc.sb(f"q_{h}", [P, 2, S], F32R) for h in ("hi", "lo")]
                self.k_t = [sc.sb(f"k_{h}", [P, 2, M], F32R) for h in ("hi", "lo")]
                self.pt = [sc.sb(f"pt_{h}", [P, 2, 2, BANK], F32R) for h in ("hi", "lo")]
                self.stat = sc.sb("stat", [P, 4, 3, 4])

            def preps(self, s):
                head = s // 2 + 1
                return [(head, part) for part in range(3)] if s % 2 == (s < 0) and head < MEM_H else []

            def needs(self, s):
                return (s // 2, 2) if s % 2 == 0 else None

            def gate_units(self, s):
                return 1 if 1 <= s <= self.steps else 0

            def _job(self, job):
                head, part = job
                if part == 0:
                    return self.k, range(2), [t[:, head % 2, :] for t in self.k_t], vecs[:, KN_M:KN_M + 1]
                return (self.q, range(4 * part - 4, 4 * part), [t[:, head % 2, (part - 1) * BANK:part * BANK] for t in self.q_t],
                        vecs[:, QN_M:QN_M + 1])

            def prep_pe(self, job, bank):
                tok, tiles, _, _ = self._job(job)
                for i, t in enumerate(tiles):
                    last = nc.tensor.transpose(psum[:, bank, i * P:(i + 1) * P], tok[:, t, job[0] * P:(job[0] + 1) * P], ident[:])
                return last

            def prep_act(self, job, bank):
                _, tiles, dst, gain = self._job(job)
                return nc.scalar.activation(dst[0], psum[:, bank, 0:len(tiles) * P], ACT.Copy, scale=gain)

            def prep_dve(self, job, bank):
                _, tiles, dst, gain = self._job(job)
                return nc.vector.scalar_tensor_tensor(out=dst[1], in0=psum[:, bank, 0:len(tiles) * P], scalar=gain,
                                                      in1=dst[0].bitcast(F32), op0=ALU.mult, op1=ALU.subtract)

            def dve_before(self, dve):
                pass

            def sync(self, sp, piece):
                pass

            def pe_inputs(self, pe, s):
                pass

            def scores(self, s):
                head, half = divmod(s, 2)
                for j in range(4):
                    rows = slice((4 * half + j) * P, (4 * half + j + 1) * P)
                    out = psum[:, SCORE + 2 * (s % 2) + j // 2, (j % 2) * M:(j % 2 + 1) * M]
                    last = three(out, self.q_t[0][:, head % 2, rows], self.q_t[1][:, head % 2, rows],
                                 self.k_t[0][:, head % 2, :], self.k_t[1][:, head % 2, :], True, True)
                return last

            def row_max(self, done, s):
                b = s % 3
                done(nc.vector.tensor_reduce(self.stat[:, 0, b, :], pair(s % 2, S).rearrange("p (j m) -> p j m", m=M), AX.X, ALU.max))
                return nc.vector.tensor_scalar(self.stat[:, 1, b, :], self.stat[:, 0, b, :], -self.SCALE, None, ALU.mult)

            def exps(self, s, probs):
                for j in range(4):
                    cols = slice(j * M, (j + 1) * M)
                    last = nc.scalar.activation(probs[:, cols], pair(s % 2, S)[:, cols], ACT.Exp, scale=self.SCALE,
                                                bias=self.stat[:, 1, s % 3, j:j + 1], accum_out=self.stat[:, 2, s % 3, j:j + 1])
                return last

            def normalize(self, done, s, probs):
                done(nc.vector.reciprocal(self.stat[:, 3, s % 3, :], self.stat[:, 2, s % 3, :]))
                for j in range(4):
                    cols = slice(j * M, (j + 1) * M)
                    last = nc.vector.tensor_scalar(probs[:, cols], probs[:, cols], self.stat[:, 3, s % 3, j:j + 1], None, ALU.mult)
                return last

            def turns(self, s):
                return [([(j * M + m * P, j * P) for j in range(4)], self.pt[0][:, s % 2, m, :], self.pt[1][:, s % 2, m, :])
                        for m in range(2)]

            def ends_unit(self, s):
                return True

            def values(self, u):
                head = u // 2
                cols = slice(head * MEM_D, (head + 1) * MEM_D)
                for m in range(2):
                    last = three(psum[:, OUT, :], self.v_hi[:, m, cols], self.v_lo[:, m, cols],
                                 self.pt[0][:, u % 2, m, :], self.pt[1][:, u % 2, m, :], m == 0, m == 1)
                return last

            def _dst(self, t, u):
                return t[:, u // 2, (u % 2) * BANK:(u % 2 + 1) * BANK]

            def out_round(self, u):
                return nc.scalar.activation(self._dst(self.out_hi, u), psum[:, OUT, :], ACT.Copy)

            def out_rest(self, u):
                return nc.vector.tensor_tensor(self._dst(self.out_lo, u), psum[:, OUT, :],
                                               self._dst(self.out_hi, u).bitcast(F32), ALU.subtract)

        class Swa(HalfHeads):
            name = "swaattn"
            steps = SWA_KV * NT
            pt_slots, lo_slots, prob_slots = 2, 1, 3
            max_writes_probs = True
            KW = 2 * P

            def __init__(self, q, k, values, out_hi, out_lo):
                self.q, self.k, self.v, self.out_hi, self.out_lo = q, k, values, out_hi, out_lo
                self.out_stages = (("act", self.out_part), ("dve", self.out_sum), ("act", self.out_round), ("dve", self.out_rest))

            def allocate(self, sc):
                self.q1 = sc.sb("q1", [P, 2, GROUP, BANK], F32R)
                self.k1 = sc.sb("k1", [P, SWA_KV, S], F32R)
                self.k2 = sc.sb("k2", [HD, SWA_KV, S], F32R)
                self.pt_hi = sc.sb("pt_hi", [P, 2, 2, BANK], F32R)
                self.pt_lo = sc.sb("pt_lo", [P, 2, BANK], F32R)
                self.bias = sc.sb("bias", [P, SWA_H, self.KW])
                self.stat = sc.sb("stat", [P, 6, 3, GROUP])
                self.allocate_out(sc, 2 * P, 1)
                self.bias_landed = sc.sem("bias_landed")

            def preps(self, s):
                if s < 0:
                    return [("k", 0, 0)] + [("q", 0, j) for j in range(GROUP)]
                jobs = [("q", s // 4 + 1, s % 4)] if s // 4 + 1 < self.steps // 4 else []
                return jobs + {0: [("k", 0, 1)], 3: [("k", 1, 0)], 5: [("k", 1, 1)]}.get(s, [])

            def needs(self, s):
                return ("q", s // 4, GROUP - 1) if s % 4 == 0 else None

            def gate_units(self, s):
                return 1 + s % 2 if 1 <= s <= self.steps else 0

            def _job(self, job):
                kind, at, j = job
                if kind == "k":
                    cols = slice(j * BANK, (j + 1) * BANK)
                    return self.k, at * HD, j, self.k1[0:HD, at, cols], self.k1[HD:P, at, cols], self.k2[:, at, cols], KN_A
                g, half = divmod(at, 2)
                return self.q, (GROUP * g + j) * HD, half, self.q1[0:HD, at % 2, j, :], None, self.q1[HD:P, at % 2, j, :], QN_A

            def prep_pe(self, job, bank):
                tok, col, half, *_ = self._job(job)
                for t in range(4):
                    last = nc.tensor.transpose(psum[0:HD, bank, t * P:(t + 1) * P], tok[:, 4 * half + t, col:col + HD], ident[:])
                return last

            def prep_act(self, job, bank):
                *_, hi, again, _, at = self._job(job)
                gain = vecs[0:HD, at:at + 1]
                if again is not None:
                    nc.scalar.activation(again, psum[0:HD, bank, :], ACT.Copy, scale=gain)
                return nc.scalar.activation(hi, psum[0:HD, bank, :], ACT.Copy, scale=gain)

            def prep_dve(self, job, bank):
                *_, hi, _, lo, at = self._job(job)
                return nc.vector.scalar_tensor_tensor(out=lo, in0=psum[0:HD, bank, :], scalar=vecs[0:HD, at:at + 1],
                                                      in1=hi.bitcast(F32), op0=ALU.mult, op1=ALU.subtract)

            def dve_before(self, dve):
                dve.wait_ge(self.bias_landed, 16)

            def sync(self, sp, piece):
                if piece == 0:
                    sp.dma_start(self.bias[:], bass.AP(diagonals.tensor, P - 1, [[SWA_H * (DIAGS + 1) - 1, P], [DIAGS + 1, SWA_H], [1, self.KW]])
                                 ).then_inc(self.bias_landed, 16)

            def pe_inputs(self, pe, s):
                pass

            def _cols(self, s, j):
                return slice(j * self.KW + (P if s % NT == 0 else 0), (j + 1) * self.KW)

            def scores(self, s):
                g, n = divmod(s, NT)
                keys = slice(max(n - 1, 0) * P, (n + 1) * P)
                rows, chunk = slice(n % 4 * P, (n % 4 + 1) * P), s // 4 % 2
                for j in range(GROUP):
                    out = pair(s % 2, S)[:, self._cols(s, j)]
                    nc.tensor.matmul(out, self.q1[:, chunk, j, rows], self.k1[:, g, keys], start=True, stop=False)
                    last = nc.tensor.matmul(out, self.q1[0:HD, chunk, j, rows], self.k2[:, g, keys], start=False, stop=True)
                return last

            def row_max(self, done, s):
                g, b, st = s // NT, s % 3, self.stat
                for j in range(GROUP):
                    h, cols = GROUP * g + j, self._cols(s, j)
                    done.count(nc.vector.tensor_tensor_reduce(
                        out=self.probs[:, b, cols], in0=pair(s % 2, S)[:, cols],
                        in1=self.bias[:, h, cols.start - j * self.KW:], scale=1.0, scalar=sinks[:, h:h + 1],
                        op0=ALU.add, op1=ALU.max, accum_out=st[:, 0, b, j:j + 1]))
                done.wait()
                nc.vector.tensor_scalar(st[:, 1, b, :], st[:, 0, b, :], -1.0, None, ALU.mult)
                return nc.vector.tensor_tensor(st[:, 2, b, :], sinks[:, GROUP * g:GROUP * (g + 1)], st[:, 0, b, :], ALU.subtract)

            def exps(self, s, probs):
                st, b = self.stat, s % 3
                nc.scalar.activation(st[:, 3, b, :], st[:, 2, b, :], ACT.Exp)
                for j in range(GROUP):
                    cols = self._cols(s, j)
                    last = nc.scalar.activation(probs[:, cols], probs[:, cols], ACT.Exp, bias=st[:, 1, b, j:j + 1],
                                                accum_out=st[:, 4, b, j:j + 1])
                return last

            def normalize(self, done, s, probs):
                st, b = self.stat, s % 3
                done(nc.vector.tensor_tensor(st[:, 5, b, :], st[:, 4, b, :], st[:, 3, b, :], ALU.add))
                done(nc.vector.reciprocal(st[:, 5, b, :], st[:, 5, b, :]))
                for j in range(GROUP):
                    cols = self._cols(s, j)
                    last = nc.vector.tensor_scalar(probs[:, cols], probs[:, cols], self.stat[:, 5, s % 3, j:j + 1], None, ALU.mult)
                return last

            def turns(self, s):
                return [([(j * self.KW + kb * P, j * P) for j in range(GROUP)], self.pt_hi[:, s % 2, kb, :], self.pt_lo[:, kb, :])
                        for kb in ((1,) if s % NT == 0 else (0, 1))]

            def ends_unit(self, s):
                return True

            def values(self, u):
                g, n = divmod(u, NT)
                kbs = (1,) if n == 0 else (0, 1)
                for kb in kbs:
                    last = self.value_product(psum[:, OUT, :], self.v[:, n - 1 + kb, g, :], self.pt_hi[:, u % 2, kb, :],
                                              self.pt_lo[:, kb, :], kb == kbs[0], kb == 1)
                return last

            def _heads(self, ap, parity):
                return ap.rearrange("p (a b c) -> p a b c", b=2, c=P)[:, :, parity, :]

            def out_part(self, u):
                for parity in range(2):
                    rows = slice(parity * HD, (parity + 1) * HD)
                    last = nc.scalar.activation(self.part[rows, 0, :].rearrange("p (a c) -> p a c", c=P),
                                                self._heads(psum[HD:P, OUT, :], parity), ACT.Copy)
                return last

            def out_sum(self, u):
                for parity in range(2):
                    rows = slice(parity * HD, (parity + 1) * HD)
                    last = nc.vector.tensor_tensor(self.total[rows, 0, :].rearrange("p (a c) -> p a c", c=P),
                                                   self._heads(psum[0:HD, OUT, :], parity),
                                                   self.part[rows, 0, :].rearrange("p (a c) -> p a c", c=P), ALU.add)
                return last

            def _dst(self, t, u):
                g, n = divmod(u, NT)
                return t[:, 2 * g:2 * g + 2, n * P:(n + 1) * P]

            def out_round(self, u):
                return nc.scalar.activation(self._dst(self.out_hi, u), self.total[:, 0, :].rearrange("p (a c) -> p a c", c=P), ACT.Copy)

            def out_rest(self, u):
                return nc.vector.tensor_tensor(self._dst(self.out_lo, u), self.total[:, 0, :].rearrange("p (a c) -> p a c", c=P),
                                               self._dst(self.out_hi, u).bitcast(F32), ALU.subtract)

        def merge_block(swa_hi, swa_lo):
            weights = [io["w_o_swa"], io["w_o_fox"], io["w_o_mem"]]
            with Scope("merge") as sc:
                w = Weights(sc, 3, stages=3, slots=3)
                halves = {0: (swa_hi, swa_lo)}
                for b in (1, 2):
                    halves[b] = tuple(sc.sb(f"branch{b}_{h}", [P, 4, S], F32R) for h in ("hi", "lo"))
                branch_landed = [sc.sem(f"branch_landed{n}") for n in range(8)]
                branch_hi, branch_lo = sc.sem("branch_hi"), sc.sem("branch_lo")
                gate = sc.sb("gate", [P, 3, S])
                gate_landed = [sc.sem(f"gate_landed{b}") for b in range(3)]
                merged = sc.sb("merged", [P, 2, BANK])
                product = sc.sb("product", [P, 2, BANK])
                gated, multiplied, added, hi_done, lo_done = (sc.sem(k) for k in ("gated", "multiplied", "added", "hi_done", "lo_done"))
                w_branch = [wo[0].rearrange("(k p) n -> p k n", p=P) for wo in weights]

                with nc.Block(no_gpsimd_drain=True) as block:
                    @block.sync
                    def _(sp):
                        with sp.Fori(0, KD) as i:
                            for b in range(3):
                                w.load(sp, i, b, w_branch[b][:, :, bass.ds(i * P, P)])
                                sp.wait_ge(multiplied, i * 6 + 2 * b + 2)
                                sp.sem_inc(w.asked, 1)
                                sp.dma_start(gate[:, b, :], gate_logits[bass.ds(i + b * KD, 1), :, :].rearrange("a p n -> (a p) n")
                                             ).then_inc(gate_landed[b], 16)
                        clear_retired(sp)

                    @block.gpsimd
                    def _(pool):
                        w.start_pool(pool)
                        with pool.Fori(0, KD) as i:
                            for n in range(3):
                                w.split_piece(pool, i, n)

                    @block.tensor
                    def _(pe):
                        w.start_pe(pe)
                        with pe.Fori(0, KD) as i:
                            for b in range(3):
                                w.ready(pe, i, b)
                                pe.wait_ge(multiplied, i * 6 + 2 * b + 2)
                                o_hi, o_lo = halves[b]
                                for kk in range(4):
                                    if b:
                                        pe.wait_ge(branch_lo, 4 * (b - 1) + kk + 1)
                                    for half in range(2):
                                        cols, wc = slice(half * BANK, (half + 1) * BANK), slice(kk * P, (kk + 1) * P)
                                        last = three(psum[:, 2 * b + half, :], w.hi[:, b, wc], w.lo[:, b, wc],
                                                     o_hi[:, kk, cols], o_lo[:, kk, cols], kk == 0, kk == 3)
                                last.then_inc(w.used, 1)

                    @block.scalar
                    def _(act):
                        for n in range(8):
                            act.dma_start(halves[1 + n // 4][1][:, n % 4, :].bitcast(F32), branch_out[1 + n // 4][n % 4]
                                          ).then_inc(branch_landed[n], 16)
                        for n in range(8):
                            hi, lo = (t[:, n % 4, :] for t in halves[1 + n // 4])
                            act.wait_ge(branch_landed[n], 16)
                            nc.scalar.activation(hi, lo.bitcast(F32), ACT.Copy).then_inc(branch_hi, 1)
                        with act.Fori(0, KD) as i:
                            for b in range(3):
                                act.wait_ge(gate_landed[b], i * 16 + 16)
                                nc.scalar.activation(gate[:, b, :], gate[:, b, :], ACT.Sigmoid,
                                                     bias=vecs[:, bass.ds(i + (B_GATE + b * KD), 1)]).then_inc(gated, 1)
                            for half in range(2):
                                act.wait_ge(added, i * 4 + (half + 5))
                                cols = slice(half * BANK, (half + 1) * BANK)
                                nc.scalar.activation(act_hi[:, bass.ds(i, 1), cols].rearrange("p a n -> p (a n)"), merged[:, half, :],
                                                     ACT.Copy).then_inc(hi_done, 1)

                    @block.vector
                    def _(dve):
                        dve.sem_inc(multiplied, 6)
                        for n in range(8):
                            hi, lo = (t[:, n % 4, :] for t in halves[1 + n // 4])
                            dve.wait_ge(branch_hi, n + 1)
                            nc.vector.tensor_tensor(lo, lo.bitcast(F32), hi.bitcast(F32), ALU.subtract).then_inc(branch_lo, 1)
                        dve.sem_inc(added, 2)
                        dve.sem_inc(lo_done, 2)
                        with dve.Fori(0, KD) as i:
                            for b in range(3):
                                dve.wait_ge(w.used, i * 3 + (b + 1 + w.slots))
                                dve.wait_ge(gated, i * 3 + (b + 1))
                                for half in range(2):
                                    cols = slice(half * BANK, (half + 1) * BANK)
                                    if b:
                                        dst = product
                                        dve.wait_ge(added, i * 4 + (2 * b + half - 1))
                                    else:
                                        dst = merged
                                        dve.wait_ge(lo_done, i * 2 + (half + 1))
                                    nc.vector.tensor_tensor(dst[:, half, :], psum[:, 2 * b + half, :], gate[:, b, cols],
                                                            ALU.mult).then_inc(multiplied, 1)
                                if b:
                                    for half in range(2):
                                        dve.wait_ge(multiplied, i * 6 + (2 * b + half + 1 + 6))
                                        nc.vector.tensor_tensor(merged[:, half, :], merged[:, half, :], product[:, half, :],
                                                                ALU.add).then_inc(added, 1)
                            for half in range(2):
                                cols = slice(half * BANK, (half + 1) * BANK)
                                dve.wait_ge(hi_done, i * 2 + (half + 1))
                                nc.vector.tensor_tensor(act_lo[:, bass.ds(i, 1), cols].rearrange("p a n -> p (a n)"), merged[:, half, :],
                                                        act_hi[:, bass.ds(i, 1), cols].rearrange("p a n -> p (a n)").bitcast(F32),
                                                        ALU.subtract).then_inc(lo_done, 1)

        def out_block(x2, next_w, next_load, lead):
            with Scope("wout") as sc:
                w = Weights(sc, 2 * KD)
                w.by_act = [0]
                normed_rows = sc.sb("normed", [P, NT, D])
                stats = sc.sb("stats", [P, 2, NT])
                x_landed = [sc.sem(f"x_landed{t}") for t in range(NT)]
                filled, added, squared, stat, scaled, turned, hi_done, lo_done = (sc.sem(k) for k in (
                    "filled", "added", "squared", "stat", "scaled", "turned", "hi_done", "lo_done"))
                groups = [(g, k) for g in range(2) for k in range(KD)]

                with nc.Block(no_gpsimd_drain=True) as block:
                    @block.sync
                    def _(sp):
                        for n in range(2 * KD):
                            w.load(sp, 0, n, w_rows(io["w_out"], n % KD, n // KD * BANK, (n // KD + 1) * BANK))
                            for t in range(NT if n == 3 else 0):
                                sp.dma_start(x2[:, t, :], io["x"][0, t * P:(t + 1) * P, :]).then_inc(x_landed[t], 16)
                        for n in range(lead):
                            next_load(sp, 0, n)
                        clear_retired(sp)

                    @block.gpsimd
                    def _(pool):
                        w.start_pool(pool)
                        next_w.start_pool(pool)
                        for n in range(2 * KD):
                            w.split_piece(pool, 0, n)
                        split = 0
                        for t in range(NT):
                            one = slice(t, t + 1)
                            pool.wait_ge(squared, t + 1)
                            nc.gpsimd.tensor_scalar(stats[:, 1, one], stats[:, 0, one], 1.0 / D, EPS, ALU.mult, ALU.add).then_inc(stat, 1)
                            pool.wait_ge(stat, 2 * t + 1)
                            nc.gpsimd.tensor_tensor(stats[:, 1, one], stats[:, 1, one], minus_half[:, one], ALU.pow).then_inc(stat, 1)
                            while split < lead * (t + 1) // NT:
                                next_w.split_piece(pool, 0, split)
                                split += 1

                    @block.scalar
                    def _(act):
                        def hi(some):
                            for n in some:
                                g, k = groups[n]
                                act.wait_ge(turned, n + 1)
                                nc.scalar.activation(act_hi[:, k, g * BANK:(g + 1) * BANK], psum[:, n % 4, :], ACT.Copy,
                                                     scale=vecs[:, G_MLP + k:G_MLP + k + 1]).then_inc(hi_done, 1)

                        w.act_hi(act, 0)
                        for t in range(NT):
                            act.wait_ge(added, NT + t + 1)
                            nc.scalar.activation(normed_rows[:, t, :], x2[:, t, :], ACT.Square,
                                                 accum_out=stats[:, 0, t:t + 1]).then_inc(squared, 1)
                            if t >= 5:
                                hi(range(4 * t - 20, min(4 * t - 16, KD)))
                        hi(range(KD, 2 * KD))

                    @block.tensor
                    def _(pe):
                        w.start_pe(pe)
                        next_w.start_pe(pe)

                        def product(c, k, t):
                            rows, r = slice(t * P, (t + 1) * P), (c * KD + k) % w.slots
                            return three(psum[:, t, :], act_hi[:, k, rows], act_lo[:, k, rows], w.hi[:, r, :], w.lo[:, r, :],
                                         k == 0, k == KD - 1)

                        def turn(some):
                            for n in some:
                                g, k = groups[n]
                                pe.wait_ge(scaled, 4 * (g + 1))
                                if n >= 4:
                                    pe.wait_ge(lo_done, n - 3)
                                for t in range(4):
                                    last = nc.tensor.transpose(psum[:, n % 4, t * P:(t + 1) * P],
                                                               normed_rows[:, 4 * g + t, k * P:(k + 1) * P], ident[:])
                                last.then_inc(turned, 1)

                        for k in range(KD):
                            w.ready(pe, 0, k)
                            for t in range(NT):
                                last = product(0, k, t)
                                if k == KD - 1 and t < NT - 1:
                                    last.then_inc(filled, 1)
                            last.then_inc(w.used, 1)
                        for t in range(NT):
                            pe.wait_ge(added, t + 1)
                            for k in range(KD):
                                if t == 0:
                                    w.ready(pe, 0, KD + k)
                                last = product(1, k, t)
                            last.then_inc(filled, 1)
                            if t >= 6:
                                turn(range(4 * t - 24, 4 * t - 20))
                        turn(range(KD, 2 * KD))

                    @block.vector
                    def _(dve):
                        def lo(some):
                            for n in some:
                                g, k = groups[n]
                                cols = slice(g * BANK, (g + 1) * BANK)
                                dve.wait_ge(hi_done, n + 1)
                                nc.vector.scalar_tensor_tensor(
                                    out=act_lo[:, k, cols], in0=psum[:, n % 4, :], scalar=vecs[:, G_MLP + k:G_MLP + k + 1],
                                    in1=act_hi[:, k, cols].bitcast(F32), op0=ALU.mult, op1=ALU.subtract).then_inc(lo_done, 1)

                        def scale(t):
                            dve.wait_ge(stat, 2 * t + 2)
                            nc.vector.tensor_scalar(normed_rows[:, t, :], x2[:, t, :], stats[:, 1, t:t + 1], None,
                                                    ALU.mult).then_inc(scaled, 1)

                        for c in range(2):
                            for t in range(NT):
                                if c == 0 and t == NT - 1:
                                    dve.wait_ge(w.used, w.slots + KD)
                                else:
                                    dve.wait_ge(filled, c * (NT - 1) + t + 1)
                                dve.wait_ge(x_landed[t], 16)
                                cols = slice(c * BANK, (c + 1) * BANK)
                                nc.vector.tensor_tensor(x2[:, t, cols], x2[:, t, cols], psum[:, t, :], ALU.add).then_inc(added, 1)
                                if c and t:
                                    scale(t - 1)
                                if c and t >= 7:
                                    lo(range(0, 4))
                        scale(NT - 1)
                        lo(range(4, 2 * KD))

        def mlp_part():
            FB = 8
            TURNS = FF // (FB * P)
            UP, DOWN = 2 * FB, 2 * FB
            OUTS = 2 * NT
            LEAD = 4
            with Scope("mlp") as sc:
                x2 = sc.sb("x2", [P, NT, D])
                w = Weights(sc, UP + DOWN, slots=4)
                w_up = io["w_mlp_up"][0].rearrange("(k p) n -> p k n", p=P)
                w_down = io["w_mlp_down"][0].rearrange("(t k p) n -> p t k n", p=P, k=FB)

                def load(sp, i, n):
                    if n < UP:
                        source = w_up[:, 4 * (n % 2):4 * (n % 2) + 4, bass.ds(i * (FB * P) + n // 2 * P, P)]
                    else:
                        c, k = divmod(n - UP, FB)
                        source = w_down[:, bass.ds(i, 1), k, c * BANK:(c + 1) * BANK].rearrange("p a n -> p (a n)")
                    w.load(sp, i, n, source)

                out_block(x2, w, load, LEAD)
                u_hi = sc.sb("u_hi", [P, FB, S], F32R)
                u_lo = sc.sb("u_lo", [P, FB, S], F32R)
                relu = sc.sb("relu", [P, 2, BANK])
                square = sc.sb("square", [P, 2, BANK])
                relu_done, square_done, hi_done, lo_done, filled, added = (sc.sem(k) for k in (
                    "relu_done", "square_done", "hi_done", "lo_done", "filled", "added"))
                out_stored = sc.sem("out_stored")
                with nc.Block(no_gpsimd_drain=True) as block:
                    @block.sync
                    def _(sp):
                        with sp.Fori(0, TURNS - 1) as i:
                            for n in range(LEAD, LEAD + w.per):
                                load(sp, i + n // w.per, n % w.per)
                        for n in range(LEAD, w.per):
                            load(sp, TURNS - 1, n)
                        for c in range(2):
                            for t in range(NT):
                                cols = slice(c * BANK, (c + 1) * BANK)
                                sp.wait_ge(added, OUTS * TURNS + c * NT + t + 1)
                                sp.dma_start(io["out"][0, t * P:(t + 1) * P, cols], x2[:, t, cols]).then_inc(out_stored, 16)
                        sp.wait_ge(out_stored, 16 * 2 * NT)
                        clear_retired(sp)

                    @block.gpsimd
                    def _(pool):
                        with pool.Fori(0, TURNS - 1) as i:
                            for n in range(LEAD, LEAD + w.per):
                                w.split_piece(pool, i + n // w.per, n % w.per)
                        for n in range(LEAD, w.per):
                            w.split_piece(pool, TURNS - 1, n)

                    @block.tensor
                    def _(pe):
                        with pe.Fori(0, TURNS) as i:
                            for fb in range(FB):
                                for h in range(2):
                                    n = 2 * fb + h
                                    w.ready(pe, i, n)
                                    if h == 0 and fb < 2:
                                        pe.wait_ge(added, i * OUTS + OUTS - 2 + 2 * fb)
                                    elif h == 0:
                                        pe.wait_ge(relu_done, i * (2 * FB) + 2 * fb - 2)
                                    for kk in range(4):
                                        for half in range(2):
                                            cols = slice(half * BANK, (half + 1) * BANK)
                                            wc = slice(kk * P, (kk + 1) * P)
                                            k = 4 * h + kk
                                            last = three(psum[:, 2 * (fb % 2) + half, :], w.hi[:, n % w.slots, wc], w.lo[:, n % w.slots, wc],
                                                         act_hi[:, k, cols], act_lo[:, k, cols], k == 0, k == KD - 1)
                                    last.then_inc(w.used, 1)
                            for c in range(2):
                                for k in range(FB):
                                    n = UP + c * FB + k
                                    w.ready(pe, i, n)
                                    if c == 0:
                                        pe.wait_ge(lo_done, i * (2 * FB) + 2 * k + 4)
                                    for t in range(NT):
                                        bank = (t + 4) % 8
                                        if k == 0 and c == 0 and bank < 4:
                                            pe.wait_ge(relu_done, i * (2 * FB) + 2 * FB - 3 + bank)
                                        if k == 0 and c == 1:
                                            pe.wait_ge(added, i * OUTS + OUTS + t + 1)
                                        rows = slice(t * P, (t + 1) * P)
                                        last = three(psum[:, bank, :], u_hi[:, k, rows], u_lo[:, k, rows],
                                                     w.hi[:, n % w.slots, :], w.lo[:, n % w.slots, :], k == 0, k == FB - 1)
                                        if k == FB - 1 and t < NT - 1:
                                            last.then_inc(filled, 1)
                                    last.then_inc(w.used, 1)

                    @block.scalar
                    def _(act):
                        with act.Fori(0, TURNS) as i:
                            for fb in range(FB):
                                act.wait_ge(w.used, i * w.per + 2 * fb + 2 + w.slots)
                                for half in range(2):
                                    n = 2 * fb + half
                                    nc.scalar.activation(relu[:, half, :], psum[:, 2 * (fb % 2) + half, :], ACT.Relu).then_inc(relu_done, 1)
                                    act.wait_ge(relu_done, i * (2 * FB) + n + 1)
                                    act.wait_ge(lo_done, i * (2 * FB) + n + 1)
                                    nc.scalar.activation(square[:, half, :], relu[:, half, :], ACT.Square).then_inc(square_done, 1)

                    @block.vector
                    def _(dve):
                        dve.sem_inc(lo_done, 2)
                        dve.sem_inc(added, OUTS)
                        with dve.Fori(0, TURNS) as i:
                            dve.wait_ge(w.used, i * w.per + w.slots)
                            for n in range(2 * FB):
                                cols = slice((n % 2) * BANK, (n % 2 + 1) * BANK)
                                dve.wait_ge(square_done, i * (2 * FB) + n + 1)
                                nc.vector.tensor_copy(u_hi[:, n // 2, cols], square[:, n % 2, :]).then_inc(hi_done, 1)
                                dve.wait_ge(hi_done, i * (2 * FB) + n + 1)
                                nc.vector.tensor_tensor(u_lo[:, n // 2, cols], square[:, n % 2, :],
                                                        u_hi[:, n // 2, cols].bitcast(F32), ALU.subtract).then_inc(lo_done, 1)
                            for c in range(2):
                                for t in range(NT):
                                    if t < NT - 1:
                                        dve.wait_ge(filled, i * (2 * NT - 2) + c * (NT - 1) + t + 1)
                                    else:
                                        dve.wait_ge(w.used, i * w.per + UP + (c + 1) * FB + w.slots)
                                    cols = slice(c * BANK, (c + 1) * BANK)
                                    nc.vector.tensor_tensor(x2[:, t, cols], x2[:, t, cols], psum[:, (t + 4) % 8, :], ALU.add).then_inc(added, 1)

        def w_rows(weights, k, lo, hi):
            return weights[0, k * P:(k + 1) * P, lo:hi]

        w_in = io["w_in"]

        def columns(weights, lo, width):
            return lambda k: [w_rows(weights, k, lo, lo + width)]

        tokens = (act_hi, act_lo, NT)
        setup_block()
        with ExitStack() as outs:
            out_hi = tensor(outs, "out_hi", [P, 4, S], F32R)
            out_lo = tensor(outs, "out_lo", [P, 4, S], F32R)

            for grp in range(FOX_H // GROUP):
                with Scope(f"fox{grp}") as fx:
                    gw = GROUP * HD
                    qk = fx.sb("qk", [P, NT, BANK])
                    values = fx.sb("values", [P, NT, GROUP, 2 * HD], F32R)
                    logits = fx.sb("logits", [P, NT, FOX_H]) if grp == 0 else None

                    def qk_source(k):
                        first = w_rows(w_in, k, C_QF + grp * gw, C_QF + grp * gw + 1)
                        return [bass.AP(w_in.tensor, first.offset, [[w_in.shape[2], P], [C_KF - C_QF, 2], [1, gw]])]

                    def v_source(k):
                        v = w_rows(w_in, k, C_VF + grp * gw, C_VF + (grp + 1) * gw)
                        return [v] + ([w_rows(w_in, k, C_FL, C_FL + FOX_H)] if grp == 0 else [])

                    value = {"view": lambda ps: ps[:, 0:gw].rearrange("p (h d) -> p h d", d=HD),
                             "hi": lambda t: values[:, t, :, 0:HD], "lo": lambda t: values[:, t, :, HD:2 * HD]}
                    if grp == 0:
                        value["logits"] = lambda t: logits[:, t, :]
                    project_block(f"foxproj{grp}", [
                        {"rows": tokens, "width": BANK, "src": qk_source, "norm": {"heads": 2 * GROUP, "hd": HD, "dst": qk}},
                        {"rows": tokens, "width": gw + (FOX_H if grp == 0 else 0), "src": v_source, "value": value}])
                    if grp == 0:
                        decay_block(logits[:].rearrange("p t h -> p (t h)"))
                    attention_block(Fox(grp, qk, values, out_hi, out_lo), range(grp * KD, (grp + 1) * KD))

            with Scope("mem") as ms:
                q = ms.sb("q", [P, NT, BANK])
                k_tok = ms.sb("k_tok", [P, 2, BANK])
                v_hi = ms.sb("v_hi", [P, 2, BANK], F32R)
                v_lo = ms.sb("v_lo", [P, 2, BANK], F32R)
                with Scope("memtok") as mt:
                    mem_hi = mt.sb("mem_hi", [P, KD, M], F32R)
                    mem_lo = mt.sb("mem_lo", [P, KD, M], F32R)
                    memory = (mem_hi, mem_lo, 2)
                    project_block("memproj", [
                        {"rows": tokens, "width": BANK, "src": columns(w_in, C_QM, BANK), "norm": {"heads": MEM_H, "hd": MEM_D, "dst": q}},
                        {"rows": memory, "width": BANK, "src": columns(io["w_mem_kv"], 0, BANK),
                         "norm": {"heads": MEM_H, "hd": MEM_D, "dst": k_tok}},
                        {"rows": memory, "width": BANK, "src": columns(io["w_mem_kv"], BANK, BANK),
                         "value": {"view": lambda ps: ps, "hi": lambda t: v_hi[:, t, :], "lo": lambda t: v_lo[:, t, :]}}],
                        store=(branch_out[1], out_hi, out_lo), mem=(mem_hi, mem_lo))
                attention_block(Mem(q, k_tok, v_hi, v_lo, out_hi, out_lo), range(2 * KD, 2 * KD + 2))

            with Scope("swa") as ss:
                q = ss.sb("q", [P, NT, BANK])
                k_tok = ss.sb("k_tok", [P, NT, SWA_KV * HD])
                values = ss.sb("values", [P, NT, SWA_KV, 2 * HD], F32R)
                kvw = SWA_KV * HD
                project_block("swaproj", [
                    {"rows": tokens, "width": BANK, "src": columns(w_in, C_QA, BANK), "norm": {"heads": SWA_H, "hd": HD, "dst": q}},
                    {"rows": tokens, "width": 2 * kvw, "src": columns(w_in, C_KA, 2 * kvw), "norm": {"heads": SWA_KV, "hd": HD, "dst": k_tok},
                     "value": {"view": lambda ps: ps[:, kvw:2 * kvw].rearrange("p (h d) -> p h d", d=HD),
                               "hi": lambda t: values[:, t, :, 0:HD], "lo": lambda t: values[:, t, :, HD:2 * HD]}}],
                    store=(branch_out[2], out_hi, out_lo))
                attention_block(Swa(q, k_tok, values, out_hi, out_lo), range(2 * KD + 2, 3 * KD))
            merge_block(out_hi, out_lo)

        mlp_part()
        with nc.Block(no_gpsimd_drain=True) as block:
            @block.sync
            def _(sp):
                clear_retired(sp)


def kernel(**inputs):
    import concourse.bacc as bacc
    from concourse.bass_utils import run_bass_kernel_spmd

    nc = bacc.Bacc("TRN2", target_bir_lowering=False, num_devices=1)
    arrays = {name: np.ascontiguousarray(a) for name, a in inputs.items()}
    arrays["bucket_table"] = bucket_table()
    io = {name: nc.dram_tensor(f"in_{name}", a.shape, mybir.dt.from_np(a.dtype), kind="ExternalInput").ap()
          for name, a in arrays.items()}
    io["out"] = nc.dram_tensor("out", (1, S, D), F32, kind="ExternalOutput").ap()
    block_program(nc, io)
    done = run_bass_kernel_spmd(nc, [{f"in_{name}": a for name, a in arrays.items()}], core_ids=[0])
    return done.results[0]["out"]
```
